# Optimizing a Trainium2 kernel written in Bass

```python
import jax, jax.numpy as jnp
from jax import lax
import numpy as np

D_MODEL = 1024
BATCH = 1
SEQ = 256
DEPTH = 1

MEM_LEN = 256
SGU_GROUPS = 4
SGU_GROUP_DIM = 128
SGU_WIDTH = SGU_GROUPS * SGU_GROUP_DIM
SGU_CHUNK = 128
MOBA_HEADS = 8
MOBA_HEAD_DIM = 64
MOBA_WIDTH = MOBA_HEADS * MOBA_HEAD_DIM
MOBA_BLOCK = 256
MOBA_TOPK = 3
Q_BLOCK = 128
MEM_HEADS = 4
MEM_HEAD_DIM = 128
MEM_WIDTH = MEM_HEADS * MEM_HEAD_DIM
N_BRANCHES = 3
SPLIT_SIZES = (SGU_WIDTH, SGU_WIDTH, MOBA_WIDTH, MOBA_WIDTH, MOBA_WIDTH, MEM_WIDTH, N_BRANCHES * D_MODEL)
IN_WIDTH = sum(SPLIT_SIZES)
N_EXPERTS = 32
TOP_K = 4
D_FF = D_MODEL
SWIGLU_ALPHA = 1.702
SWIGLU_LIMIT = 7.0
EXPERT_BLOCK = 128
EPS = 1e-6
NEG_INF = -1e30

kernel_name = 'hybrid_sgu_moba_memxattn_moe_block'

def rms_norm(x, g):
    xf = x.astype(jnp.float32)
    y = xf * lax.rsqrt(jnp.mean(xf * xf, axis=-1, keepdims=True) + EPS)
    return (y * g.astype(jnp.float32)).astype(x.dtype)

def alibi_slopes(n):
    return jnp.asarray(2.0 ** (-8.0 * np.arange(1, n + 1, dtype=np.float32) / n), dtype=jnp.float32)

def sgu_mixer(u, v, g_v, w_spatial, b_spatial):
    B, S, _ = u.shape
    nc = S // SGU_CHUNK
    v = rms_norm(v, g_v)
    vc = v.reshape(B, nc, SGU_CHUNK, SGU_GROUPS, SGU_GROUP_DIM)
    causal = jnp.tril(jnp.ones((SGU_CHUNK, SGU_CHUNK), dtype=bool))
    ws = jnp.where(causal[None], w_spatial, 0.0).astype(v.dtype)
    mixed = jnp.einsum('gts,bcsgd->bctgd', ws, vc) + b_spatial.T[None, None, :, :, None].astype(v.dtype)
    return u * mixed.reshape(B, S, SGU_WIDTH)

def moba_attention(q, k, v, g_q, g_k, slopes):
    B, S, _ = q.shape
    H, Dh, BS = MOBA_HEADS, MOBA_HEAD_DIM, MOBA_BLOCK
    scale = Dh ** -0.5
    q = rms_norm(q.reshape(B, S, H, Dh), g_q).transpose(0, 2, 1, 3)
    k = rms_norm(k.reshape(B, S, H, Dh), g_k).transpose(0, 2, 1, 3)
    v = v.reshape(B, S, H, Dh).transpose(0, 2, 1, 3)
    nb = -(-S // BS)
    pad = nb * BS - S
    k_blocks = jnp.pad(k, ((0, 0), (0, 0), (0, pad), (0, 0))).reshape(B, H, nb, BS, Dh)
    v_blocks = jnp.pad(v, ((0, 0), (0, 0), (0, pad), (0, 0))).reshape(B, H, nb, BS, Dh)
    k_mean = jnp.mean(k_blocks.astype(jnp.float32), axis=3)
    gate = jnp.einsum('bhtd,bhnd->bhtn', q.astype(jnp.float32), k_mean)
    t_all = jnp.arange(S)
    eligible = jnp.arange(nb)[None, :] < (t_all // BS)[:, None]
    gate = jnp.where(eligible, gate, NEG_INF)
    k_sel = min(MOBA_TOPK, nb)
    top_val, top_idx = lax.top_k(gate, k_sel)
    top_valid = top_val > 0.5 * NEG_INF
    nq = S // Q_BLOCK
    h_ix = jnp.arange(H)[:, None, None]

    def step(bc):
        b = bc // nq
        t0 = (bc % nq) * Q_BLOCK
        t = t0 + jnp.arange(Q_BLOCK)
        qb = lax.dynamic_slice_in_dim(lax.dynamic_index_in_dim(q, b, 0, keepdims=False), t0, Q_BLOCK, axis=1)
        idx = lax.dynamic_slice_in_dim(lax.dynamic_index_in_dim(top_idx, b, 0, keepdims=False), t0, Q_BLOCK, axis=1)
        valid = lax.dynamic_slice_in_dim(lax.dynamic_index_in_dim(top_valid, b, 0, keepdims=False), t0, Q_BLOCK, axis=1)
        kb = lax.dynamic_index_in_dim(k_blocks, b, 0, keepdims=False)
        vb = lax.dynamic_index_in_dim(v_blocks, b, 0, keepdims=False)
        k_g = kb[h_ix, idx]
        v_g = vb[h_ix, idx]
        s_sel = jnp.einsum('hqd,hqnkd->hqnk', qb, k_g).astype(jnp.float32) * scale
        key_pos = idx[..., None] * BS + jnp.arange(BS)
        s_sel = s_sel - slopes[:, None, None, None] * (t[None, :, None, None] - key_pos)
        s_sel = jnp.where(valid[..., None], s_sel, NEG_INF)
        own = t0 // BS
        k_own = lax.dynamic_index_in_dim(kb, own, 1, keepdims=False)
        v_own = lax.dynamic_index_in_dim(vb, own, 1, keepdims=False)
        s_own = jnp.einsum('hqd,hkd->hqk', qb, k_own).astype(jnp.float32) * scale
        own_pos = own * BS + jnp.arange(BS)
        s_own = s_own - slopes[:, None, None] * (t[:, None] - own_pos[None, :])
        s_own = jnp.where(own_pos[None, None, :] <= t[None, :, None], s_own, NEG_INF)
        logits = jnp.concatenate([s_sel.reshape(H, Q_BLOCK, k_sel * BS), s_own], axis=-1)
        p = jax.nn.softmax(logits, axis=-1).astype(v.dtype)
        p_sel = p[..., :k_sel * BS].reshape(H, Q_BLOCK, k_sel, BS)
        p_own = p[..., k_sel * BS:]
        return jnp.einsum('hqnk,hqnkd->hqd', p_sel, v_g) + jnp.einsum('hqk,hkd->hqd', p_own, v_own)

    out = lax.map(step, jnp.arange(B * nq))
    out = out.reshape(B, nq, H, Q_BLOCK, Dh).transpose(0, 1, 3, 2, 4)
    return out.reshape(B, S, MOBA_WIDTH)

def memory_attention(q, mem_n, w_mem_kv, g_q, g_k):
    B, S, _ = q.shape
    M = mem_n.shape[1]
    k, v = jnp.split(mem_n @ w_mem_kv, 2, axis=-1)
    q = rms_norm(q.reshape(B, S, MEM_HEADS, MEM_HEAD_DIM), g_q)
    k = rms_norm(k.reshape(B, M, MEM_HEADS, MEM_HEAD_DIM), g_k)
    v = v.reshape(B, M, MEM_HEADS, MEM_HEAD_DIM)
    s = jnp.einsum('bthd,bmhd->bhtm', q, k).astype(jnp.float32) * (MEM_HEAD_DIM ** -0.5)
    p = jax.nn.softmax(s, axis=-1).astype(v.dtype)
    return jnp.einsum('bhtm,bmhd->bthd', p, v).reshape(B, S, MEM_WIDTH)

def swiglu_clamped(hh):
    glu, lin = jnp.split(hh, 2, axis=-1)
    glu = jnp.minimum(glu, SWIGLU_LIMIT)
    lin = jnp.clip(lin, -SWIGLU_LIMIT, SWIGLU_LIMIT)
    return glu * jax.nn.sigmoid(SWIGLU_ALPHA * glu) * (lin + 1.0)

def moe_ffn(h, w_router, b_router, w_gate_up, b_gate_up, w_down, b_down):
    B, S, D = h.shape
    T = B * S
    TK = T * TOP_K
    Mb = EXPERT_BLOCK
    xt = h.reshape(T, D)
    logits = (xt @ w_router + b_router).astype(jnp.float32)
    top_logit, top_e = lax.top_k(logits, TOP_K)
    top_w = jax.nn.softmax(top_logit, axis=-1)
    flat_e = top_e.reshape(TK)
    flat_tok = (jnp.arange(TK) // TOP_K).astype(jnp.int32)
    flat_w = top_w.reshape(TK)
    order = jnp.argsort(flat_e)
    sorted_e = flat_e[order]
    counts = jnp.bincount(flat_e, length=N_EXPERTS)
    starts = jnp.cumsum(counts) - counts
    padded = (counts + Mb - 1) // Mb * Mb
    pad_ends = jnp.cumsum(padded)
    pad_starts = pad_ends - padded
    dest = pad_starts[sorted_e] + (jnp.arange(TK) - starts[sorted_e])
    n_blocks = -(-(TK + N_EXPERTS * (Mb - 1)) // Mb)
    P = n_blocks * Mb
    buf_tok = jnp.full((P,), T, jnp.int32).at[dest].set(flat_tok[order])
    buf_w = jnp.zeros((P,), jnp.float32).at[dest].set(flat_w[order])
    block_e = jnp.minimum(jnp.searchsorted(pad_ends, jnp.arange(n_blocks) * Mb, side='right'), N_EXPERTS - 1)
    x_pad = jnp.concatenate([xt, jnp.zeros((1, D), xt.dtype)], axis=0)

    def expert_block(args):
        tok, e = args
        xb = x_pad[tok]
        w1 = lax.dynamic_index_in_dim(w_gate_up, e, 0, keepdims=False)
        b1 = lax.dynamic_index_in_dim(b_gate_up, e, 0, keepdims=False)
        w2 = lax.dynamic_index_in_dim(w_down, e, 0, keepdims=False)
        b2 = lax.dynamic_index_in_dim(b_down, e, 0, keepdims=False)
        return swiglu_clamped(xb @ w1 + b1) @ w2 + b2

    y = lax.map(expert_block, (buf_tok.reshape(n_blocks, Mb), block_e)).reshape(P, D)
    y = y * buf_w[:, None].astype(y.dtype)
    out = jnp.zeros((T + 1, D), y.dtype).at[buf_tok].add(y)[:T]
    return out.reshape(B, S, D)

def setup_inputs(seed: int = 0) -> dict:
    key = jax.random.key(seed)
    ks = jax.random.split(key, 26)
    L, D, E, F = DEPTH, D_MODEL, N_EXPERTS, D_FF
    nrm = lambda k, shape, fan_in: jax.random.normal(k, shape, jnp.float32) * (fan_in ** -0.5)
    gain = lambda k, shape: 1.0 + 0.02 * jax.random.normal(k, shape, jnp.float32)
    small = lambda k, shape: 0.01 * jax.random.normal(k, shape, jnp.float32)
    return {
        'x': jax.random.normal(ks[0], (BATCH, SEQ, D), jnp.float32),
        'mem': jax.random.normal(ks[1], (BATCH, MEM_LEN, D), jnp.float32),
        'g_mix': gain(ks[2], (L, D)),
        'w_in': nrm(ks[3], (L, D, IN_WIDTH), D),
        'g_sgu_v': gain(ks[4], (L, SGU_WIDTH)),
        'w_spatial': nrm(ks[5], (L, SGU_GROUPS, SGU_CHUNK, SGU_CHUNK), SGU_CHUNK),
        'b_spatial': 1.0 + 0.1 * jax.random.normal(ks[6], (L, SGU_GROUPS, SGU_CHUNK), jnp.float32),
        'g_q_moba': gain(ks[7], (L, MOBA_HEAD_DIM)),
        'g_k_moba': gain(ks[8], (L, MOBA_HEAD_DIM)),
        'g_mem': gain(ks[9], (L, D)),
        'w_mem_kv': nrm(ks[10], (L, D, 2 * MEM_WIDTH), D),
        'g_q_mem': gain(ks[11], (L, MEM_HEAD_DIM)),
        'g_k_mem': gain(ks[12], (L, MEM_HEAD_DIM)),
        'w_br_sgu': nrm(ks[13], (L, SGU_WIDTH, D), SGU_WIDTH),
        'w_br_moba': nrm(ks[14], (L, MOBA_WIDTH, D), MOBA_WIDTH),
        'w_br_mem': nrm(ks[15], (L, MEM_WIDTH, D), MEM_WIDTH),
        'w_out': nrm(ks[16], (L, D, D), D),
        'g_ffn': gain(ks[17], (L, D)),
        'w_router': nrm(ks[18], (L, D, E), D),
        'b_router': small(ks[19], (L, E)),
        'w_gate_up': nrm(ks[20], (L, E, D, 2 * F), D),
        'b_gate_up': small(ks[21], (L, E, 2 * F)),
        'w_down': nrm(ks[22], (L, E, F, D), F),
        'b_down': small(ks[23], (L, E, D)),
    }

def reference(x, mem, g_mix, w_in, g_sgu_v, w_spatial, b_spatial, g_q_moba, g_k_moba,
              g_mem, w_mem_kv, g_q_mem, g_k_mem, w_br_sgu, w_br_moba, w_br_mem, w_out,
              g_ffn, w_router, b_router, w_gate_up, b_gate_up, w_down, b_down):
    slopes = alibi_slopes(MOBA_HEADS)
    offsets = [int(o) for o in np.cumsum(SPLIT_SIZES)[:-1]]
    for l in range(DEPTH):
        h = rms_norm(x, g_mix[l])
        proj = h @ w_in[l]
        u, v_s, q_b, k_b, v_b, q_m, gate_logits = jnp.split(proj, offsets, axis=-1)
        y_a = sgu_mixer(jax.nn.gelu(u, approximate=False), jax.nn.gelu(v_s, approximate=False),
                        g_sgu_v[l], w_spatial[l], b_spatial[l])
        y_b = moba_attention(q_b, k_b, v_b, g_q_moba[l], g_k_moba[l], slopes)
        y_c = memory_attention(q_m, rms_norm(mem, g_mem[l]), w_mem_kv[l], g_q_mem[l], g_k_mem[l])
        g_a, g_b, g_c = jnp.split(jax.nn.sigmoid(gate_logits), N_BRANCHES, axis=-1)
        merged = g_a * (y_a @ w_br_sgu[l]) + g_b * (y_b @ w_br_moba[l]) + g_c * (y_c @ w_br_mem[l])
        x = x + merged @ w_out[l]
        x = x + moe_ffn(rms_norm(x, g_ffn[l]), w_router[l], b_router[l], w_gate_up[l],
                        b_gate_up[l], w_down[l], b_down[l])
    return x


_drawn_inputs = setup_inputs


def setup_inputs(seed=0):
    import zlib

    import numpy as np

    out = dict(_drawn_inputs(seed))
    spreads = {}
    factors = {'g_sgu_v': 31.389,
     'g_q_moba': 16.372,
     'g_k_moba': 27.048,
     'g_mem': 8.0,
     'g_q_mem': 7.336,
     'g_k_mem': 4.579,
     'b_gate_up': 40.515,
     'b_down': 46.044,
     'b_spatial': 5.309,
     'g_ffn': 5.088,
     'b_router': 5.256}
    for name, (base, spread) in spreads.items():
        noise = np.random.default_rng([zlib.crc32(name.encode()), seed]).standard_normal(out[name].shape)
        drawn = base * np.exp(spread * noise) if base else spread * noise
        out[name] = __import__('jax').numpy.asarray(drawn.astype(out[name].dtype))
    for name, factor in factors.items():
        out[name] = (out[name] * factor).astype(out[name].dtype)
    return out
```

```python
from contextlib import ExitStack

import concourse.bass as bass
from concourse import mybir

F32 = mybir.dt.float32
I32 = mybir.dt.int32
ALU = mybir.AluOpType
ACT = mybir.ActivationFunctionType
AX = mybir.AxisListType

P = 128
SLOTS = 64
RING = 6
CHUNK = 4096
NEG = -1e30
SENTINEL = -3e38
REPLACED = 3e38


def build(nc, x, mem, g_mix, w_in, g_sgu_v, w_spatial, b_spatial, g_q_moba, g_k_moba, g_mem,
          w_mem_kv, g_q_mem, g_k_mem, w_br_sgu, w_br_moba, w_br_mem, w_out, g_ffn, w_router,
          b_router, w_gate_up, b_gate_up, w_down, b_down, out):
    SEQ, D = x.shape[1], x.shape[2]
    NT = SEQ // P
    KC = D // P
    E = w_router.shape[2]
    TOP_K = 4
    EPS = 1e-6
    GROUPS = w_spatial.shape[1]
    WIDTH = w_br_sgu.shape[1]
    WC = WIDTH // P
    DH = g_q_moba.shape[1]
    HEADS = WIDTH // DH
    MDH = g_q_mem.shape[1]
    MHEADS = WIDTH // MDH
    F = w_down.shape[2]
    FC = F // P
    JT = 2 * FC
    LIMIT, ALPHA = 7.0, 1.702
    BLOCKS = SEQ // SLOTS
    ITEMS = (SEQ * TOP_K - 1) // SLOTS
    GATE0 = 2 * WIDTH + 4 * WIDTH
    assert (NT, KC, WC, FC, GROUPS) == (2, 8, 4, 8, 4) and KC * 512 == CHUNK

    def col_block(w, n):
        return w[0][:, n * 512:(n + 1) * 512].rearrange("(c p) n -> p c n", p=P)

    def all_cols(w):
        return w[0].rearrange("(c p) n -> p c n", p=P)

    front = ([(col_block(w_in, n), KC) for n in (2, 3, 4, 5)] +
             [(col_block(w_mem_kv, n), KC) for n in (0, 1)] +
             [(col_block(w_in, n), KC) for n in (1, 0)] +
             [(col_block(w_in, 6 + n), KC) for n in range(6)] +
             [(all_cols(w), WC) for w in (w_br_sgu, w_br_moba, w_br_mem)] +
             [(col_block(w_out, n), KC) for n in (0, 1)])
    (C_QB, C_KB, C_VB, C_QM, C_MK, C_MV, C_VS, C_U, C_GATE) = range(9)
    C_BR, C_OUT = C_GATE + 6, C_GATE + 9
    NFRONT = len(front)
    UP_CHUNKS, DOWN_CHUNKS = 4, 2
    PER_EXPERT = UP_CHUNKS + DOWN_CHUNKS
    assert PER_EXPERT == RING

    with ExitStack() as ctx:
        def sb(name, cols, dt=F32):
            return ctx.enter_context(nc.sbuf_tensor(name, [P, cols], dt))

        def sem(name):
            return ctx.enter_context(nc.semaphore(name))

        def cube(ap, n):
            return ap.rearrange("p (a b) -> p a b", a=n)

        ring = sb("ring", RING * CHUNK)
        area_a = sb("area_a", 6144)
        area_b = sb("area_b", 2048)
        area_c = sb("area_c", 2048)
        area_d = sb("area_d", 6144)
        area_e = sb("area_e", 1024)
        area_f = sb("area_f", 1024)
        area_g = sb("area_g", 1024)
        ya = sb("ya", 1024)
        x_sb = sb("x_sb", NT * D)

        h_nat, mem_nat, memT = (cube(area_a[:, 2048 * n:2048 * (n + 1)], m)
                                for n, m in ((0, NT), (1, NT), (2, KC)))
        gates = area_a[:, :].rearrange("p (b j t) -> p b j t", b=3, j=KC)
        h2, h2T = cube(area_a[:, 0:2048], NT), cube(area_a[:, 2048:4096], KC)
        y_sb = area_a[0:SLOTS, 4096:5120]
        hT = cube(area_b[:, :], KC)
        mergedT = hT
        nat = [cube(area_c[:, 1024 * n:1024 * (n + 1)], NT) for n in range(2)]
        yT = [cube(ya[:, :], WC)] + [cube(area_c[:, 1024 * n:1024 * (n + 1)], WC) for n in range(2)]
        qT, kT, qmT, kmT = (cube(area_d[:, 1024 * n:1024 * (n + 1)], WC) for n in range(4))
        v_moba, v_mem = (cube(area_d[:, 1024 * n:1024 * (n + 1)], NT) for n in (4, 5))
        squares = area_e[:, :]
        prob = [area_e[:, 512 * n:512 * (n + 1)] for n in range(2)]
        probT = [area_f[:, 512 * n:512 * (n + 1)] for n in range(2)]
        ws_nat = cube(area_f[:, 0:512], GROUPS)
        bgu_rows = cube(area_f[:, 512:1024], 4)
        product = [area_e[:, :], area_f[:, :]]
        v_sgu = cube(area_g[:, :], NT)
        bdown_sb = area_g[0:E, :]
        x3 = cube(x_sb[:, :], NT)
        EB = KC * SLOTS
        xg, glu, sig, lin, act_h = (area_d[:, n * EB:(n + 1) * EB] for n in range(5))
        onehot = cube(area_d[:, 2560:2560 + NT * SLOTS], NT)
        scatter = [area_d[0:SLOTS, 2688 + 256 * n:2688 + 256 * (n + 1)] for n in range(2)]
        ext = cube(area_d[:, 3200:3200 + NT * (E + 4)], NT)
        ext2 = cube(area_d[:, 3300:3300 + NT * (E + 4)], NT)
        e_exp = cube(area_d[:, 3400:3400 + NT * E], NT)
        flags = area_d[:, 3500:3500 + (BLOCKS - 1) * E]
        incl = area_d[:, 3600:3600 + (BLOCKS - 1) * E]
        order = area_d[:, 3700:3700 + (BLOCKS - 1) * E]
        pick = area_d[:, 3800:3800 + (BLOCKS - 1) * E]
        pick2 = area_d[:, 3900:3900 + (BLOCKS - 1) * E]
        pick_e = area_d[:, 4000:4000 + E]
        over_bias = area_d[:, 4100:4100 + JT]
        wT_sb = area_d[0:E, 4200:4200 + SEQ]

        ident = sb("ident", P)
        before = sb("before", P)
        ones = sb("ones", P)
        iota1 = sb("iota1", SLOTS)
        rel_i = sb("rel_i", 3 * P, I32)
        rel = sb("rel", 3 * P)
        item_e = sb("item_e", (BLOCKS - 1) * E)
        item_b = sb("item_b", (BLOCKS - 1) * E)
        eps = sb("eps", 1)
        rows = sb("rows", P)
        cols = sb("cols", 24)
        G_MIX, G_MEM, G_V, G_Q, G_K, G_QM, G_KM = 0, 8, 16, 20, 21, 22, 23
        wsT = sb("wsT", GROUPS * P)
        bs_bc = sb("bs_bc", GROUPS * P)
        bguT = sb("bguT", E * JT)
        wr_sb = sb("wr_sb", KC * E)
        br_bc = sb("br_bc", E)
        gffn_bc = sb("gffn_bc", D)
        ss = sb("ss", 96)
        rstd = sb("rstd", 96)
        stat = sb("stat", 8)
        top8 = sb("top8", 16)
        rep8 = sb("rep8", 16)
        sel = sb("sel", NT * E)
        slot1 = sb("slot1", NT * E)
        wgt = sb("wgt", NT * E)
        route = sb("route", 16)
        counts = sb("counts", E)
        n_items = sb("n_items", 1, I32)
        over = sb("over", 16)
        over_e = sb("over_e", 1, I32)
        wsT3, bs3 = cube(wsT[:, :], GROUPS), cube(bs_bc[:, :], GROUPS)
        wr3 = cube(wr_sb[:, :], KC)
        sel3, slot3, wgt3 = (cube(a[:, :], NT) for a in (sel, slot1, wgt))

        psum = ctx.enter_context(nc.psum_tensor("psum", [P, 8 * 512], F32))
        pp = [psum[:, 0:1024], psum[:, 1024:2048]]
        ps_score = [psum[:, 2048:2560], psum[:, 2560:3072]]
        ps_t = psum[:, 3072:3584]
        ps_o = psum[:, 3584:4096]
        tb_banks = [ps_score[0], ps_score[1], ps_t, ps_o]
        ps_h = psum[:, 0:1024]
        ps_add = psum[:, 1024:2048]
        ps_y = psum[0:SLOTS, 2048:3072]
        ps_x = psum[:, 3072:3584]
        ps_s = psum[:, 3584:4096]

        x_in, mem_in = [sem(f"x_in{t}") for t in range(NT)], sem("mem_in")
        gains_in, bcast_in, gains_scaled = sem("gains_in"), sem("bcast_in"), sem("gains_scaled")
        ws_in, bgu_in, bdown_in = sem("ws_in"), sem("bgu_in"), sem("bdown_in")
        ring_full = [sem(f"ring_full{n}") for n in range(RING)]
        ring_free = sem("ring_free")
        pool_const, masks_done, dve_const = sem("pool_const"), sem("masks_done"), sem("dve_const")
        sumsq, root, normed, head_ss = sem("sumsq"), sem("root"), sem("normed"), sem("head_ss")
        tb_done, tb_out = sem("tb_done"), sem("tb_out")
        group_done = sem("group_done")
        group_out = [sem(f"group_out{n}") for n in range(2)]
        s_done, max_done, exp_done = sem("s_done"), sem("max_done"), sem("exp_done")
        recip_done, prob_done = sem("recip_done"), sem("prob_done")
        pt_done, pt_out, pv_done, o_out = sem("pt_done"), sem("pt_out"), sem("pv_done"), sem("o_out")
        gate_sig, pool_added, merged = sem("gate_sig"), sem("pool_added"), sem("merged")
        x_ss, x_sum, x_root, h2_done = sem("x_ss"), sem("x_sum"), sem("x_root"), sem("h2_done")
        h2T_done, h2T_out, logits_done = sem("h2T_done"), sem("h2T_out"), sem("logits_done")
        top_done, e_done, sel_done, rank_done = sem("top_done"), sem("e_done"), sem("sel_done"), sem("rank_done")
        wgt_done, wT_done, wT_out, items_done = sem("wgt_done"), sem("wT_done"), sem("wT_out"), sem("items_done")
        onehot_done, gathered, xg_out = sem("onehot_done"), sem("gathered"), sem("xg_out")
        st_done, st_out = sem("st_done"), sem("st_out")
        up_done, glu_done, sig_done, h_done = sem("up_done"), sem("glu_done"), sem("sig_done"), sem("h_done")
        y_out, scattered, summed = sem("y_out"), sem("scattered"), sem("summed")
        lin_done = sem("lin_done")
        v_chain, e_chain, o_chain = sem("v_chain"), sem("e_chain"), sem("o_chain")
        o_item, o_onehot, o_gath, o_xg = sem("o_item"), sem("o_onehot"), sem("o_gath"), sem("o_xg")
        o_st, o_stout, o_full, o_up = sem("o_st"), sem("o_stout"), sem("o_full"), sem("o_up")
        o_glu, o_sig, o_h, o_down = sem("o_glu"), sem("o_sig"), sem("o_h"), sem("o_down")
        o_y, o_scat, o_sum = sem("o_y"), sem("o_scat"), sem("o_sum")
        item_seen, out_done = sem("item_seen"), sem("out_done")

        def slot(n):
            return ring[:, (n % RING) * CHUNK:(n % RING + 1) * CHUNK]

        def fills(n):
            return 16 * (n // RING + 1)

        def expert_fills(e, k):
            n = NFRONT + k
            return (e + (n // RING + 1)) * 16

        up_slots = [NFRONT + k for k in range(UP_CHUNKS)]
        down_slots = [NFRONT + UP_CHUNKS + k for k in range(DOWN_CHUNKS)]

        def up_src(e, k):
            return w_gate_up[0, e][k * 2 * P:(k + 1) * 2 * P, :].rearrange("(c p) n -> p c n", p=P)

        def down_src(e, k):
            return w_down[0, e][k * 4 * P:(k + 1) * 4 * P, :].rearrange("(c p) n -> p c n", p=P)

        ALL_HEADS = HEADS + MHEADS
        HEAD_STEPS = 6 * 4

        def is_moba(h):
            return h < HEADS

        def score_segments(h):
            return [(0, P, 0), (P, 3 * P, 1)] if is_moba(h) else [(0, 256, 0), (256, 512, 1)]

        def o_unit(h):
            return h // 2 if is_moba(h) else HEADS // 2 + (h - HEADS)

        SGU_GROUP = C_GATE + 1
        BR_GROUP, OUT_GROUP = C_BR + 1, C_BR + 1 + 2 * 3

        def last_group(n):
            if n <= C_GATE:
                return n
            if n < C_BR:
                return n + 1
            return BR_GROUP + 2 * (n - C_BR) + 1 if n < C_OUT else OUT_GROUP + n - C_OUT

        def mergedT_half(half):
            return area_b[:, 1024 * half:1024 * (half + 1)]

        SS_X, SS_MEM, SS_V, SS_X2, SS_X2SUM, SS_QK, SS_SUM, SS_MAX = 0, 2, 4, 6, 10, 16, 80, 88

        def stat_r(h, t):
            return rstd[:, SS_SUM + 2 * (h % 4) + t:SS_SUM + 2 * (h % 4) + t + 1]

        def stat_s(h, t):
            return ss[:, SS_SUM + 2 * (h % 4) + t:SS_SUM + 2 * (h % 4) + t + 1]

        def stat_m(h, t):
            return ss[:, SS_MAX + 2 * (h % 4) + t:SS_MAX + 2 * (h % 4) + t + 1]

        def group_is_out(eng, g):
            eng.wait_ge(group_out[g % 2], g // 2 + 1)

        block = ctx.enter_context(nc.Block())

        @block.sync
        def _(sp):
            for n, (src, c) in enumerate(front):
                if n >= RING:
                    sp.wait_ge(group_done, last_group(n - RING) + 1)
                sp.dma_start(cube(slot(n), c), src).then_inc(ring_full[n % RING], 16)
                if n == C_GATE + 3:
                    sp.wait_ge(group_done, SGU_GROUP + 1)
                    sp.dma_start(bdown_sb, b_down[0]).then_inc(bdown_in, 16)

            def expert_chunk(e, k):
                n = NFRONT + k
                src, c = (up_src(e, k), 2) if k < UP_CHUNKS else (down_src(e, k - UP_CHUNKS), 4)
                sp.dma_start(cube(slot(n), c), src).then_inc(ring_full[n % RING], 16)

            for k in range(PER_EXPERT):
                sp.wait_ge(group_done, last_group(NFRONT - RING + k) + 1)
                expert_chunk(0, k)
            with sp.Fori(1, E) as e:
                for k in range(PER_EXPERT):
                    sp.wait_ge(ring_free, e * PER_EXPERT + (k + 1 - PER_EXPERT))
                    expert_chunk(e, k)

            sp.wait_ge(items_done, 1)
            n_over = sp.value_load(n_items[0:1, 0:1], min_val=0, max_val=ITEMS)
            with sp.Fori(0, ITEMS) as i:
                with sp.If(n_over > i):
                    sp.wait_ge(o_item, i + 1)
                    sp.wait_ge(o_down, i + 1)
                    sp.wait_ge(ring_free, E * PER_EXPERT)
                    sp.sem_inc(item_seen, 1)
                    oe = sp.value_load(over_e[0:1, 0:1], min_val=0, max_val=E - 1)
                    for k in range(UP_CHUNKS):
                        sp.dma_start(cube(slot(up_slots[k]), 2), up_src(oe, k)).then_inc(o_full, 16)
                    for k in range(DOWN_CHUNKS):
                        sp.dma_start(cube(slot(down_slots[k]), 4), down_src(oe, k)).then_inc(o_full, 16)
                    with nc.allow_non_contiguous_dma(reason="one bias, for rare items only"):
                        sp.dma_start(over_bias, b_gate_up[0, oe].rearrange("(j p) -> p j", p=P)).then_inc(
                            o_full, 16)

            sp.wait_ge(summed, NT * (E + 1))
            sp.wait_ge(o_sum, n_over * NT + 1)
            sp.dma_start(out[0].rearrange("(t p) d -> p t d", p=P), x3).then_inc(out_done, 16)
            sp.wait_ge(out_done, 16)

        @block.gpsimd
        def _(pool):
            n_const = 0
            small = [(rows[G_MIX:G_MIX + KC, :], g_mix[0].rearrange("(c p) -> c p", p=P)),
                     (rows[G_MEM:G_MEM + KC, :], g_mem[0].rearrange("(c p) -> c p", p=P)),
                     (rows[G_V:G_V + WC, :], g_sgu_v[0].rearrange("(c p) -> c p", p=P)),
                     (rows[G_Q:G_Q + 1, 0:DH], g_q_moba), (rows[G_Q:G_Q + 1, DH:P], g_q_moba),
                     (rows[G_K:G_K + 1, 0:DH], g_k_moba), (rows[G_K:G_K + 1, DH:P], g_k_moba),
                     (rows[G_QM:G_QM + 1, :], g_q_mem), (rows[G_KM:G_KM + 1, :], g_k_mem)]
            for dst, src in small:
                pool.dma_start(dst, src).then_inc(gains_in, 16)

            nc.gpsimd.memset(ident[:, :], 0.0).then_inc(pool_const, 1)
            nc.gpsimd.memset(before[:, :], 1.0).then_inc(pool_const, 1)
            nc.gpsimd.memset(ones[:, :], 1.0).then_inc(pool_const, 1)
            pool.wait_ge(pool_const, 3)
            nc.gpsimd.affine_select(out=ident[:, :], in_=ident[:, :], compare_op=ALU.not_equal, fill=1.0,
                                    base=0, pattern=[[-1, P]], channel_multiplier=1).then_inc(masks_done, 1)

            pool.dma_start(ws_nat, w_spatial[0].rearrange("g t s -> t g s")).then_inc(ws_in, 16)
            pool.dma_start(bgu_rows, b_gate_up[0].rearrange("(q e) (j p) -> (e j) q p", q=4, p=P)).then_inc(
                bgu_in, 16)
            pool.dma_start(bs_bc[:, :], b_spatial.rearrange("l g t -> l (g t)").to_broadcast([P, GROUPS * P])
                           ).then_inc(bcast_in, 16)
            pool.dma_start(wr3, w_router[0].rearrange("(c p) e -> p c e", p=P)).then_inc(bcast_in, 16)
            pool.dma_start(br_bc[:, :], b_router.to_broadcast([P, E])).then_inc(bcast_in, 16)
            pool.dma_start(gffn_bc[:, :], g_ffn.to_broadcast([P, D])).then_inc(bcast_in, 16)

            nc.gpsimd.affine_select(out=before[:, :], in_=before[:, :], compare_op=ALU.is_gt, fill=0.0,
                                    base=0, pattern=[[1, P]], channel_multiplier=-1).then_inc(masks_done, 1)
            nc.gpsimd.iota(rel[:, 0:P], pattern=[[1, P]], base=0, channel_multiplier=-1,
                           allow_small_or_imprecise_dtypes=True).then_inc(pool_const, 1)
            nc.gpsimd.iota(rel[:, P:3 * P], pattern=[[1, 2 * P]], base=-P, channel_multiplier=-1,
                           allow_small_or_imprecise_dtypes=True).then_inc(pool_const, 1)
            nc.gpsimd.iota(iota1[:, :], pattern=[[1, SLOTS]], base=1, channel_multiplier=0,
                           allow_small_or_imprecise_dtypes=True).then_inc(pool_const, 1)
            nc.gpsimd.iota(item_e[:, :], pattern=[[0, BLOCKS - 1], [1, E]], base=0, channel_multiplier=0,
                           allow_small_or_imprecise_dtypes=True).then_inc(pool_const, 1)
            nc.gpsimd.iota(item_b[:, :], pattern=[[SLOTS, BLOCKS - 1], [0, E]], base=SLOTS,
                           channel_multiplier=0, allow_small_or_imprecise_dtypes=True).then_inc(pool_const, 1)
            pool.wait_ge(pool_const, 8)
            nc.gpsimd.affine_select(out=rel[:, 0:P], in_=rel[:, 0:P], compare_op=ALU.is_ge, fill=NEG,
                                    base=0, pattern=[[-1, P]], channel_multiplier=1).then_inc(masks_done, 1)
            nc.gpsimd.affine_select(out=rel[:, P:3 * P], in_=rel[:, P:3 * P], compare_op=ALU.is_ge, fill=NEG,
                                    base=P, pattern=[[-1, 2 * P]], channel_multiplier=1).then_inc(masks_done, 1)
            pool.wait_ge(ws_in, 16)
            nc.gpsimd.affine_select(out=ws_nat, in_=ws_nat, compare_op=ALU.is_ge, fill=0.0, base=0,
                                    pattern=[[0, GROUPS], [-1, P]], channel_multiplier=1).then_inc(masks_done, 1)

            for h in range(ALL_HEADS):
                pool.wait_ge(recip_done, h + 1)
                for a, b, t in score_segments(h):
                    last = nc.gpsimd.tensor_scalar(prob[h % 2][:, a:b], prob[h % 2][:, a:b],
                                                   stat_r(h, t), None, ALU.mult)
                last.then_inc(prob_done, 1)
            for half in range(2):
                group_is_out(pool, BR_GROUP + 2 + half)
                nc.gpsimd.tensor_tensor(cube(mergedT_half(half), 4), cube(mergedT_half(half), 4),
                                        cube(product[half], 4), ALU.add).then_inc(pool_added, 1)

        @block.scalar
        def _(act):
            x_tiles = x[0].rearrange("(t p) d -> p t d", p=P)
            for t in range(NT):
                act.dma_start(x3[:, t, :], x_tiles[:, t, :]).then_inc(x_in[t], 16)
            act.dma_start(mem_nat, mem[0].rearrange("(t p) d -> p t d", p=P)).then_inc(mem_in, 16)

            def copy(dst, src, **kw):
                return nc.scalar.activation(dst, src, ACT.Copy, **kw)

            def take_root(cols_, n, count):
                return nc.scalar.activation(rstd[:, cols_:cols_ + n], ss[:, cols_:cols_ + n], ACT.Sqrt,
                                            bias=eps[:, 0:1], scale=1.0 / count).then_inc(root, 1)

            act.wait_ge(dve_const, 1)
            for t in range(NT):
                act.wait_ge(x_in[t], 16)
                nc.scalar.activation(squares, x3[:, t, :], ACT.Square,
                                     accum_out=ss[:, SS_X + t:SS_X + t + 1]).then_inc(sumsq, 1)
                act.wait_ge(sumsq, t + 1)
            take_root(SS_X, NT, D)
            act.wait_ge(mem_in, 16)
            for t in range(NT):
                nc.scalar.activation(squares, mem_nat[:, t, :], ACT.Square,
                                     accum_out=ss[:, SS_MEM + t:SS_MEM + t + 1]).then_inc(sumsq, 1)
                act.wait_ge(sumsq, NT + t + 1)
            take_root(SS_MEM, NT, D)

            batch = [0]

            def batch_out(*copies):
                b = batch[0]
                act.wait_ge(tb_done, b + 1)
                for dst, col, width, scale in copies:
                    last = copy(dst, tb_banks[b % 4][:, col:col + width],
                                **({} if scale is None else {"scale": scale}))
                last.then_inc(tb_out, 1)
                batch[0] += 1

            def model_chunks(dstT, gain):
                for m in range(KC // 2):
                    batch_out(*((dstT[:, 2 * m + c, :], 256 * c, 256,
                                 cols[:, gain + 2 * m + c:gain + 2 * m + c + 1]) for c in range(2)))

            def heads_out(dstT, gain):
                for t in range(NT):
                    batch_out((dstT[:, :, t * P:(t + 1) * P], 0, 512, cols[:, gain:gain + 1]))

            def group_copy(g, dst, func=ACT.Copy):
                act.wait_ge(group_done, g + 1)
                for half in range(2):
                    last = nc.scalar.activation(dst[half], pp[g % 2][:, 512 * half:512 * (half + 1)], func)
                last.then_inc(group_out[g % 2], 1)

            def halves(ap):
                return [ap[:, n, :] for n in range(2)]

            batch_out((cols[:, 0:24], 0, 24, None))
            act.wait_ge(tb_out, 1)
            for c, n in ((G_Q, DH), (G_QM, MDH)):
                copy(cols[:, c:c + 1], cols[:, c:c + 1], scale=float(n) ** -0.5).then_inc(gains_scaled, 1)
            model_chunks(hT, G_MIX)
            group_copy(C_QB, halves(nat[0]))
            act.wait_ge(head_ss, 1)
            take_root(SS_QK, NT * HEADS, DH)
            model_chunks(memT, G_MEM)
            group_copy(C_KB, halves(nat[1]))
            act.wait_ge(head_ss, 2)
            take_root(SS_QK + 16, NT * HEADS, DH)
            batch_out((wsT[:, :], 0, 512, None))
            batch_out((bguT[:, :], 0, 512, None))
            act.wait_ge(gains_scaled, 2)
            heads_out(qT, G_Q)
            group_copy(C_VB, halves(v_moba))
            heads_out(kT, G_K)
            group_copy(C_QM, halves(nat[0]))
            act.wait_ge(head_ss, 3)
            take_root(SS_QK + 32, NT * MHEADS, MDH)
            group_copy(C_MK, halves(nat[1]))
            act.wait_ge(head_ss, 4)
            take_root(SS_QK + 48, NT * MHEADS, MDH)
            heads_out(qmT, G_QM)
            group_copy(C_MV, halves(v_mem))
            heads_out(kmT, G_KM)
            group_copy(C_VS, halves(v_sgu), ACT.Gelu)
            group_copy(C_U, [ya[:, 0:512], ya[:, 512:1024]], ACT.Gelu)
            act.wait_ge(head_ss, 5)
            take_root(SS_V, NT, WIDTH)

            def exps(h):
                act.wait_ge(max_done, h + 1)
                for a, b, t in score_segments(h):
                    src = prob[h % 2][:, a:b] if is_moba(h) else ps_score[h % 2][:, a:b]
                    last = nc.scalar.activation(prob[h % 2][:, a:b], src, ACT.Exp, bias=stat_m(h, t),
                                                accum_out=stat_s(h, t))
                last.then_inc(exp_done, 1)

            def prob_out(h):
                act.wait_ge(pt_done, h + 1)
                if h >= 2:
                    act.wait_ge(pv_done, h - 1)
                width = 3 * P if is_moba(h) else 4 * P
                copy(probT[h % 2][:, 0:width], ps_t[:, 0:width]).then_inc(pt_out, 1)

            def head_out(h):
                act.wait_ge(pv_done, h + 1)
                u = o_unit(h)
                dst = yT[1][:, u, :] if is_moba(h) else yT[2][:, h - HEADS, :]
                copy(dst, ps_o[:, 256 * (u % 2):256 * (u % 2 + 1)]).then_inc(o_out, 1)

            def gate_out(m):
                g = C_GATE if m == 0 else C_GATE + 1 + m
                dst = gates[:, m // 2, 4 * (m % 2):4 * (m % 2) + 4, :].rearrange("p j t -> p (j t)")
                group_copy(g, [dst[:, 0:512], dst[:, 512:1024]], ACT.Sigmoid if m >= 4 else ACT.Copy)

            for s in range(HEAD_STEPS):
                if 2 <= s < ALL_HEADS + 2:
                    prob_out(s - 2)
                if s < ALL_HEADS:
                    exps(s)
                if 3 <= s < ALL_HEADS + 3 and (not is_moba(s - 3) or (s - 3) % 2 == 1):
                    head_out(s - 3)
                if s % 4 == 3:
                    gate_out(s // 4)
                if s == 16:
                    for b in range(2):
                        group_is_out(act, C_GATE + 2 + 2 * b)
                        both = gates[:, b, :, :].rearrange("p j t -> p (j t)")
                        nc.scalar.activation(both, both, ACT.Sigmoid).then_inc(gate_sig, 1)

            for n in range(2):
                group_is_out(act, OUT_GROUP + n)
                for t in range(NT):
                    last = nc.scalar.activation(product[n][:, 512 * t:512 * (t + 1)],
                                                x3[:, t, 512 * n:512 * (n + 1)], ACT.Square,
                                                accum_out=ss[:, SS_X2 + 2 * t + n:SS_X2 + 2 * t + n + 1])
                last.then_inc(x_ss, 1)
            act.wait_ge(x_sum, 1)
            nc.scalar.activation(rstd[:, SS_X2SUM:SS_X2SUM + NT], ss[:, SS_X2SUM:SS_X2SUM + NT], ACT.Sqrt,
                                 bias=eps[:, 0:1], scale=1.0 / D).then_inc(x_root, 1)
            for m in range(KC // 2):
                act.wait_ge(h2T_done, m + 1)
                copy(h2T[:, 2 * m:2 * m + 2, :].rearrange("p c t -> p (c t)"), tb_banks[m]).then_inc(h2T_out, 1)
            act.wait_ge(top_done, 1)
            for t in range(NT):
                last = nc.scalar.activation(e_exp[:, t, :], ext[:, t, 0:E], ACT.Exp, bias=stat[:, t:t + 1])
            last.then_inc(e_done, 1)

            def tokens_out(e, parity):
                act.wait_ge(gathered, e + 1)
                copy(xg, ps_x).then_inc(xg_out, 1)
                act.wait_ge(st_done, e + 1)
                copy(scatter[parity], ps_s[0:SLOTS, 0:NT * P]).then_inc(st_out, 1)

            def y_copy(e):
                act.wait_ge(ring_free, e * PER_EXPERT + PER_EXPERT)
                copy(y_sb, ps_y).then_inc(y_out, 1)

            def sigmoids(e):
                for half in range(2):
                    act.wait_ge(glu_done, e * 2 + (half + 1))
                    a = slice(256 * half, 256 * (half + 1))
                    nc.scalar.activation(sig[:, a], glu[:, a], ACT.Sigmoid, scale=ALPHA).then_inc(sig_done, 1)

            tokens_out(0, 0)
            act.wait_ge(wT_done, 1)
            copy(wT_sb, ps_score[0][0:E, 0:SEQ]).then_inc(wT_out, 1)
            sigmoids(0)
            tokens_out(1, 1)
            with act.Fori(0, (E - 2) // 2) as pair:
                for parity, e in ((1, pair * 2 + 1), (0, pair * 2 + 2)):
                    y_copy(e - 1)
                    sigmoids(e)
                    tokens_out(e + 1, 1 - parity)
            y_copy(E - 2)
            sigmoids(E - 1)
            y_copy(E - 1)

            act.wait_ge(items_done, 1)
            n_over = act.value_load(n_items[0:1, 0:1], min_val=0, max_val=ITEMS)
            with act.Fori(0, ITEMS) as i:
                with act.If(n_over > i):
                    act.wait_ge(o_gath, i + 1)
                    copy(xg, ps_x).then_inc(o_xg, 1)
                    act.wait_ge(o_st, i + 2)
                    copy(scatter[0], ps_s[0:SLOTS, 0:NT * P]).then_inc(o_stout, 1)
                    act.wait_ge(o_glu, i + 1)
                    nc.scalar.activation(sig, glu, ACT.Sigmoid, scale=ALPHA).then_inc(o_sig, 1)
                    act.wait_ge(o_down, i + 2)
                    copy(y_sb, ps_y).then_inc(o_y, 1)

        @block.tensor
        def _(pe):
            mm = nc.tensor.matmul
            batch = [0]

            def transposes(*parts):
                b = batch[0]
                if b >= 4:
                    pe.wait_ge(tb_out, b - 3)
                for src, col in parts:
                    k = src.shape[0]
                    last = nc.tensor.transpose(tb_banks[b % 4][:, col:col + k], src, ident[0:k, 0:k])
                last.then_inc(tb_done, 1)
                batch[0] += 1

            def model_batches(src):
                for m in range(KC // 2):
                    transposes(*((src[:, t, (2 * m + c) * P:(2 * m + c + 1) * P], 256 * c + P * t)
                                 for c in range(2) for t in range(NT)))

            def head_batches(src):
                for t in range(NT):
                    transposes(*((src[:, t, c * P:(c + 1) * P], P * c) for c in range(WC)))

            def start_group(g):
                if g >= 2:
                    group_is_out(pe, g - 2)

            def chunk_in(n):
                pe.wait_ge(ring_full[n % RING], fills(n))
                return cube(slot(n), front[n][1])

            def natural(n, g, lhsT):
                start_group(g)
                w = chunk_in(n)
                for t in range(NT):
                    for c in range(KC):
                        last = mm(pp[g % 2][:, 512 * t:512 * (t + 1)], lhsT[:, c, t * P:(t + 1) * P],
                                  w[:, c, :], start=(c == 0), stop=(c == KC - 1))
                last.then_inc(group_done, 1)

            def column_tile(w, g, j, col, rhs, nk):
                for c in range(nk):
                    last = mm(pp[g % 2][:, 256 * j:256 * (j + 1)], w[:, c, col:col + P], rhs[:, c, :],
                              start=(c == 0), stop=(c == nk - 1))
                return last

            pe.wait_ge(masks_done, 1)
            pe.wait_ge(gains_in, 9 * 16)
            transposes((rows[0:24, :], 0))
            pe.wait_ge(normed, NT)
            model_batches(h_nat)
            pe.wait_ge(tb_out, 5)
            natural(C_QB, C_QB, hT)
            pe.wait_ge(normed, 2 * NT)
            model_batches(mem_nat)
            natural(C_KB, C_KB, hT)
            pe.wait_ge(masks_done, 5)
            transposes(*((ws_nat[:, g, :], P * g) for g in range(GROUPS)))
            pe.wait_ge(bgu_in, 16)
            transposes(*((bgu_rows[:, q, :], P * q) for q in range(4)))
            pe.wait_ge(normed, 2 * NT + 1)
            head_batches(nat[0])
            natural(C_VB, C_VB, hT)
            pe.wait_ge(normed, 2 * NT + 2)
            head_batches(nat[1])
            natural(C_QM, C_QM, hT)
            pe.wait_ge(tb_out, 9)
            natural(C_MK, C_MK, memT)
            pe.wait_ge(normed, 2 * NT + 3)
            head_batches(nat[0])
            natural(C_MV, C_MV, memT)
            pe.wait_ge(normed, 2 * NT + 4)
            head_batches(nat[1])
            natural(C_VS, C_VS, hT)
            start_group(C_U)
            w = chunk_in(C_U)
            for j in range(4):
                last = column_tile(w, C_U, j, j * P, hT, KC)
            last.then_inc(group_done, 1)

            pe.wait_ge(tb_out, batch[0])

            def scores(h):
                if h >= 2:
                    pe.wait_ge(exp_done, h - 1)
                bank = ps_score[h % 2]
                if is_moba(h):
                    rows_, pair = slice(DH * (h % 2), DH * (h % 2 + 1)), h // 2
                    mm(bank[:, 0:P], qT[rows_, pair, 0:P], kT[rows_, pair, 0:P], start=True, stop=True)
                    last = mm(bank[:, P:3 * P], qT[rows_, pair, P:2 * P], kT[rows_, pair, :],
                              start=True, stop=True)
                else:
                    for t in range(NT):
                        last = mm(bank[:, 256 * t:256 * (t + 1)], qmT[:, h - HEADS, t * P:(t + 1) * P],
                                  kmT[:, h - HEADS, :], start=True, stop=True)
                last.then_inc(s_done, 1)

            def prob_transposes(h):
                pe.wait_ge(prob_done, h + 1)
                if h >= 1:
                    pe.wait_ge(pt_out, h)
                moves = [(0, 0), (1, 1), (2, 2)] if is_moba(h) else [(0, 0), (1, 2), (2, 1), (3, 3)]
                for a, b in moves:
                    last = nc.tensor.transpose(ps_t[:, b * P:(b + 1) * P], prob[h % 2][:, a * P:(a + 1) * P],
                                               ident[:, :])
                last.then_inc(pt_done, 1)

            def values(h):
                pe.wait_ge(pt_out, h + 1)
                u = o_unit(h)
                if u >= 1:
                    pe.wait_ge(o_out, u)
                c0, p2 = 256 * (u % 2), probT[h % 2]
                if is_moba(h):
                    r0 = DH * (h % 2)
                    mm(ps_o[r0:r0 + DH, c0:c0 + 256], v_moba[:, 0, h * DH:(h + 1) * DH], p2[:, 0:256],
                       start=True, stop=False, skip_group_check=True)
                    last = mm(ps_o[r0:r0 + DH, c0 + P:c0 + 256], v_moba[:, 1, h * DH:(h + 1) * DH],
                              p2[:, 256:384], start=False, stop=True, skip_group_check=True)
                else:
                    for t in range(2):
                        last = mm(ps_o[:, c0:c0 + 256], v_mem[:, t, (h - HEADS) * MDH:(h - HEADS + 1) * MDH],
                                  p2[:, 256 * t:256 * (t + 1)], start=(t == 0), stop=(t == 1))
                last.then_inc(pv_done, 1)

            for s in range(HEAD_STEPS):
                if 3 <= s < ALL_HEADS + 3:
                    values(s - 3)
                if 2 <= s < ALL_HEADS + 2:
                    prob_transposes(s - 2)
                if s < ALL_HEADS:
                    scores(s)
                m, j = divmod(s, 4)
                g = C_GATE if m == 0 else C_GATE + 1 + m
                if j == 0:
                    start_group(g)
                    w = chunk_in(C_GATE + m)
                last = column_tile(w, g, j, j * P, hT, KC)
                if j == 3:
                    last.then_inc(group_done, 1)
                if s == 3:
                    start_group(SGU_GROUP)
                    pe.wait_ge(normed, 2 * NT + 5)
                    for gg in range(GROUPS):
                        for t in range(NT):
                            last = mm(pp[SGU_GROUP % 2][:, 256 * gg + P * t:256 * gg + P * (t + 1)],
                                      v_sgu[:, t, gg * P:(gg + 1) * P], wsT3[:, gg, :], start=True, stop=True)
                    last.then_inc(group_done, 1)

            for b in range(3):
                w = chunk_in(C_BR + b)
                if b == 0:
                    group_is_out(pe, SGU_GROUP)
                else:
                    pe.wait_ge(o_out, WC * b)
                for half in range(2):
                    g = BR_GROUP + 2 * b + half
                    start_group(g)
                    for j in range(4):
                        last = column_tile(w, g, j, (4 * half + j) * P, yT[b], WC)
                    last.then_inc(group_done, 1)
            for n in range(2):
                g = OUT_GROUP + n
                start_group(g)
                w = chunk_in(C_OUT + n)
                for c in range(KC):
                    if n == 0 and c % 4 == 0:
                        pe.wait_ge(merged, c // 4 + 1)
                    for t in range(NT):
                        last = mm(pp[g % 2][:, 512 * t:512 * (t + 1)], mergedT[:, c, t * P:(t + 1) * P],
                                  w[:, c, :], start=(c == 0), stop=(c == KC - 1))
                last.then_inc(group_done, 1)

            for m in range(KC // 2):
                pe.wait_ge(h2_done, NT * (m // 2 + 1))
                for c in range(2):
                    for t in range(NT):
                        last = nc.tensor.transpose(tb_banks[m][:, 256 * c + P * t:256 * c + P * (t + 1)],
                                                   h2[:, t, (2 * m + c) * P:(2 * m + c + 1) * P], ident[:, :])
                last.then_inc(h2T_done, 1)
            pe.wait_ge(bcast_in, 4 * 16)
            pe.wait_ge(h2T_out, KC // 2)
            for t in range(NT):
                for c in range(KC):
                    last = mm(pp[0][:, E * t:E * (t + 1)], h2T[:, c, t * P:(t + 1) * P], wr3[:, c, :],
                              start=(c == 0), stop=(c == KC - 1))
            last.then_inc(logits_done, 1)
            pe.wait_ge(masks_done, 2)
            pe.wait_ge(sel_done, 1)
            mm(pp[1][:, 0:E], before[:, :], sel3[:, 0, :], start=True, stop=True)
            mm(pp[1][:, E:2 * E], ones[:, :], sel3[:, 0, :], start=True, stop=False)
            mm(pp[1][:, E:2 * E], before[:, :], sel3[:, 1, :], start=False, stop=True)
            mm(pp[1][:, 2 * E:3 * E], ones[:, :], sel3[:, 0, :], start=True, stop=False)
            mm(pp[1][:, 2 * E:3 * E], ones[:, :], sel3[:, 1, :], start=False, stop=True).then_inc(rank_done, 1)

            def gather_mms():
                for c in range(KC):
                    for t in range(NT):
                        last = mm(ps_x[:, SLOTS * c:SLOTS * (c + 1)], h2[:, t, c * P:(c + 1) * P],
                                  onehot[:, t, :], start=(t == 0), stop=(t == NT - 1))
                return last

            def scatter_transposes():
                for t in range(NT):
                    last = nc.tensor.transpose(ps_s[0:SLOTS, P * t:P * (t + 1)], onehot[:, t, :], ident[:, :])
                return last

            def up_mms(k, tiles=range(JT)):
                w = cube(slot(up_slots[k]), 2)
                for c in range(2):
                    kc = 2 * k + c
                    for j in tiles:
                        col = 512 * (j % FC // 4) + SLOTS * (4 * (j // FC) + j % 4)
                        last = mm(ps_h[:, col:col + SLOTS], w[:, c, j * P:(j + 1) * P],
                                  xg[:, SLOTS * kc:SLOTS * (kc + 1)], start=(kc == 0 and j in (0, 4)),
                                  stop=(kc == KC - 1), skip_group_check=True)
                return last

            def half_tiles(half):
                return [FC * b + 4 * half + j for b in range(2) for j in range(4)]

            def down_mms(k):
                w = cube(slot(down_slots[k]), 4)
                for c in range(4):
                    kc = 4 * k + c
                    for n in range(2):
                        last = mm(ps_y[:, 512 * n:512 * (n + 1)], act_h[:, SLOTS * kc:SLOTS * (kc + 1)],
                                  w[:, c, 512 * n:512 * (n + 1)], start=(kc == 0), stop=(kc == FC - 1))
                return last

            def gather(e):
                pe.wait_ge(onehot_done, e + 1)
                pe.wait_ge(xg_out, e)
                pe.wait_ge(st_out, e)
                gather_mms().then_inc(gathered, 1)
                scatter_transposes().then_inc(st_done, 1)

            def scatter_mms(t, lhsT, rhs):
                for n in range(2):
                    last = mm(ps_add[:, 512 * n:512 * (n + 1)], lhsT[:, t * P:(t + 1) * P],
                              rhs[:, 512 * n:512 * (n + 1)], start=True, stop=True)
                return last

            def scatter_back(e, t, parity):
                if t == 0:
                    pe.wait_ge(y_out, e + 1)
                    pe.wait_ge(st_out, e + 1)
                pe.wait_ge(summed, e * NT + (NT + t))
                scatter_mms(t, scatter[parity], y_sb).then_inc(scattered, 1)

            def expert(e, parity, between, after):
                pe.wait_ge(xg_out, e + 1)
                for k in range(UP_CHUNKS):
                    n = up_slots[k]
                    pe.wait_ge(ring_full[n % RING], expert_fills(e, k))
                    if k == UP_CHUNKS - 1:
                        up_mms(k, half_tiles(0)).then_inc(up_done, 1)
                        up_mms(k, half_tiles(1)).then_inc(ring_free, 1)
                    else:
                        up_mms(k).then_inc(ring_free, 1)
                    if k == 1:
                        between()
                after()
                for k in range(DOWN_CHUNKS):
                    n = down_slots[k]
                    pe.wait_ge(ring_full[n % RING], expert_fills(e, UP_CHUNKS + k))
                    pe.wait_ge(h_done, e * 2 + (k + 1))
                    down_mms(k).then_inc(ring_free, 1)

            def bias_back(t):
                if t == 0:
                    pe.wait_ge(wT_out, 1)
                    pe.wait_ge(bdown_in, 16)
                else:
                    pe.wait_ge(summed, t)
                scatter_mms(t, wT_sb, bdown_sb).then_inc(scattered, 1)

            gather(0)
            pe.wait_ge(wgt_done, 1)
            for t in range(NT):
                last = nc.tensor.transpose(ps_score[0][0:E, P * t:P * (t + 1)], wgt3[:, t, :], ident[:, :])
            last.then_inc(wT_done, 1)

            def after_first():
                bias_back(1)
                gather(1)

            expert(0, 0, lambda: bias_back(0), after_first)
            with pe.Fori(0, (E - 2) // 2) as pair:
                for parity, e in ((1, pair * 2 + 1), (0, pair * 2 + 2)):
                    def between():
                        scatter_back(e - 1, 0, 1 - parity)

                    def after():
                        scatter_back(e - 1, 1, 1 - parity)
                        gather(e + 1)

                    expert(e, parity, between, after)
            expert(E - 1, 1, lambda: scatter_back(E - 2, 0, 0), lambda: scatter_back(E - 2, 1, 0))
            for t in range(NT):
                scatter_back(E - 1, t, 1)

            pe.sem_inc(o_down, 1)
            pe.sem_inc(o_st, 1)
            pe.wait_ge(items_done, 1)
            n_over = pe.value_load(n_items[0:1, 0:1], min_val=0, max_val=ITEMS)
            with pe.Fori(0, ITEMS) as i:
                with pe.If(n_over > i):
                    pe.wait_ge(o_onehot, i + 1)
                    gather_mms().then_inc(o_gath, 1)
                    scatter_transposes().then_inc(o_st, 1)
                    pe.wait_ge(o_full, i * 112 + 112)
                    pe.wait_ge(o_xg, i + 1)
                    for k in range(UP_CHUNKS):
                        last = up_mms(k)
                    last.then_inc(o_up, 1)
                    pe.wait_ge(o_h, i + 1)
                    for k in range(DOWN_CHUNKS):
                        last = down_mms(k)
                    last.then_inc(o_down, 1)
                    pe.wait_ge(o_y, i + 1)
                    pe.wait_ge(o_stout, i + 1)
                    pe.wait_ge(summed, NT * (E + 1))
                    scatter_mms(0, scatter[0], y_sb).then_inc(o_scat, 1)
                    pe.wait_ge(o_sum, i * NT + 2)
                    scatter_mms(1, scatter[0], y_sb).then_inc(o_scat, 1)
                    pe.wait_ge(o_sum, i * NT + 3)

        @block.vector
        def _(dve):
            v = nc.vector
            links = [0]

            def link(ins):
                links[0] += 1
                ins.then_inc(v_chain, 1)
                dve.wait_ge(v_chain, links[0])

            link(v.memset(eps[:, :], EPS))
            v.memset(rep8[:, :], SENTINEL).then_inc(dve_const, 1)

            for n, (src, dst, col) in enumerate(((x3, h_nat, SS_X), (mem_nat, mem_nat, SS_MEM))):
                dve.wait_ge(root, n + 1)
                link(v.reciprocal(rstd[:, col:col + NT], rstd[:, col:col + NT]))
                for t in range(NT):
                    v.tensor_scalar(dst[:, t, :], src[:, t, :], rstd[:, col + t:col + t + 1], None,
                                    ALU.mult).then_inc(normed, 1)

            def head_sums(n, g, src, heads, col):
                group_is_out(dve, g)
                if n == 0:
                    dve.wait_ge(sumsq, 2 * NT)
                link(v.tensor_tensor(cube(squares, NT), src, src, ALU.mult))
                v.tensor_reduce(ss[:, col:col + NT * heads],
                                squares.rearrange("p (th d) -> p th d", th=NT * heads), AX.X,
                                ALU.add).then_inc(head_ss, 1)

            def head_norm(n, src, heads, col):
                dve.wait_ge(root, 3 + n)
                link(v.reciprocal(rstd[:, col:col + NT * heads], rstd[:, col:col + NT * heads]))
                flat = src.rearrange("p t n -> p (t n)").rearrange("p (th d) -> p th d", th=NT * heads)
                scale = rstd[:, col:col + NT * heads].unsqueeze(2).to_broadcast(flat.shape)
                v.tensor_tensor(flat, flat, scale, ALU.mult).then_inc(normed, 1)

            for n, (g, src, heads) in enumerate(((C_QB, nat[0], HEADS), (C_KB, nat[1], HEADS),
                                                 (C_QM, nat[0], MHEADS), (C_MK, nat[1], MHEADS))):
                head_sums(n, g, src, heads, SS_QK + 16 * n)
                head_norm(n, src, heads, SS_QK + 16 * n)
            head_sums(4, C_VS, v_sgu, 1, SS_V)
            dve.wait_ge(root, 7)
            link(v.reciprocal(rstd[:, SS_V:SS_V + NT], rstd[:, SS_V:SS_V + NT]))
            for t in range(NT):
                last = v.tensor_scalar(v_sgu[:, t, :], v_sgu[:, t, :], rstd[:, SS_V + t:SS_V + t + 1], None,
                                       ALU.mult)
            last.then_inc(normed, 1)

            def maxima(h):
                dve.wait_ge(s_done, h + 1)
                if h >= 2:
                    dve.wait_ge(pt_done, h - 1)
                m0, m1 = stat_m(h, 0), stat_m(h, 1)
                both = ss[:, SS_MAX + 2 * (h % 4):SS_MAX + 2 * (h % 4) + 2]
                if is_moba(h):
                    logits = prob[h % 2]
                    scaled = 2.0 ** (-8.0 * (h + 1) / HEADS)
                    link(v.scalar_tensor_tensor(logits[:, 0:3 * P], rel[:, :], scaled,
                                                ps_score[h % 2][:, 0:3 * P], ALU.mult, ALU.add))
                    v.tensor_reduce(m0, logits[:, 0:P], AX.X, ALU.max)
                    link(v.tensor_reduce(m1, logits[:, P:3 * P], AX.X, ALU.max))
                else:
                    link(v.tensor_reduce(both, cube(ps_score[h % 2], 2), AX.X, ALU.max))
                v.tensor_scalar(both, both, -1.0, None, ALU.mult).then_inc(max_done, 1)

            def reciprocals(h):
                dve.wait_ge(exp_done, h + 1)
                c = SS_SUM + 2 * (h % 4)
                v.reciprocal(rstd[:, c:c + 2], ss[:, c:c + 2]).then_inc(recip_done, 1)

            dve.wait_ge(masks_done, 4)
            for s in range(ALL_HEADS + 1):
                if s >= 1:
                    reciprocals(s - 1)
                if s < ALL_HEADS:
                    maxima(s)
                if s == 4:
                    dve.wait_ge(bcast_in, 4 * 16)
                    dve.wait_ge(group_done, SGU_GROUP + 1)
                    group_is_out(dve, C_U)
                    bank = pp[SGU_GROUP % 2]
                    for gg in range(GROUPS):
                        part = cube(bank[:, 256 * gg:256 * (gg + 1)], NT)
                        last = v.scalar_tensor_tensor(
                            part, part, cols[:, G_V + gg:G_V + gg + 1],
                            bs3[:, gg:gg + 1, :].to_broadcast([P, NT, P]), ALU.mult, ALU.add)
                    link(last)
                    v.tensor_tensor(ya[:, :], bank, ya[:, :], ALU.mult).then_inc(group_out[SGU_GROUP % 2], 1)

            for b in range(3):
                if b < 2:
                    dve.wait_ge(gate_sig, b + 1)
                else:
                    group_is_out(dve, C_GATE + 6)
                for half in range(2):
                    g = BR_GROUP + 2 * b + half
                    dve.wait_ge(group_done, g + 1)
                    gate = gates[:, b, 4 * half:4 * half + 4, :].rearrange("p j t -> p (j t)")
                    dst = mergedT_half(half) if b == 0 else product[half]
                    if b == 2:
                        dve.wait_ge(pool_added, half + 1)
                    v.tensor_tensor(dst, pp[g % 2], gate, ALU.mult).then_inc(group_out[g % 2], 1)
                    if b == 2:
                        group_is_out(dve, g)
                        v.tensor_tensor(mergedT_half(half), mergedT_half(half), dst, ALU.add).then_inc(merged, 1)

            for n in range(2):
                g = OUT_GROUP + n
                dve.wait_ge(group_done, g + 1)
                for t in range(NT):
                    last = v.tensor_tensor(x3[:, t, 512 * n:512 * (n + 1)], pp[g % 2][:, 512 * t:512 * (t + 1)],
                                           x3[:, t, 512 * n:512 * (n + 1)], ALU.add)
                last.then_inc(group_out[g % 2], 1)
            v.memset(ext[:, :, E:E + 4], SENTINEL)
            dve.wait_ge(x_ss, 2)
            v.tensor_reduce(ss[:, SS_X2SUM:SS_X2SUM + NT], cube(ss[:, SS_X2:SS_X2 + 4], NT), AX.X,
                            ALU.add).then_inc(x_sum, 1)
            dve.wait_ge(x_root, 1)
            link(v.reciprocal(rstd[:, SS_X2SUM:SS_X2SUM + NT], rstd[:, SS_X2SUM:SS_X2SUM + NT]))
            for n in range(2):
                for t in range(NT):
                    a = slice(512 * n, 512 * (n + 1))
                    v.scalar_tensor_tensor(h2[:, t, a], x3[:, t, a], rstd[:, SS_X2SUM + t:SS_X2SUM + t + 1],
                                           gffn_bc[:, a], ALU.mult, ALU.mult).then_inc(h2_done, 1)

            dve.wait_ge(logits_done, 1)
            link(v.tensor_tensor(ext[:, :, 0:E], cube(pp[0][:, 0:NT * E], NT),
                                 br_bc[:, :].unsqueeze(1).to_broadcast([P, NT, E]), ALU.add))
            top3, rep3 = cube(top8[:, :], NT), cube(rep8[:, :], NT)
            for t in range(NT):
                last = v.max(top3[:, t, :], ext[:, t, :])
            link(last)
            v.tensor_scalar(stat[:, 0:NT], top3[:, :, 0], -1.0, None, ALU.mult).then_inc(top_done, 1)
            link(v.tensor_copy(rep3[:, :, 0:TOP_K], top3[:, :, 0:TOP_K]))
            for t in range(NT):
                last = v.match_replace(ext2[:, t, :], rep3[:, t, :], ext[:, t, :], REPLACED)
            link(last)
            v.tensor_tensor(sel3, ext2[:, :, 0:E], ext[:, :, 0:E], ALU.not_equal).then_inc(sel_done, 1)
            dve.wait_ge(rank_done, 1)
            link(v.scalar_tensor_tensor(slot3, cube(pp[1][:, 0:NT * E], NT), 1.0, sel3, ALU.add, ALU.mult))

            def make_onehot(e):
                dve.wait_ge(st_done, e)
                for t in range(NT):
                    last = v.tensor_scalar(onehot[:, t, :], iota1[:, :], slot1[:, bass.ds(e + E * t, 1)], None,
                                           ALU.is_equal)
                last.then_inc(onehot_done, 1)

            for t in range(NT):
                last = v.tensor_scalar(onehot[:, t, :], iota1[:, :], slot3[:, t, 0:1], None, ALU.is_equal)
            last.then_inc(onehot_done, 1)

            v.tensor_copy(counts[:, :], pp[1][:, 2 * E:3 * E])
            dve.wait_ge(e_done, 1)
            link(v.tensor_tensor(e_exp, e_exp, sel3, ALU.mult))
            link(v.tensor_reduce(route[:, 0:NT], e_exp, AX.X, ALU.add))
            link(v.reciprocal(route[:, NT:2 * NT], route[:, 0:NT]))
            for t in range(NT):
                last = v.tensor_scalar(wgt3[:, t, :], e_exp[:, t, :], route[:, NT + t:NT + t + 1], None, ALU.mult)
            last.then_inc(wgt_done, 1)

            for b in range(BLOCKS - 1):
                last = v.tensor_scalar(flags[:, E * b:E * (b + 1)], counts[:, :],
                                       float(SLOTS * (b + 1)), None, ALU.is_gt)
            link(last)
            NF = (BLOCKS - 1) * E
            link(v.tensor_tensor_scan(incl, ones[:, 0:NF], flags, 0.0, ALU.mult, ALU.add))
            v.tensor_copy(n_items[:, :], incl[:, NF - 1:NF])
            v.memset(over[:, 0:1], 1.0)
            v.tensor_tensor(order, incl, flags, ALU.mult).then_inc(items_done, 1)

            LINKS = 6

            def swiglu(e, half):
                if half == 0:
                    dve.wait_ge(up_done, e + 1)
                else:
                    dve.wait_ge(ring_free, e * PER_EXPERT + UP_CHUNKS)
                a = slice(256 * half, 256 * (half + 1))
                gate_at = slice(512 * half, 512 * half + 256)
                up_at = slice(512 * half + 256, 512 * (half + 1))

                def bias(off):
                    return bguT[:, bass.ds(e * JT + (off + 4 * half), 4)].unsqueeze(2).to_broadcast([P, 4, SLOTS])

                def step(ins, n):
                    ins.then_inc(e_chain, 1)
                    dve.wait_ge(e_chain, e * LINKS + (3 * half + n))

                step(v.tensor_tensor(cube(glu[:, a], 4), cube(ps_h[:, gate_at], 4), bias(0), ALU.add), 1)
                v.tensor_scalar(glu[:, a], glu[:, a], LIMIT, None, ALU.min).then_inc(glu_done, 1)
                step(v.tensor_tensor(cube(lin[:, a], 4), cube(ps_h[:, up_at], 4), bias(FC), ALU.add), 2)
                step(v.tensor_scalar(lin[:, a], lin[:, a], -LIMIT, LIMIT, ALU.max, ALU.min), 3)
                v.scalar_tensor_tensor(lin[:, a], lin[:, a], 1.0, glu[:, a], ALU.add,
                                       ALU.mult).then_inc(lin_done, 1)
                dve.wait_ge(lin_done, e * 2 + (half + 1))
                dve.wait_ge(sig_done, e * 2 + (half + 1))
                v.tensor_tensor(act_h[:, a], lin[:, a], sig[:, a], ALU.mult).then_inc(h_done, 1)

            def sum_up(e, t):
                dve.wait_ge(scattered, e * NT + (NT + t + 1))
                v.scalar_tensor_tensor(x3[:, t, :], ps_add, wgt[:, bass.ds(e + E * t, 1)], x3[:, t, :],
                                       ALU.mult, ALU.add).then_inc(summed, 1)

            def sum_bias(t):
                dve.wait_ge(scattered, t + 1)
                v.tensor_tensor(x3[:, t, :], ps_add, x3[:, t, :], ALU.add).then_inc(summed, 1)

            make_onehot(1)
            sum_bias(0)
            swiglu(0, 0)
            swiglu(0, 1)
            sum_bias(1)
            with dve.Fori(1, E - 1) as e:
                make_onehot(e + 1)
                sum_up(e - 1, 0)
                swiglu(e, 0)
                swiglu(e, 1)
                sum_up(e - 1, 1)
            sum_up(E - 2, 0)
            swiglu(E - 1, 0)
            swiglu(E - 1, 1)
            sum_up(E - 2, 1)
            for t in range(NT):
                sum_up(E - 1, t)

            dve.sem_inc(o_sum, 1)
            OLINKS = 15
            n_over = dve.value_load(n_items[0:1, 0:1], min_val=0, max_val=ITEMS)
            with dve.Fori(0, ITEMS) as i:
                with dve.If(n_over > i):
                    count = [0]

                    def step(ins):
                        count[0] += 1
                        ins.then_inc(o_chain, 1)
                        dve.wait_ge(o_chain, i * OLINKS + count[0])

                    step(v.tensor_scalar(pick, order, over[:, 0:1], None, ALU.is_equal))
                    step(v.tensor_tensor(pick2, pick, item_e[:, :], ALU.mult))
                    step(v.tensor_reduce(over[:, 1:2], pick2, AX.X, ALU.add))
                    v.tensor_copy(over_e[:, :], over[:, 1:2]).then_inc(o_item, 1)
                    step(v.tensor_tensor(pick2, pick, item_b[:, :], ALU.mult))
                    step(v.tensor_reduce(over[:, 2:3], pick2, AX.X, ALU.add))
                    step(v.tensor_tensor(pick_e, pick[:, 0:E], pick[:, E:2 * E], ALU.add))
                    step(v.tensor_tensor(pick_e, pick_e, pick[:, 2 * E:3 * E], ALU.add))
                    for dst, src in ((3, slot3), (5, wgt3)):
                        step(v.tensor_tensor(cube(pick2[:, 0:NT * E], NT), src,
                                             pick_e.unsqueeze(1).to_broadcast([P, NT, E]), ALU.mult))
                        step(v.tensor_reduce(over[:, dst:dst + NT], cube(pick2[:, 0:NT * E], NT), AX.X, ALU.add))
                    step(v.tensor_scalar(over[:, 3:5], over[:, 3:5], over[:, 2:3], None, ALU.subtract))
                    dve.wait_ge(o_st, i + 1)
                    for t in range(NT):
                        last = v.tensor_scalar(onehot[:, t, :], iota1[:, :], over[:, 3 + t:4 + t], None,
                                               ALU.is_equal)
                    last.then_inc(o_onehot, 1)
                    v.tensor_scalar(over[:, 0:1], over[:, 0:1], 1.0, None, ALU.add)

                    dve.wait_ge(o_up, i + 1)
                    for dst, n in ((glu, 0), (lin, 1)):
                        for half in range(2):
                            b0 = FC * n + 4 * half
                            bias = over_bias[:, b0:b0 + 4].unsqueeze(2).to_broadcast([P, 4, SLOTS])
                            at = 512 * half + 256 * n
                            last = v.tensor_tensor(cube(dst[:, 256 * half:256 * (half + 1)], 4),
                                                   cube(ps_h[:, at:at + 256], 4), bias, ALU.add)
                    step(last)
                    v.tensor_scalar(glu, glu, LIMIT, None, ALU.min).then_inc(o_glu, 1)
                    step(v.tensor_scalar(lin, lin, -LIMIT, LIMIT, ALU.max, ALU.min))
                    step(v.scalar_tensor_tensor(lin, lin, 1.0, glu, ALU.add, ALU.mult))
                    assert count[0] == OLINKS
                    dve.wait_ge(o_sig, i + 1)
                    v.tensor_tensor(act_h, lin, sig, ALU.mult).then_inc(o_h, 1)
                    for t in range(NT):
                        dve.wait_ge(o_scat, i * NT + (t + 1))
                        v.scalar_tensor_tensor(x3[:, t, :], ps_add, over[:, 5 + t:6 + t], x3[:, t, :],
                                               ALU.mult, ALU.add).then_inc(o_sum, 1)


_INS = ['x', 'mem', 'g_mix', 'w_in', 'g_sgu_v', 'w_spatial', 'b_spatial', 'g_q_moba', 'g_k_moba',
        'g_mem', 'w_mem_kv', 'g_q_mem', 'g_k_mem', 'w_br_sgu', 'w_br_moba', 'w_br_mem', 'w_out',
        'g_ffn', 'w_router', 'b_router', 'w_gate_up', 'b_gate_up', 'w_down', 'b_down']


def kernel(**inputs):
    import numpy as np
    import concourse.bacc as bacc
    from concourse.bass_utils import run_bass_kernel_spmd

    nc = bacc.Bacc("TRN2", target_bir_lowering=False, num_devices=1)
    arrays, args = {}, []
    for name in _INS:
        a = np.ascontiguousarray(inputs[name])
        arrays[f"in_{name}"] = a
        args.append(nc.dram_tensor(f"in_{name}", a.shape, mybir.dt.from_np(a.dtype), kind="ExternalInput").ap())
    shape = inputs["x"].shape
    args.append(nc.dram_tensor("out_0", shape, F32, kind="ExternalOutput").ap())
    build(nc, *args)
    r = run_bass_kernel_spmd(nc, [arrays], core_ids=[0])
    return r.results[0]["out_0"]
```

```python
from contextlib import ExitStack

import concourse.bass as bass
from concourse import mybir

F32 = mybir.dt.float32
I32 = mybir.dt.int32
ALU = mybir.AluOpType
ACT = mybir.ActivationFunctionType
AX = mybir.AxisListType

P = 128
SLOTS = 64
RING = 6
CHUNK = 4096
NEG = -1e30
SENTINEL = -3e38
REPLACED = 3e38


def build(nc, x, mem, g_mix, w_in, g_sgu_v, w_spatial, b_spatial, g_q_moba, g_k_moba, g_mem,
          w_mem_kv, g_q_mem, g_k_mem, w_br_sgu, w_br_moba, w_br_mem, w_out, g_ffn, w_router,
          b_router, w_gate_up, b_gate_up, w_down, b_down, out):
    SEQ, D = x.shape[1], x.shape[2]
    NT = SEQ // P
    KC = D // P
    E = w_router.shape[2]
    TOP_K = 4
    EPS = 1e-6
    GROUPS = w_spatial.shape[1]
    WIDTH = w_br_sgu.shape[1]
    WC = WIDTH // P
    DH = g_q_moba.shape[1]
    HEADS = WIDTH // DH
    MDH = g_q_mem.shape[1]
    MHEADS = WIDTH // MDH
    F = w_down.shape[2]
    FC = F // P
    LIMIT, ALPHA = 7.0, 1.702
    BLOCKS = SEQ // SLOTS
    ITEMS = (SEQ * TOP_K - 1) // SLOTS
    GATE0 = 2 * WIDTH + 4 * WIDTH
    assert (NT, KC, WC, FC, GROUPS) == (2, 8, 4, 8, 4) and KC * 512 == CHUNK

    def col_block(w, n):
        return w[0][:, n * 512:(n + 1) * 512].rearrange("(c p) n -> p c n", p=P)

    def all_cols(w):
        return w[0].rearrange("(c p) n -> p c n", p=P)

    front = ([(col_block(w_in, n), KC) for n in (2, 3, 4, 5)] +
             [(col_block(w_mem_kv, n), KC) for n in (0, 1)] +
             [(col_block(w_in, n), KC) for n in (1, 0)] +
             [(col_block(w_in, 6 + n), KC) for n in range(6)] +
             [(all_cols(w), WC) for w in (w_br_sgu, w_br_moba, w_br_mem)] +
             [(col_block(w_out, n), KC) for n in (0, 1)])
    (C_QB, C_KB, C_VB, C_QM, C_MK, C_MV, C_VS, C_U, C_GATE) = range(9)
    C_BR, C_OUT = C_GATE + 6, C_GATE + 9
    NFRONT = len(front)
    UP_CHUNKS, DOWN_CHUNKS = 4, 2
    PER_EXPERT = UP_CHUNKS + DOWN_CHUNKS
    assert PER_EXPERT == RING

    with ExitStack() as ctx:
        def sb(name, cols, dt=F32):
            return ctx.enter_context(nc.sbuf_tensor(name, [P, cols], dt))

        def sem(name):
            return ctx.enter_context(nc.semaphore(name))

        def cube(ap, n):
            return ap.rearrange("p (a b) -> p a b", a=n)

        ring = sb("ring", RING * CHUNK)
        area_a = sb("area_a", 6144)
        area_b = sb("area_b", 2048)
        area_c = sb("area_c", 2048)
        area_d = sb("area_d", 6144)
        area_e = sb("area_e", 1024)
        area_f = sb("area_f", 1024)
        area_g = sb("area_g", 1024)
        ya = sb("ya", 1024)
        x_sb = sb("x_sb", NT * D)

        h_nat, mem_nat, memT = (cube(area_a[:, 2048 * n:2048 * (n + 1)], m)
                                for n, m in ((0, NT), (1, NT), (2, KC)))
        gates = area_a[:, :].rearrange("p (b j t) -> p b j t", b=3, j=KC)
        h2, h2T = cube(area_a[:, 0:2048], NT), cube(area_a[:, 2048:4096], KC)
        y_sb = area_a[:, 4096:4608]
        bgu_sb = area_b[0:E, :]
        hT = cube(area_b[:, :], KC)
        mergedT = hT
        nat = [cube(area_c[:, 1024 * n:1024 * (n + 1)], NT) for n in range(2)]
        yT = [cube(ya[:, :], WC)] + [cube(area_c[:, 1024 * n:1024 * (n + 1)], WC) for n in range(2)]
        qT, kT, qmT, kmT = (cube(area_d[:, 1024 * n:1024 * (n + 1)], WC) for n in range(4))
        v_moba, v_mem = (cube(area_d[:, 1024 * n:1024 * (n + 1)], NT) for n in (4, 5))
        squares = area_e[:, :]
        prob = [area_e[:, 512 * n:512 * (n + 1)] for n in range(2)]
        probT = [area_f[:, 512 * n:512 * (n + 1)] for n in range(2)]
        ws_nat = cube(area_f[:, 0:512], GROUPS)
        product = [area_e[:, :], area_f[:, :]]
        v_sgu = cube(area_g[:, :], NT)
        bdown_sb = area_g[0:E, :]
        x3 = cube(x_sb[:, :], NT)
        EB = KC * SLOTS
        xg, glu, sig, act_h, hT_sb = (area_d[:, n * EB:(n + 1) * EB] for n in range(5))
        onehot = cube(area_d[:, 4480:4480 + NT * P], NT)
        scatter = [area_d[:, 2560 + 256 * n:2560 + 256 * (n + 1)] for n in range(2)]
        expert_row = area_d[0:E, 3100:3100 + SLOTS]
        ext = cube(area_d[:, 3200:3200 + NT * (E + 4)], NT)
        ext2 = cube(area_d[:, 3300:3300 + NT * (E + 4)], NT)
        e_exp = cube(area_d[:, 3400:3400 + NT * E], NT)
        flags = area_d[:, 3500:3500 + (BLOCKS - 1) * E]
        incl = area_d[:, 3600:3600 + (BLOCKS - 1) * E]
        order = area_d[:, 3700:3700 + (BLOCKS - 1) * E]
        pick = area_d[:, 3800:3800 + (BLOCKS - 1) * E]
        pick2 = area_d[:, 3900:3900 + (BLOCKS - 1) * E]
        pick_e = area_d[:, 4000:4000 + E]
        wT_sb = area_d[0:E, 4200:4200 + SEQ]

        ident = sb("ident", P)
        before = sb("before", P)
        ones = sb("ones", P)
        iota1 = sb("iota1", 2 * SLOTS)
        part = sb("part", SLOTS)
        turn = sb("turn", 1)
        rel = sb("rel", 3 * P)
        item_e = sb("item_e", (BLOCKS - 1) * E)
        item_b = sb("item_b", (BLOCKS - 1) * E)
        eps = sb("eps", 1)
        rows = sb("rows", P)
        cols = sb("cols", 24)
        G_MIX, G_MEM, G_V, G_Q, G_K, G_QM, G_KM = 0, 8, 16, 20, 21, 22, 23
        wsT = sb("wsT", GROUPS * P)
        bs_bc = sb("bs_bc", GROUPS * P)
        wr_sb = sb("wr_sb", KC * E)
        br_bc = sb("br_bc", E)
        gffn_bc = sb("gffn_bc", D)
        ss = sb("ss", 96)
        rstd = sb("rstd", 96)
        stat = sb("stat", 8)
        top8 = sb("top8", 16)
        rep8 = sb("rep8", 16)
        sel = sb("sel", NT * E)
        slot1 = sb("slot1", NT * E)
        wgt = sb("wgt", NT * E)
        route = sb("route", 16)
        counts = sb("counts", E)
        n_items = sb("n_items", 1, I32)
        over = sb("over", 16)
        over_e = sb("over_e", 1, I32)
        wsT3, bs3 = cube(wsT[:, :], GROUPS), cube(bs_bc[:, :], GROUPS)
        wr3 = cube(wr_sb[:, :], KC)
        sel3, slot3, wgt3 = (cube(a[:, :], NT) for a in (sel, slot1, wgt))

        psum = ctx.enter_context(nc.psum_tensor("psum", [P, 8 * 512], F32))
        pp = [psum[:, 0:1024], psum[:, 1024:2048]]
        ps_score = [psum[:, 2048:2560], psum[:, 2560:3072]]
        ps_t = psum[:, 3072:3584]
        ps_o = psum[:, 3584:4096]
        tb_banks = [ps_score[0], ps_score[1], ps_t, ps_o]
        ps_gate, ps_up = psum[:, 0:512], psum[:, 512:1024]
        ps_add = psum[:, 1024:2048]
        ps_y = psum[:, 2048:2560]
        ps_hT = psum[:, 2560:3072]
        ps_x = psum[:, 3072:3584]
        ps_s = psum[:, 3584:4096]

        x_in, mem_in = [sem(f"x_in{t}") for t in range(NT)], sem("mem_in")
        gains_in, bcast_in, gains_scaled = sem("gains_in"), sem("bcast_in"), sem("gains_scaled")
        ws_in, bgu_in, bdown_in = sem("ws_in"), sem("bgu_in"), sem("bdown_in")
        ring_full = [sem(f"ring_full{n}") for n in range(RING)]
        ring_free = sem("ring_free")
        pool_const, masks_done, dve_const = sem("pool_const"), sem("masks_done"), sem("dve_const")
        sumsq, root, normed, head_ss = sem("sumsq"), sem("root"), sem("normed"), sem("head_ss")
        tb_done, tb_out = sem("tb_done"), sem("tb_out")
        group_done = sem("group_done")
        group_out = [sem(f"group_out{n}") for n in range(2)]
        s_done, max_done, exp_done = sem("s_done"), sem("max_done"), sem("exp_done")
        recip_done, prob_done = sem("recip_done"), sem("prob_done")
        pt_done, pt_out, pv_done, o_out = sem("pt_done"), sem("pt_out"), sem("pv_done"), sem("o_out")
        gate_sig, pool_added, merged = sem("gate_sig"), sem("pool_added"), sem("merged")
        x_ss, x_sum, x_root, h2_done = sem("x_ss"), sem("x_sum"), sem("x_root"), sem("h2_done")
        h2T_done, h2T_out, logits_done = sem("h2T_done"), sem("h2T_out"), sem("logits_done")
        top_done, e_done, sel_done, rank_done = sem("top_done"), sem("e_done"), sem("sel_done"), sem("rank_done")
        wgt_done, wT_done, wT_out, items_done = sem("wgt_done"), sem("wT_done"), sem("wT_out"), sem("items_done")
        onehot_done, gathered, xg_out = sem("onehot_done"), sem("gathered"), sem("xg_out")
        st_done, st_out = sem("st_done"), sem("st_out")
        glu_done, sig_done, h_done = sem("glu_done"), sem("sig_done"), sem("h_done")
        hT_done, hT_out, row_done = sem("hT_done"), sem("hT_out"), sem("row_done")
        y_out, scattered, summed = sem("y_out"), sem("scattered"), sem("summed")
        v_chain, e_chain, o_chain = sem("v_chain"), sem("e_chain"), sem("o_chain")
        o_item, o_onehot, o_gath, o_xg = sem("o_item"), sem("o_onehot"), sem("o_gath"), sem("o_xg")
        o_st, o_stout, o_full, o_up = sem("o_st"), sem("o_stout"), sem("o_full"), sem("o_up")
        o_glu, o_sig, o_h, o_down = sem("o_glu"), sem("o_sig"), sem("o_h"), sem("o_down")
        o_y, o_scat, o_sum = sem("o_y"), sem("o_scat"), sem("o_sum")
        o_hT, o_hTout, o_row = sem("o_hT"), sem("o_hTout"), sem("o_row")
        item_seen, out_done = sem("item_seen"), sem("out_done")

        def slot(n):
            return ring[:, (n % RING) * CHUNK:(n % RING + 1) * CHUNK]

        def fills(n):
            return 16 * (n // RING + 1)

        def expert_fills(e, k):
            n = NFRONT + k
            return (e + (n // RING + 1)) * 16

        up_slots = [NFRONT + k for k in range(UP_CHUNKS)]
        down_slots = [NFRONT + UP_CHUNKS + k for k in range(DOWN_CHUNKS)]

        def up_src(e, k):
            return w_gate_up[0, e][k * 2 * P:(k + 1) * 2 * P, :].rearrange("(c p) n -> p c n", p=P)

        def down_src(e, k):
            return w_down[0, e][k * 4 * P:(k + 1) * 4 * P, :].rearrange("(c p) n -> p c n", p=P)

        ALL_HEADS = HEADS + MHEADS
        HEAD_STEPS = 6 * 4

        def is_moba(h):
            return h < HEADS

        def score_segments(h):
            return [(0, P, 0), (P, 3 * P, 1)] if is_moba(h) else [(0, 256, 0), (256, 512, 1)]

        def o_unit(h):
            return h // 2 if is_moba(h) else HEADS // 2 + (h - HEADS)

        SGU_GROUP = C_GATE + 1
        BR_GROUP, OUT_GROUP = C_BR + 1, C_BR + 1 + 2 * 3

        def last_group(n):
            if n <= C_GATE:
                return n
            if n < C_BR:
                return n + 1
            return BR_GROUP + 2 * (n - C_BR) + 1 if n < C_OUT else OUT_GROUP + n - C_OUT

        def mergedT_half(half):
            return area_b[:, 1024 * half:1024 * (half + 1)]

        SS_X, SS_MEM, SS_V, SS_X2, SS_X2SUM, SS_QK, SS_SUM, SS_MAX = 0, 2, 4, 6, 10, 16, 80, 88

        def stat_r(h, t):
            return rstd[:, SS_SUM + 2 * (h % 4) + t:SS_SUM + 2 * (h % 4) + t + 1]

        def stat_s(h, t):
            return ss[:, SS_SUM + 2 * (h % 4) + t:SS_SUM + 2 * (h % 4) + t + 1]

        def stat_m(h, t):
            return ss[:, SS_MAX + 2 * (h % 4) + t:SS_MAX + 2 * (h % 4) + t + 1]

        def group_is_out(eng, g):
            eng.wait_ge(group_out[g % 2], g // 2 + 1)

        block = ctx.enter_context(nc.Block())

        @block.sync
        def _(sp):
            x_tiles = x[0].rearrange("(t p) d -> p t d", p=P)
            for t in range(NT):
                sp.dma_start(x3[:, t, :], x_tiles[:, t, :]).then_inc(x_in[t], 16)
            for dst, src in ((rows[G_MIX:G_MIX + KC, :], g_mix[0].rearrange("(c p) -> c p", p=P)),
                             (rows[G_MEM:G_MEM + KC, :], g_mem[0].rearrange("(c p) -> c p", p=P)),
                             (rows[G_V:G_V + WC, :], g_sgu_v[0].rearrange("(c p) -> c p", p=P)),
                             (rows[G_Q:G_Q + 1, 0:DH], g_q_moba), (rows[G_Q:G_Q + 1, DH:P], g_q_moba),
                             (rows[G_K:G_K + 1, 0:DH], g_k_moba), (rows[G_K:G_K + 1, DH:P], g_k_moba),
                             (rows[G_QM:G_QM + 1, :], g_q_mem), (rows[G_KM:G_KM + 1, :], g_k_mem)):
                sp.dma_start(dst, src).then_inc(gains_in, 16)
            for n, (src, c) in enumerate(front):
                if n >= RING:
                    sp.wait_ge(group_done, last_group(n - RING) + 1)
                sp.dma_start(cube(slot(n), c), src).then_inc(ring_full[n % RING], 16)
                if n == 0:
                    sp.dma_start(mem_nat, mem[0].rearrange("(t p) d -> p t d", p=P)).then_inc(mem_in, 16)
                if n == 1:
                    sp.dma_start(ws_nat, w_spatial[0].rearrange("g t s -> t g s")).then_inc(ws_in, 16)
                    for dst, src in ((bs_bc[:, :], b_spatial.rearrange("l g t -> l (g t)").to_broadcast(
                                         [P, GROUPS * P])),
                                     (wr3, w_router[0].rearrange("(c p) e -> p c e", p=P)),
                                     (br_bc[:, :], b_router.to_broadcast([P, E])),
                                     (gffn_bc[:, :], g_ffn.to_broadcast([P, D]))):
                        sp.dma_start(dst, src).then_inc(bcast_in, 16)
                if n == C_GATE + 3:
                    sp.wait_ge(group_done, SGU_GROUP + 1)
                    sp.dma_start(bdown_sb, b_down[0]).then_inc(bdown_in, 16)

            def expert_chunk(e, k):
                n = NFRONT + k
                src, c = (up_src(e, k), 2) if k < UP_CHUNKS else (down_src(e, k - UP_CHUNKS), 4)
                sp.dma_start(cube(slot(n), c), src).then_inc(ring_full[n % RING], 16)

            for k in range(PER_EXPERT):
                sp.wait_ge(group_done, last_group(NFRONT - RING + k) + 1)
                expert_chunk(0, k)
            sp.dma_start(bgu_sb, b_gate_up[0]).then_inc(bgu_in, 16)
            with sp.Fori(1, E) as e:
                for k in range(PER_EXPERT):
                    sp.wait_ge(ring_free, e * PER_EXPERT + (k + 1 - PER_EXPERT))
                    expert_chunk(e, k)

            sp.wait_ge(items_done, 1)
            n_over = sp.value_load(n_items[0:1, 0:1], min_val=0, max_val=ITEMS)
            with sp.Fori(0, ITEMS) as i:
                with sp.If(n_over > i):
                    sp.wait_ge(o_item, i + 1)
                    sp.wait_ge(o_down, i + 1)
                    sp.wait_ge(ring_free, E * PER_EXPERT)
                    sp.sem_inc(item_seen, 1)
                    oe = sp.value_load(over_e[0:1, 0:1], min_val=0, max_val=E - 1)
                    for k in range(UP_CHUNKS):
                        sp.dma_start(cube(slot(up_slots[k]), 2), up_src(oe, k)).then_inc(o_full, 16)
                    for k in range(DOWN_CHUNKS):
                        sp.dma_start(cube(slot(down_slots[k]), 4), down_src(oe, k)).then_inc(o_full, 16)

            sp.wait_ge(summed, NT * (E + 1))
            sp.wait_ge(o_sum, n_over * NT + 1)
            sp.dma_start(out[0].rearrange("(t p) d -> p t d", p=P), x3).then_inc(out_done, 16)
            sp.wait_ge(out_done, 16)

        @block.gpsimd
        def _(pool):
            nc.gpsimd.memset(ident[:, :], 0.0).then_inc(pool_const, 1)
            nc.gpsimd.memset(before[:, :], 1.0).then_inc(pool_const, 1)
            nc.gpsimd.memset(ones[:, :], 1.0).then_inc(pool_const, 1)
            pool.wait_ge(pool_const, 3)
            nc.gpsimd.affine_select(out=ident[:, :], in_=ident[:, :], compare_op=ALU.not_equal, fill=1.0,
                                    base=0, pattern=[[-1, P]], channel_multiplier=1).then_inc(masks_done, 1)

            nc.gpsimd.affine_select(out=before[:, :], in_=before[:, :], compare_op=ALU.is_gt, fill=0.0,
                                    base=0, pattern=[[1, P]], channel_multiplier=-1).then_inc(masks_done, 1)
            nc.gpsimd.iota(rel[:, 0:P], pattern=[[1, P]], base=0, channel_multiplier=-1,
                           allow_small_or_imprecise_dtypes=True).then_inc(pool_const, 1)
            nc.gpsimd.iota(rel[:, P:3 * P], pattern=[[1, 2 * P]], base=-P, channel_multiplier=-1,
                           allow_small_or_imprecise_dtypes=True).then_inc(pool_const, 1)
            nc.gpsimd.iota(iota1[:, :], pattern=[[0, 2], [1, SLOTS]], base=1, channel_multiplier=0,
                           allow_small_or_imprecise_dtypes=True).then_inc(pool_const, 1)
            nc.gpsimd.iota(part[:, :], pattern=[[0, SLOTS]], base=0, channel_multiplier=1,
                           allow_small_or_imprecise_dtypes=True).then_inc(pool_const, 1)
            nc.gpsimd.iota(item_e[:, :], pattern=[[0, BLOCKS - 1], [1, E]], base=0, channel_multiplier=0,
                           allow_small_or_imprecise_dtypes=True).then_inc(pool_const, 1)
            nc.gpsimd.iota(item_b[:, :], pattern=[[SLOTS, BLOCKS - 1], [0, E]], base=SLOTS,
                           channel_multiplier=0, allow_small_or_imprecise_dtypes=True).then_inc(pool_const, 1)
            pool.wait_ge(pool_const, 9)
            nc.gpsimd.affine_select(out=rel[:, 0:P], in_=rel[:, 0:P], compare_op=ALU.is_ge, fill=NEG,
                                    base=0, pattern=[[-1, P]], channel_multiplier=1).then_inc(masks_done, 1)
            nc.gpsimd.affine_select(out=rel[:, P:3 * P], in_=rel[:, P:3 * P], compare_op=ALU.is_ge, fill=NEG,
                                    base=P, pattern=[[-1, 2 * P]], channel_multiplier=1).then_inc(masks_done, 1)
            pool.wait_ge(ws_in, 16)
            nc.gpsimd.affine_select(out=ws_nat, in_=ws_nat, compare_op=ALU.is_ge, fill=0.0, base=0,
                                    pattern=[[0, GROUPS], [-1, P]], channel_multiplier=1).then_inc(masks_done, 1)

            for h in range(ALL_HEADS):
                pool.wait_ge(recip_done, h + 1)
                for a, b, t in score_segments(h):
                    last = nc.gpsimd.tensor_scalar(prob[h % 2][:, a:b], prob[h % 2][:, a:b],
                                                   stat_r(h, t), None, ALU.mult)
                last.then_inc(prob_done, 1)
            for half in range(2):
                group_is_out(pool, BR_GROUP + 2 + half)
                nc.gpsimd.tensor_tensor(cube(mergedT_half(half), 4), cube(mergedT_half(half), 4),
                                        cube(product[half], 4), ALU.add).then_inc(pool_added, 1)

        @block.scalar
        def _(act):
            def copy(dst, src, **kw):
                return nc.scalar.activation(dst, src, ACT.Copy, **kw)

            def take_root(cols_, n, count):
                return nc.scalar.activation(rstd[:, cols_:cols_ + n], ss[:, cols_:cols_ + n], ACT.Sqrt,
                                            bias=eps[:, 0:1], scale=1.0 / count).then_inc(root, 1)

            act.wait_ge(dve_const, 1)
            nc.scalar.activation(stat[:, 4:5], eps[:, :], ACT.Sqrt)
            for t in range(NT):
                act.wait_ge(x_in[t], 16)
                nc.scalar.activation(squares, x3[:, t, :], ACT.Square,
                                     accum_out=ss[:, SS_X + t:SS_X + t + 1]).then_inc(sumsq, 1)
                act.wait_ge(sumsq, t + 1)
            take_root(SS_X, NT, D)

            batch = [0]

            def batch_out(*copies):
                b = batch[0]
                act.wait_ge(tb_done, b + 1)
                for dst, col, width, scale in copies:
                    last = copy(dst, tb_banks[b % 4][:, col:col + width],
                                **({} if scale is None else {"scale": scale}))
                last.then_inc(tb_out, 1)
                batch[0] += 1

            def model_chunks(dstT, gain):
                for m in range(KC // 2):
                    batch_out(*((dstT[:, 2 * m + c, :], 256 * c, 256,
                                 cols[:, gain + 2 * m + c:gain + 2 * m + c + 1]) for c in range(2)))

            def heads_out(dstT, gain):
                for t in range(NT):
                    batch_out((dstT[:, :, t * P:(t + 1) * P], 0, 512, cols[:, gain:gain + 1]))

            def group_copy(g, dst, func=ACT.Copy):
                act.wait_ge(group_done, g + 1)
                for half in range(2):
                    last = nc.scalar.activation(dst[half], pp[g % 2][:, 512 * half:512 * (half + 1)], func)
                last.then_inc(group_out[g % 2], 1)

            def halves(ap):
                return [ap[:, n, :] for n in range(2)]

            batch_out((cols[:, 0:24], 0, 24, None))
            act.wait_ge(tb_out, 1)
            for c, n in ((G_Q, DH), (G_QM, MDH)):
                copy(cols[:, c:c + 1], cols[:, c:c + 1], scale=float(n) ** -0.5).then_inc(gains_scaled, 1)
            model_chunks(hT, G_MIX)
            act.wait_ge(mem_in, 16)
            for t in range(NT):
                nc.scalar.activation(squares, mem_nat[:, t, :], ACT.Square,
                                     accum_out=ss[:, SS_MEM + t:SS_MEM + t + 1]).then_inc(sumsq, 1)
                act.wait_ge(sumsq, NT + t + 1)
            take_root(SS_MEM, NT, D)
            group_copy(C_QB, halves(nat[0]))
            act.wait_ge(head_ss, 1)
            take_root(SS_QK, NT * HEADS, DH)
            model_chunks(memT, G_MEM)
            group_copy(C_KB, halves(nat[1]))
            act.wait_ge(head_ss, 2)
            take_root(SS_QK + 16, NT * HEADS, DH)
            batch_out((wsT[:, :], 0, 512, None))
            act.wait_ge(gains_scaled, 2)
            heads_out(qT, G_Q)
            group_copy(C_VB, halves(v_moba))
            heads_out(kT, G_K)
            group_copy(C_QM, halves(nat[0]))
            act.wait_ge(head_ss, 3)
            take_root(SS_QK + 32, NT * MHEADS, MDH)
            group_copy(C_MK, halves(nat[1]))
            act.wait_ge(head_ss, 4)
            take_root(SS_QK + 48, NT * MHEADS, MDH)
            heads_out(qmT, G_QM)
            group_copy(C_MV, halves(v_mem))
            heads_out(kmT, G_KM)
            group_copy(C_VS, halves(v_sgu), ACT.Gelu)
            group_copy(C_U, [ya[:, 0:512], ya[:, 512:1024]], ACT.Gelu)
            act.wait_ge(head_ss, 5)
            take_root(SS_V, NT, WIDTH)

            def exps(h):
                act.wait_ge(max_done, h + 1)
                for a, b, t in score_segments(h):
                    src = prob[h % 2][:, a:b] if is_moba(h) else ps_score[h % 2][:, a:b]
                    last = nc.scalar.activation(prob[h % 2][:, a:b], src, ACT.Exp, bias=stat_m(h, t),
                                                accum_out=stat_s(h, t))
                last.then_inc(exp_done, 1)

            def prob_out(h):
                act.wait_ge(pt_done, h + 1)
                if h >= 2:
                    act.wait_ge(pv_done, h - 1)
                width = 3 * P if is_moba(h) else 4 * P
                copy(probT[h % 2][:, 0:width], ps_t[:, 0:width]).then_inc(pt_out, 1)

            def head_out(h):
                act.wait_ge(pv_done, h + 1)
                u = o_unit(h)
                dst = yT[1][:, u, :] if is_moba(h) else yT[2][:, h - HEADS, :]
                copy(dst, ps_o[:, 256 * (u % 2):256 * (u % 2 + 1)]).then_inc(o_out, 1)

            def gate_out(m):
                g = C_GATE if m == 0 else C_GATE + 1 + m
                dst = gates[:, m // 2, 4 * (m % 2):4 * (m % 2) + 4, :].rearrange("p j t -> p (j t)")
                group_copy(g, [dst[:, 0:512], dst[:, 512:1024]], ACT.Sigmoid if m >= 4 else ACT.Copy)

            for s in range(HEAD_STEPS):
                if 2 <= s < ALL_HEADS + 2:
                    prob_out(s - 2)
                if s < ALL_HEADS:
                    exps(s)
                if 3 <= s < ALL_HEADS + 3 and (not is_moba(s - 3) or (s - 3) % 2 == 1):
                    head_out(s - 3)
                if s % 4 == 3:
                    gate_out(s // 4)
                if s == 16:
                    for b in range(2):
                        group_is_out(act, C_GATE + 2 + 2 * b)
                        both = gates[:, b, :, :].rearrange("p j t -> p (j t)")
                        nc.scalar.activation(both, both, ACT.Sigmoid).then_inc(gate_sig, 1)

            for n in range(2):
                group_is_out(act, OUT_GROUP + n)
                for t in range(NT):
                    last = nc.scalar.activation(product[n][:, 512 * t:512 * (t + 1)],
                                                x3[:, t, 512 * n:512 * (n + 1)], ACT.Square,
                                                accum_out=ss[:, SS_X2 + 2 * t + n:SS_X2 + 2 * t + n + 1])
                last.then_inc(x_ss, 1)
            act.wait_ge(x_sum, 1)
            nc.scalar.activation(rstd[:, SS_X2SUM:SS_X2SUM + NT], ss[:, SS_X2SUM:SS_X2SUM + NT], ACT.Sqrt,
                                 bias=eps[:, 0:1], scale=1.0 / D).then_inc(x_root, 1)
            for m in range(KC // 2):
                act.wait_ge(h2T_done, m + 1)
                copy(h2T[:, 2 * m:2 * m + 2, :].rearrange("p c t -> p (c t)"), tb_banks[m]).then_inc(h2T_out, 1)
            act.wait_ge(top_done, 1)
            for t in range(NT):
                last = nc.scalar.activation(e_exp[:, t, :], ext[:, t, 0:E], ACT.Exp, bias=stat[:, t:t + 1])
            last.then_inc(e_done, 1)

            def tokens_out(e, parity):
                act.wait_ge(gathered, e + 1)
                copy(xg, ps_x).then_inc(xg_out, 1)
                act.wait_ge(st_done, e + 1)
                copy(scatter[parity], ps_s[:, 0:NT * P]).then_inc(st_out, 1)

            def y_copy(e):
                act.wait_ge(ring_free, e * PER_EXPERT + PER_EXPERT)
                copy(y_sb, ps_y).then_inc(y_out, 1)

            def sigmoid(e):
                act.wait_ge(glu_done, e + 1)
                nc.scalar.activation(sig, glu, ACT.Sigmoid, scale=ALPHA).then_inc(sig_done, 1)

            def hidden_out(e):
                act.wait_ge(hT_done, e + 1)
                copy(hT_sb, ps_hT).then_inc(hT_out, 1)

            tokens_out(0, 0)
            act.wait_ge(wT_done, 1)
            copy(wT_sb, ps_y[0:E, 0:SEQ]).then_inc(wT_out, 1)
            sigmoid(0)
            tokens_out(1, 1)
            hidden_out(0)
            with act.Fori(0, (E - 2) // 2) as pair:
                for parity, e in ((1, pair * 2 + 1), (0, pair * 2 + 2)):
                    y_copy(e - 1)
                    sigmoid(e)
                    tokens_out(e + 1, 1 - parity)
                    hidden_out(e)
            y_copy(E - 2)
            sigmoid(E - 1)
            hidden_out(E - 1)
            y_copy(E - 1)

            act.wait_ge(items_done, 1)
            n_over = act.value_load(n_items[0:1, 0:1], min_val=0, max_val=ITEMS)
            with act.Fori(0, ITEMS) as i:
                with act.If(n_over > i):
                    act.wait_ge(o_gath, i + 1)
                    copy(xg, ps_x).then_inc(o_xg, 1)
                    act.wait_ge(o_st, i + 2)
                    copy(scatter[0], ps_s[:, 0:NT * P]).then_inc(o_stout, 1)
                    act.wait_ge(o_glu, i + 1)
                    nc.scalar.activation(sig, glu, ACT.Sigmoid, scale=ALPHA).then_inc(o_sig, 1)
                    act.wait_ge(o_hT, i + 1)
                    copy(hT_sb, ps_hT).then_inc(o_hTout, 1)
                    act.wait_ge(o_down, i + 2)
                    copy(y_sb, ps_y).then_inc(o_y, 1)

        @block.tensor
        def _(pe):
            mm = nc.tensor.matmul
            batch = [0]

            def transposes(*parts):
                b = batch[0]
                if b >= 4:
                    pe.wait_ge(tb_out, b - 3)
                for src, col in parts:
                    k = src.shape[0]
                    last = nc.tensor.transpose(tb_banks[b % 4][:, col:col + k], src, ident[0:k, 0:k])
                last.then_inc(tb_done, 1)
                batch[0] += 1

            def model_batches(src):
                for m in range(KC // 2):
                    transposes(*((src[:, t, (2 * m + c) * P:(2 * m + c + 1) * P], 256 * c + P * t)
                                 for c in range(2) for t in range(NT)))

            def head_batches(src):
                for t in range(NT):
                    transposes(*((src[:, t, c * P:(c + 1) * P], P * c) for c in range(WC)))

            def start_group(g):
                if g >= 2:
                    group_is_out(pe, g - 2)

            def chunk_in(n):
                pe.wait_ge(ring_full[n % RING], fills(n))
                return cube(slot(n), front[n][1])

            def natural(n, g, lhsT):
                start_group(g)
                w = chunk_in(n)
                for t in range(NT):
                    for c in range(KC):
                        last = mm(pp[g % 2][:, 512 * t:512 * (t + 1)], lhsT[:, c, t * P:(t + 1) * P],
                                  w[:, c, :], start=(c == 0), stop=(c == KC - 1))
                last.then_inc(group_done, 1)

            def column_tile(w, g, j, col, rhs, nk):
                for c in range(nk):
                    last = mm(pp[g % 2][:, 256 * j:256 * (j + 1)], w[:, c, col:col + P], rhs[:, c, :],
                              start=(c == 0), stop=(c == nk - 1))
                return last

            pe.wait_ge(masks_done, 1)
            pe.wait_ge(gains_in, 9 * 16)
            transposes((rows[0:24, :], 0))
            pe.wait_ge(normed, NT)
            model_batches(h_nat)
            pe.wait_ge(tb_out, 5)
            natural(C_QB, C_QB, hT)
            pe.wait_ge(normed, 2 * NT)
            model_batches(mem_nat)
            natural(C_KB, C_KB, hT)
            pe.wait_ge(masks_done, 5)
            transposes(*((ws_nat[:, g, :], P * g) for g in range(GROUPS)))
            pe.wait_ge(normed, 2 * NT + 1)
            head_batches(nat[0])
            natural(C_VB, C_VB, hT)
            pe.wait_ge(normed, 2 * NT + 2)
            head_batches(nat[1])
            natural(C_QM, C_QM, hT)
            pe.wait_ge(tb_out, 9)
            natural(C_MK, C_MK, memT)
            pe.wait_ge(normed, 2 * NT + 3)
            head_batches(nat[0])
            natural(C_MV, C_MV, memT)
            pe.wait_ge(normed, 2 * NT + 4)
            head_batches(nat[1])
            natural(C_VS, C_VS, hT)
            start_group(C_U)
            w = chunk_in(C_U)
            for j in range(4):
                last = column_tile(w, C_U, j, j * P, hT, KC)
            last.then_inc(group_done, 1)

            pe.wait_ge(tb_out, batch[0])

            def scores(h):
                if h >= 2:
                    pe.wait_ge(exp_done, h - 1)
                bank = ps_score[h % 2]
                if is_moba(h):
                    rows_, pair = slice(DH * (h % 2), DH * (h % 2 + 1)), h // 2
                    mm(bank[:, 0:P], qT[rows_, pair, 0:P], kT[rows_, pair, 0:P], start=True, stop=True)
                    last = mm(bank[:, P:3 * P], qT[rows_, pair, P:2 * P], kT[rows_, pair, :],
                              start=True, stop=True)
                else:
                    for t in range(NT):
                        last = mm(bank[:, 256 * t:256 * (t + 1)], qmT[:, h - HEADS, t * P:(t + 1) * P],
                                  kmT[:, h - HEADS, :], start=True, stop=True)
                last.then_inc(s_done, 1)

            def prob_transposes(h):
                pe.wait_ge(prob_done, h + 1)
                if h >= 1:
                    pe.wait_ge(pt_out, h)
                moves = [(0, 0), (1, 1), (2, 2)] if is_moba(h) else [(0, 0), (1, 2), (2, 1), (3, 3)]
                for a, b in moves:
                    last = nc.tensor.transpose(ps_t[:, b * P:(b + 1) * P], prob[h % 2][:, a * P:(a + 1) * P],
                                               ident[:, :])
                last.then_inc(pt_done, 1)

            def values(h):
                pe.wait_ge(pt_out, h + 1)
                u = o_unit(h)
                if u >= 1:
                    pe.wait_ge(o_out, u)
                c0, p2 = 256 * (u % 2), probT[h % 2]
                if is_moba(h):
                    r0 = DH * (h % 2)
                    mm(ps_o[r0:r0 + DH, c0:c0 + 256], v_moba[:, 0, h * DH:(h + 1) * DH], p2[:, 0:256],
                       start=True, stop=False, skip_group_check=True)
                    last = mm(ps_o[r0:r0 + DH, c0 + P:c0 + 256], v_moba[:, 1, h * DH:(h + 1) * DH],
                              p2[:, 256:384], start=False, stop=True, skip_group_check=True)
                else:
                    for t in range(2):
                        last = mm(ps_o[:, c0:c0 + 256], v_mem[:, t, (h - HEADS) * MDH:(h - HEADS + 1) * MDH],
                                  p2[:, 256 * t:256 * (t + 1)], start=(t == 0), stop=(t == 1))
                last.then_inc(pv_done, 1)

            for s in range(HEAD_STEPS):
                if 3 <= s < ALL_HEADS + 3:
                    values(s - 3)
                if 2 <= s < ALL_HEADS + 2:
                    prob_transposes(s - 2)
                if s < ALL_HEADS:
                    scores(s)
                m, j = divmod(s, 4)
                g = C_GATE if m == 0 else C_GATE + 1 + m
                if j == 0:
                    start_group(g)
                    w = chunk_in(C_GATE + m)
                last = column_tile(w, g, j, j * P, hT, KC)
                if j == 3:
                    last.then_inc(group_done, 1)
                if s == 3:
                    start_group(SGU_GROUP)
                    pe.wait_ge(normed, 2 * NT + 5)
                    for gg in range(GROUPS):
                        for t in range(NT):
                            last = mm(pp[SGU_GROUP % 2][:, 256 * gg + P * t:256 * gg + P * (t + 1)],
                                      v_sgu[:, t, gg * P:(gg + 1) * P], wsT3[:, gg, :], start=True, stop=True)
                    last.then_inc(group_done, 1)

            for b in range(3):
                w = chunk_in(C_BR + b)
                if b == 0:
                    group_is_out(pe, SGU_GROUP)
                else:
                    pe.wait_ge(o_out, WC * b)
                for half in range(2):
                    g = BR_GROUP + 2 * b + half
                    start_group(g)
                    for j in range(4):
                        last = column_tile(w, g, j, (4 * half + j) * P, yT[b], WC)
                    last.then_inc(group_done, 1)
            for n in range(2):
                g = OUT_GROUP + n
                start_group(g)
                w = chunk_in(C_OUT + n)
                for c in range(KC):
                    if n == 0 and c % 4 == 0:
                        pe.wait_ge(merged, c // 4 + 1)
                    for t in range(NT):
                        last = mm(pp[g % 2][:, 512 * t:512 * (t + 1)], mergedT[:, c, t * P:(t + 1) * P],
                                  w[:, c, :], start=(c == 0), stop=(c == KC - 1))
                last.then_inc(group_done, 1)

            for m in range(KC // 2):
                pe.wait_ge(h2_done, NT * (m // 2 + 1))
                for c in range(2):
                    for t in range(NT):
                        last = nc.tensor.transpose(tb_banks[m][:, 256 * c + P * t:256 * c + P * (t + 1)],
                                                   h2[:, t, (2 * m + c) * P:(2 * m + c + 1) * P], ident[:, :])
                last.then_inc(h2T_done, 1)
            pe.wait_ge(bcast_in, 4 * 16)
            pe.wait_ge(h2T_out, KC // 2)
            for t in range(NT):
                for c in range(KC):
                    last = mm(pp[0][:, E * t:E * (t + 1)], h2T[:, c, t * P:(t + 1) * P], wr3[:, c, :],
                              start=(c == 0), stop=(c == KC - 1))
            last.then_inc(logits_done, 1)
            pe.wait_ge(masks_done, 2)
            pe.wait_ge(sel_done, 1)
            mm(pp[1][:, 0:E], before[:, :], sel3[:, 0, :], start=True, stop=True)
            mm(pp[1][:, E:2 * E], ones[:, :], sel3[:, 0, :], start=True, stop=False)
            mm(pp[1][:, E:2 * E], before[:, :], sel3[:, 1, :], start=False, stop=True)
            mm(pp[1][:, 2 * E:3 * E], ones[:, :], sel3[:, 0, :], start=True, stop=False)
            mm(pp[1][:, 2 * E:3 * E], ones[:, :], sel3[:, 1, :], start=False, stop=True).then_inc(rank_done, 1)

            def gather_mms():
                for c in range(KC):
                    for t in range(NT):
                        last = mm(ps_x[:, SLOTS * c:SLOTS * (c + 1)], h2[:, t, c * P:(c + 1) * P],
                                  onehot[:, t, 0:SLOTS], start=(t == 0), stop=(t == NT - 1))
                return last

            def scatter_transposes():
                for t in range(NT):
                    last = nc.tensor.transpose(ps_s[:, P * t:P * (t + 1)], onehot[:, t, :], ident[:, :])
                return last

            def bias_mms():
                for bank, col in ((ps_gate, 0), (ps_up, F)):
                    for half in range(2):
                        mm(bank[SLOTS * half:SLOTS * (half + 1), :], expert_row,
                           bgu_sb[:, col + 512 * half:col + 512 * (half + 1)], start=True, stop=False)

            def up_mms(k):
                w = cube(slot(up_slots[k]), 2)
                for c in range(2):
                    kc = 2 * k + c
                    for bank, col in ((ps_gate, 0), (ps_up, F)):
                        for half in range(2):
                            last = mm(bank[SLOTS * half:SLOTS * (half + 1), :],
                                      xg[:, SLOTS * kc:SLOTS * (kc + 1)],
                                      w[:, c, col + 512 * half:col + 512 * (half + 1)],
                                      start=False, stop=(kc == KC - 1))
                return last

            def hidden_transposes():
                for c in range(4):
                    last = nc.tensor.transpose(ps_hT[:, P * c:P * (c + 1)], act_h[:, P * c:P * (c + 1)],
                                               ident[:, :])
                return last

            def down_mms(k):
                w = cube(slot(down_slots[k]), 4)
                for c in range(4):
                    for half in range(2):
                        last = mm(ps_y[SLOTS * half:SLOTS * (half + 1), :],
                                  hT_sb[:, P * c + SLOTS * k:P * c + SLOTS * (k + 1)],
                                  w[:, c, 512 * half:512 * (half + 1)],
                                  start=(k == 0 and c == 0), stop=(k == 1 and c == 3))
                return last

            def gather(e):
                pe.wait_ge(onehot_done, e + 1)
                pe.wait_ge(xg_out, e)
                pe.wait_ge(st_out, e)
                gather_mms().then_inc(gathered, 1)
                scatter_transposes().then_inc(st_done, 1)

            def scatter_mms(t, parity):
                for half in range(2):
                    rows_ = slice(SLOTS * half, SLOTS * (half + 1))
                    last = mm(ps_add[:, 512 * half:512 * (half + 1)], scatter[parity][rows_, t * P:(t + 1) * P],
                              y_sb[rows_, :], start=True, stop=True)
                return last

            def scatter_back(e, t, parity):
                if t == 0:
                    pe.wait_ge(y_out, e + 1)
                    pe.wait_ge(st_out, e + 1)
                pe.wait_ge(summed, e * NT + (NT + t))
                scatter_mms(t, parity).then_inc(scattered, 1)

            def expert(e, between, after):
                pe.wait_ge(xg_out, e + 1)
                pe.wait_ge(row_done, e + 1)
                bias_mms()
                for k in range(UP_CHUNKS):
                    n = up_slots[k]
                    pe.wait_ge(ring_full[n % RING], expert_fills(e, k))
                    up_mms(k).then_inc(ring_free, 1)
                    if k == 1:
                        between()
                after()
                pe.wait_ge(h_done, e + 1)
                hidden_transposes().then_inc(hT_done, 1)
                pe.wait_ge(hT_out, e + 1)
                for k in range(DOWN_CHUNKS):
                    n = down_slots[k]
                    pe.wait_ge(ring_full[n % RING], expert_fills(e, UP_CHUNKS + k))
                    down_mms(k).then_inc(ring_free, 1)

            def bias_back(t):
                if t == 0:
                    pe.wait_ge(wT_out, 1)
                    pe.wait_ge(bdown_in, 16)
                else:
                    pe.wait_ge(summed, t)
                for n in range(2):
                    last = mm(ps_add[:, 512 * n:512 * (n + 1)], wT_sb[:, t * P:(t + 1) * P],
                              bdown_sb[:, 512 * n:512 * (n + 1)], start=True, stop=True)
                last.then_inc(scattered, 1)

            gather(0)
            pe.wait_ge(wgt_done, 1)
            for t in range(NT):
                last = nc.tensor.transpose(ps_y[0:E, P * t:P * (t + 1)], wgt3[:, t, :], ident[:, :])
            last.then_inc(wT_done, 1)

            def after_first():
                bias_back(1)
                gather(1)

            pe.wait_ge(bgu_in, 16)
            expert(0, lambda: bias_back(0), after_first)
            with pe.Fori(0, (E - 2) // 2) as pair:
                for parity, e in ((1, pair * 2 + 1), (0, pair * 2 + 2)):
                    def between():
                        scatter_back(e - 1, 0, 1 - parity)

                    def after():
                        scatter_back(e - 1, 1, 1 - parity)
                        gather(e + 1)

                    expert(e, between, after)
            expert(E - 1, lambda: scatter_back(E - 2, 0, 0), lambda: scatter_back(E - 2, 1, 0))
            for t in range(NT):
                scatter_back(E - 1, t, 1)

            pe.sem_inc(o_down, 1)
            pe.sem_inc(o_st, 1)
            pe.wait_ge(items_done, 1)
            n_over = pe.value_load(n_items[0:1, 0:1], min_val=0, max_val=ITEMS)
            with pe.Fori(0, ITEMS) as i:
                with pe.If(n_over > i):
                    pe.wait_ge(o_onehot, i + 1)
                    gather_mms().then_inc(o_gath, 1)
                    scatter_transposes().then_inc(o_st, 1)
                    pe.wait_ge(o_full, i * 96 + 96)
                    pe.wait_ge(o_xg, i + 1)
                    pe.wait_ge(o_row, i + 1)
                    bias_mms()
                    for k in range(UP_CHUNKS):
                        last = up_mms(k)
                    last.then_inc(o_up, 1)
                    pe.wait_ge(o_h, i + 1)
                    hidden_transposes().then_inc(o_hT, 1)
                    pe.wait_ge(o_hTout, i + 1)
                    for k in range(DOWN_CHUNKS):
                        last = down_mms(k)
                    last.then_inc(o_down, 1)
                    pe.wait_ge(o_y, i + 1)
                    pe.wait_ge(o_stout, i + 1)
                    pe.wait_ge(summed, NT * (E + 1))
                    scatter_mms(0, 0).then_inc(o_scat, 1)
                    pe.wait_ge(o_sum, i * NT + 2)
                    scatter_mms(1, 0).then_inc(o_scat, 1)
                    pe.wait_ge(o_sum, i * NT + 3)

        @block.vector
        def _(dve):
            v = nc.vector
            links = [0]

            def link(ins):
                links[0] += 1
                ins.then_inc(v_chain, 1)
                dve.wait_ge(v_chain, links[0])

            link(v.memset(eps[:, :], EPS))
            link(v.memset(turn[:, :], 0.0))
            v.memset(rep8[:, :], SENTINEL).then_inc(dve_const, 1)

            for n, (src, dst, col) in enumerate(((x3, h_nat, SS_X), (mem_nat, mem_nat, SS_MEM))):
                dve.wait_ge(root, n + 1)
                link(v.reciprocal(rstd[:, col:col + NT], rstd[:, col:col + NT]))
                for t in range(NT):
                    v.tensor_scalar(dst[:, t, :], src[:, t, :], rstd[:, col + t:col + t + 1], None,
                                    ALU.mult).then_inc(normed, 1)

            def head_sums(n, g, src, heads, col):
                group_is_out(dve, g)
                if n == 0:
                    dve.wait_ge(sumsq, 2 * NT)
                link(v.tensor_tensor(cube(squares, NT), src, src, ALU.mult))
                v.tensor_reduce(ss[:, col:col + NT * heads],
                                squares.rearrange("p (th d) -> p th d", th=NT * heads), AX.X,
                                ALU.add).then_inc(head_ss, 1)

            def head_norm(n, src, heads, col):
                dve.wait_ge(root, 3 + n)
                link(v.reciprocal(rstd[:, col:col + NT * heads], rstd[:, col:col + NT * heads]))
                flat = src.rearrange("p t n -> p (t n)").rearrange("p (th d) -> p th d", th=NT * heads)
                scale = rstd[:, col:col + NT * heads].unsqueeze(2).to_broadcast(flat.shape)
                v.tensor_tensor(flat, flat, scale, ALU.mult).then_inc(normed, 1)

            for n, (g, src, heads) in enumerate(((C_QB, nat[0], HEADS), (C_KB, nat[1], HEADS),
                                                 (C_QM, nat[0], MHEADS), (C_MK, nat[1], MHEADS))):
                head_sums(n, g, src, heads, SS_QK + 16 * n)
                head_norm(n, src, heads, SS_QK + 16 * n)
            head_sums(4, C_VS, v_sgu, 1, SS_V)
            dve.wait_ge(root, 7)
            link(v.reciprocal(rstd[:, SS_V:SS_V + NT], rstd[:, SS_V:SS_V + NT]))
            for t in range(NT):
                last = v.tensor_scalar(v_sgu[:, t, :], v_sgu[:, t, :], rstd[:, SS_V + t:SS_V + t + 1], None,
                                       ALU.mult)
            last.then_inc(normed, 1)

            def maxima(h):
                dve.wait_ge(s_done, h + 1)
                if h >= 2:
                    dve.wait_ge(pt_done, h - 1)
                m0, m1 = stat_m(h, 0), stat_m(h, 1)
                both = ss[:, SS_MAX + 2 * (h % 4):SS_MAX + 2 * (h % 4) + 2]
                if is_moba(h):
                    logits = prob[h % 2]
                    scaled = 2.0 ** (-8.0 * (h + 1) / HEADS)
                    link(v.scalar_tensor_tensor(logits[:, 0:3 * P], rel[:, :], scaled,
                                                ps_score[h % 2][:, 0:3 * P], ALU.mult, ALU.add))
                    v.tensor_reduce(m0, logits[:, 0:P], AX.X, ALU.max)
                    link(v.tensor_reduce(m1, logits[:, P:3 * P], AX.X, ALU.max))
                else:
                    link(v.tensor_reduce(both, cube(ps_score[h % 2], 2), AX.X, ALU.max))
                v.tensor_scalar(both, both, -1.0, None, ALU.mult).then_inc(max_done, 1)

            def reciprocals(h):
                dve.wait_ge(exp_done, h + 1)
                c = SS_SUM + 2 * (h % 4)
                v.reciprocal(rstd[:, c:c + 2], ss[:, c:c + 2]).then_inc(recip_done, 1)

            dve.wait_ge(masks_done, 4)
            for s in range(ALL_HEADS + 1):
                if s >= 1:
                    reciprocals(s - 1)
                if s < ALL_HEADS:
                    maxima(s)
                if s == 4:
                    dve.wait_ge(bcast_in, 4 * 16)
                    dve.wait_ge(group_done, SGU_GROUP + 1)
                    group_is_out(dve, C_U)
                    bank = pp[SGU_GROUP % 2]
                    for gg in range(GROUPS):
                        group = cube(bank[:, 256 * gg:256 * (gg + 1)], NT)
                        last = v.scalar_tensor_tensor(
                            group, group, cols[:, G_V + gg:G_V + gg + 1],
                            bs3[:, gg:gg + 1, :].to_broadcast([P, NT, P]), ALU.mult, ALU.add)
                    link(last)
                    v.tensor_tensor(ya[:, :], bank, ya[:, :], ALU.mult).then_inc(group_out[SGU_GROUP % 2], 1)

            for b in range(3):
                if b < 2:
                    dve.wait_ge(gate_sig, b + 1)
                else:
                    group_is_out(dve, C_GATE + 6)
                for half in range(2):
                    g = BR_GROUP + 2 * b + half
                    dve.wait_ge(group_done, g + 1)
                    gate = gates[:, b, 4 * half:4 * half + 4, :].rearrange("p j t -> p (j t)")
                    dst = mergedT_half(half) if b == 0 else product[half]
                    if b == 2:
                        dve.wait_ge(pool_added, half + 1)
                    v.tensor_tensor(dst, pp[g % 2], gate, ALU.mult).then_inc(group_out[g % 2], 1)
                    if b == 2:
                        group_is_out(dve, g)
                        v.tensor_tensor(mergedT_half(half), mergedT_half(half), dst, ALU.add).then_inc(merged, 1)

            for n in range(2):
                g = OUT_GROUP + n
                dve.wait_ge(group_done, g + 1)
                for t in range(NT):
                    last = v.tensor_tensor(x3[:, t, 512 * n:512 * (n + 1)], pp[g % 2][:, 512 * t:512 * (t + 1)],
                                           x3[:, t, 512 * n:512 * (n + 1)], ALU.add)
                last.then_inc(group_out[g % 2], 1)
            v.memset(ext[:, :, E:E + 4], SENTINEL)
            dve.wait_ge(x_ss, 2)
            v.tensor_reduce(ss[:, SS_X2SUM:SS_X2SUM + NT], cube(ss[:, SS_X2:SS_X2 + 4], NT), AX.X,
                            ALU.add).then_inc(x_sum, 1)
            dve.wait_ge(x_root, 1)
            link(v.reciprocal(rstd[:, SS_X2SUM:SS_X2SUM + NT], rstd[:, SS_X2SUM:SS_X2SUM + NT]))
            for n in range(2):
                for t in range(NT):
                    a = slice(512 * n, 512 * (n + 1))
                    v.scalar_tensor_tensor(h2[:, t, a], x3[:, t, a], rstd[:, SS_X2SUM + t:SS_X2SUM + t + 1],
                                           gffn_bc[:, a], ALU.mult, ALU.mult).then_inc(h2_done, 1)

            dve.wait_ge(logits_done, 1)
            link(v.tensor_tensor(ext[:, :, 0:E], cube(pp[0][:, 0:NT * E], NT),
                                 br_bc[:, :].unsqueeze(1).to_broadcast([P, NT, E]), ALU.add))
            top3, rep3 = cube(top8[:, :], NT), cube(rep8[:, :], NT)
            for t in range(NT):
                last = v.max(top3[:, t, :], ext[:, t, :])
            link(last)
            v.tensor_scalar(stat[:, 0:NT], top3[:, :, 0], -1.0, None, ALU.mult).then_inc(top_done, 1)
            link(v.tensor_copy(rep3[:, :, 0:TOP_K], top3[:, :, 0:TOP_K]))
            for t in range(NT):
                last = v.match_replace(ext2[:, t, :], rep3[:, t, :], ext[:, t, :], REPLACED)
            link(last)
            v.tensor_tensor(sel3, ext2[:, :, 0:E], ext[:, :, 0:E], ALU.not_equal).then_inc(sel_done, 1)
            dve.wait_ge(rank_done, 1)
            link(v.scalar_tensor_tensor(slot3, cube(pp[1][:, 0:NT * E], NT), 1.0, sel3, ALU.add, ALU.mult))

            def make_onehot(e):
                dve.wait_ge(st_done, e)
                for t in range(NT):
                    last = v.tensor_scalar(onehot[:, t, :], iota1[:, :], slot1[:, bass.ds(e + E * t, 1)], None,
                                           ALU.is_equal)
                last.then_inc(onehot_done, 1)

            for t in range(NT):
                last = v.tensor_scalar(onehot[:, t, :], iota1[:, :], slot3[:, t, 0:1], None, ALU.is_equal)
            last.then_inc(onehot_done, 1)

            v.tensor_copy(counts[:, :], pp[1][:, 2 * E:3 * E])
            dve.wait_ge(e_done, 1)
            link(v.tensor_tensor(e_exp, e_exp, sel3, ALU.mult))
            link(v.tensor_reduce(route[:, 0:NT], e_exp, AX.X, ALU.add))
            link(v.reciprocal(route[:, NT:2 * NT], route[:, 0:NT]))
            for t in range(NT):
                last = v.tensor_scalar(wgt3[:, t, :], e_exp[:, t, :], route[:, NT + t:NT + t + 1], None, ALU.mult)
            last.then_inc(wgt_done, 1)

            for b in range(BLOCKS - 1):
                last = v.tensor_scalar(flags[:, E * b:E * (b + 1)], counts[:, :],
                                       float(SLOTS * (b + 1)), None, ALU.is_gt)
            link(last)
            NF = (BLOCKS - 1) * E
            link(v.tensor_tensor_scan(incl, ones[:, 0:NF], flags, 0.0, ALU.mult, ALU.add))
            v.tensor_copy(n_items[:, :], incl[:, NF - 1:NF])
            v.memset(over[:, 0:1], 1.0)
            v.tensor_tensor(order, incl, flags, ALU.mult).then_inc(items_done, 1)

            def make_row(e):
                v.tensor_scalar(expert_row, part[0:E, :], turn[0:E, 0:1], None, ALU.is_equal).then_inc(row_done, 1)
                dve.wait_ge(row_done, e + 1)
                v.tensor_scalar(turn[:, :], turn[:, :], 1.0, None, ALU.add)

            def swiglu(e):
                dve.wait_ge(ring_free, e * PER_EXPERT + UP_CHUNKS)

                def step(ins, n):
                    ins.then_inc(e_chain, 1)
                    dve.wait_ge(e_chain, e * 2 + n)

                v.tensor_scalar(glu, ps_gate, LIMIT, None, ALU.min).then_inc(glu_done, 1)
                step(v.tensor_scalar(ps_up, ps_up, -LIMIT, LIMIT, ALU.max, ALU.min), 1)
                step(v.scalar_tensor_tensor(ps_up, ps_up, 1.0, glu, ALU.add, ALU.mult), 2)
                dve.wait_ge(sig_done, e + 1)
                v.tensor_tensor(act_h, ps_up, sig, ALU.mult).then_inc(h_done, 1)

            def sum_up(e, t):
                dve.wait_ge(scattered, e * NT + (NT + t + 1))
                v.scalar_tensor_tensor(x3[:, t, :], ps_add, wgt[:, bass.ds(e + E * t, 1)], x3[:, t, :],
                                       ALU.mult, ALU.add).then_inc(summed, 1)

            def sum_bias(t):
                dve.wait_ge(scattered, t + 1)
                v.tensor_tensor(x3[:, t, :], ps_add, x3[:, t, :], ALU.add).then_inc(summed, 1)

            dve.wait_ge(pool_const, 9)
            make_row(0)
            make_onehot(1)
            sum_bias(0)
            swiglu(0)
            make_row(1)
            sum_bias(1)
            with dve.Fori(1, E - 1) as e:
                make_onehot(e + 1)
                sum_up(e - 1, 0)
                swiglu(e)
                make_row(e + 1)
                sum_up(e - 1, 1)
            sum_up(E - 2, 0)
            swiglu(E - 1)
            sum_up(E - 2, 1)
            for t in range(NT):
                sum_up(E - 1, t)

            dve.sem_inc(o_sum, 1)
            OLINKS = 14
            n_over = dve.value_load(n_items[0:1, 0:1], min_val=0, max_val=ITEMS)
            with dve.Fori(0, ITEMS) as i:
                with dve.If(n_over > i):
                    count = [0]

                    def step(ins):
                        count[0] += 1
                        ins.then_inc(o_chain, 1)
                        dve.wait_ge(o_chain, i * OLINKS + count[0])

                    step(v.tensor_scalar(pick, order, over[:, 0:1], None, ALU.is_equal))
                    step(v.tensor_tensor(pick2, pick, item_e[:, :], ALU.mult))
                    step(v.tensor_reduce(over[:, 1:2], pick2, AX.X, ALU.add))
                    v.tensor_copy(over_e[:, :], over[:, 1:2]).then_inc(o_item, 1)
                    step(v.tensor_tensor(pick2, pick, item_b[:, :], ALU.mult))
                    step(v.tensor_reduce(over[:, 2:3], pick2, AX.X, ALU.add))
                    step(v.tensor_tensor(pick_e, pick[:, 0:E], pick[:, E:2 * E], ALU.add))
                    step(v.tensor_tensor(pick_e, pick_e, pick[:, 2 * E:3 * E], ALU.add))
                    for dst, src in ((3, slot3), (5, wgt3)):
                        step(v.tensor_tensor(cube(pick2[:, 0:NT * E], NT), src,
                                             pick_e.unsqueeze(1).to_broadcast([P, NT, E]), ALU.mult))
                        step(v.tensor_reduce(over[:, dst:dst + NT], cube(pick2[:, 0:NT * E], NT), AX.X, ALU.add))
                    step(v.tensor_scalar(over[:, 3:5], over[:, 3:5], over[:, 2:3], None, ALU.subtract))
                    dve.wait_ge(o_st, i + 1)
                    for t in range(NT):
                        last = v.tensor_scalar(onehot[:, t, :], iota1[:, :], over[:, 3 + t:4 + t], None,
                                               ALU.is_equal)
                    last.then_inc(o_onehot, 1)
                    dve.wait_ge(o_down, i + 1)
                    v.tensor_scalar(expert_row, part[0:E, :], over[0:E, 1:2], None, ALU.is_equal).then_inc(o_row, 1)
                    v.tensor_scalar(over[:, 0:1], over[:, 0:1], 1.0, None, ALU.add)

                    dve.wait_ge(o_up, i + 1)
                    v.tensor_scalar(glu, ps_gate, LIMIT, None, ALU.min).then_inc(o_glu, 1)
                    step(v.tensor_scalar(ps_up, ps_up, -LIMIT, LIMIT, ALU.max, ALU.min))
                    step(v.scalar_tensor_tensor(ps_up, ps_up, 1.0, glu, ALU.add, ALU.mult))
                    assert count[0] == OLINKS
                    dve.wait_ge(o_sig, i + 1)
                    v.tensor_tensor(act_h, ps_up, sig, ALU.mult).then_inc(o_h, 1)
                    for t in range(NT):
                        dve.wait_ge(o_scat, i * NT + (t + 1))
                        v.scalar_tensor_tensor(x3[:, t, :], ps_add, over[:, 5 + t:6 + t], x3[:, t, :],
                                               ALU.mult, ALU.add).then_inc(o_sum, 1)


_INS = ['x', 'mem', 'g_mix', 'w_in', 'g_sgu_v', 'w_spatial', 'b_spatial', 'g_q_moba', 'g_k_moba',
        'g_mem', 'w_mem_kv', 'g_q_mem', 'g_k_mem', 'w_br_sgu', 'w_br_moba', 'w_br_mem', 'w_out',
        'g_ffn', 'w_router', 'b_router', 'w_gate_up', 'b_gate_up', 'w_down', 'b_down']


def kernel(**inputs):
    import numpy as np
    import concourse.bacc as bacc
    from concourse.bass_utils import run_bass_kernel_spmd

    nc = bacc.Bacc("TRN2", target_bir_lowering=False, num_devices=1)
    arrays, args = {}, []
    for name in _INS:
        a = np.ascontiguousarray(inputs[name])
        arrays[f"in_{name}"] = a
        args.append(nc.dram_tensor(f"in_{name}", a.shape, mybir.dt.from_np(a.dtype), kind="ExternalInput").ap())
    shape = inputs["x"].shape
    args.append(nc.dram_tensor("out_0", shape, F32, kind="ExternalOutput").ap())
    build(nc, *args)
    r = run_bass_kernel_spmd(nc, [arrays], core_ids=[0])
    return r.results[0]["out_0"]
```

```python
from contextlib import ExitStack

import concourse.bass as bass
from concourse import mybir

F32 = mybir.dt.float32
F32R = mybir.dt.float32r
I32 = mybir.dt.int32
ALU = mybir.AluOpType
ACT = mybir.ActivationFunctionType
AX = mybir.AxisListType

P = 128
SLOTS = 64
FRONT_RING = 2
RING = 9
CHUNK = 4096
STAGES = 4
NEG = -1e30
SENTINEL = -3e38
REPLACED = 3e38


def build(nc, x, mem, g_mix, w_in, g_sgu_v, w_spatial, b_spatial, g_q_moba, g_k_moba, g_mem,
          w_mem_kv, g_q_mem, g_k_mem, w_br_sgu, w_br_moba, w_br_mem, w_out, g_ffn, w_router,
          b_router, w_gate_up, b_gate_up, w_down, b_down, out):
    SEQ, D = x.shape[1], x.shape[2]
    NT = SEQ // P
    KC = D // P
    E = w_router.shape[2]
    TOP_K = 4
    EPS = 1e-6
    GROUPS = w_spatial.shape[1]
    WIDTH = w_br_sgu.shape[1]
    WC = WIDTH // P
    DH = g_q_moba.shape[1]
    HEADS = WIDTH // DH
    MDH = g_q_mem.shape[1]
    MHEADS = WIDTH // MDH
    F = w_down.shape[2]
    FC = F // P
    LIMIT, ALPHA = 7.0, 1.702
    BLOCKS = SEQ // SLOTS
    ITEMS = (SEQ * TOP_K - 1) // SLOTS
    GATE0 = 2 * WIDTH + 4 * WIDTH
    assert (NT, KC, WC, FC, GROUPS) == (2, 8, 4, 8, 4) and KC * 512 == CHUNK

    def col_block(w, n):
        return w[0][:, n * 512:(n + 1) * 512].rearrange("(c p) n -> p c n", p=P)

    def all_cols(w):
        return w[0].rearrange("(c p) n -> p c n", p=P)

    front = ([(col_block(w_in, n), KC) for n in (2, 3, 4, 5)] +
             [(col_block(w_mem_kv, n), KC) for n in (0, 1)] +
             [(col_block(w_in, n), KC) for n in (1, 0)] +
             [(col_block(w_in, 6 + n), KC) for n in range(6)] +
             [(all_cols(w), WC) for w in (w_br_sgu, w_br_moba, w_br_mem)] +
             [(col_block(w_out, n), KC) for n in (0, 1)])
    (C_QB, C_KB, C_VB, C_QM, C_MK, C_MV, C_VS, C_U, C_GATE) = range(9)
    C_BR, C_OUT = C_GATE + 6, C_GATE + 9
    NFRONT = len(front)
    UP_CHUNKS, DOWN_CHUNKS = 4, 2
    PER_EXPERT = UP_CHUNKS + DOWN_CHUNKS
    TURN = 3
    assert TURN * PER_EXPERT % RING == 0 and (E - 2) % TURN == 0
    ORDER = [3, 0, 4, 5, 1, 2, 6, 7, 8]

    with ExitStack() as ctx:
        def sb(name, cols, dt=F32):
            return ctx.enter_context(nc.sbuf_tensor(name, [P, cols], dt))

        def sem(name):
            return ctx.enter_context(nc.semaphore(name))

        def cube(ap, n):
            return ap.rearrange("p (a b) -> p a b", a=n)

        ring_a = sb("ring_a", FRONT_RING * CHUNK)
        x_sb = sb("x_sb", NT * D)
        x3 = cube(x_sb[:, :], NT)
        bgu_all = sb("bgu", 2 * F)
        bdown_all = sb("bdown", D)
        bgu_sb, bdown_sb = bgu_all[0:E, :], bdown_all[0:E, :]
        probs = sb("probs", 2048)
        pool_b = sb("buffers", 2560)

        squares = probs[:, 0:1024]
        prob = [probs[:, 512 * n:512 * (n + 1)] for n in range(2)]
        probT = [probs[:, 1024 + 512 * n:1024 + 512 * (n + 1)] for n in range(2)]
        h2 = cube(probs[:, :], NT)
        ws_nat = cube(pool_b[:, 0:512], GROUPS)
        junk = probs[:, :]
        h2T = cube(pool_b[:, 0:2048], KC)
        EB = KC * SLOTS
        xg, glu, sig, act_h, hT_sb = (pool_b[:, n * EB:(n + 1) * EB] for n in range(5))
        xn = hT_sb
        y_sb = sb("y", 512)[:, :]
        onehot = cube(sb("onehot", NT * P)[:, :], NT)
        scat_sb = sb("scatter", TURN * SEQ)
        scatter = [scat_sb[:, SEQ * n:SEQ * (n + 1)] for n in range(TURN)]
        expert_row = sb("expert_row", SLOTS)[0:E, :]
        ext = cube(sb("ext", NT * (E + 4))[:, :], NT)
        ext2 = cube(sb("ext2", NT * (E + 4))[:, :], NT)
        e_exp = cube(sb("e_exp", NT * E)[:, :], NT)
        NF = (BLOCKS - 1) * E
        flags, incl, order, pick, pick2 = (sb(n, NF)[:, :] for n in ("flags", "incl", "order", "pick", "pick2"))
        pick_e = sb("pick_e", E)[:, :]
        wT_sb = scat_sb[0:E, SEQ * (TURN - 1):SEQ * TURN]

        ident = sb("ident", P)
        before = sb("before", P)
        ones = sb("ones", P)
        iota1 = sb("iota1", 2 * SLOTS)
        part = sb("part", SLOTS)
        turn = sb("turn", 1)
        rel = sb("rel", 3 * P)
        item_e = sb("item_e", (BLOCKS - 1) * E)
        item_b = sb("item_b", (BLOCKS - 1) * E)
        eps = sb("eps", 1)
        rows = sb("rows", P)
        NCOLS = 3 * KC + GROUPS + 4
        cols = sb("cols", NCOLS)
        G_MIX, G_MEM, G_FFN, B_SPATIAL, G_Q, G_K, G_QM, G_KM = 0, 8, 16, 24, 28, 29, 30, 31
        wsT = sb("wsT", GROUPS * P)
        gv_bc = sb("gv_bc", WIDTH)
        wr_sb = sb("wr_sb", KC * E)
        br_bc = sb("br_bc", E)
        gffn_bc = sb("gffn_bc", D)
        ss = sb("ss", 96)
        rstd = sb("rstd", 96)
        stat = sb("stat", 8)
        top8 = sb("top8", 16)
        rep8 = sb("rep8", 16)
        sel = sb("sel", NT * E)
        slot1 = sb("slot1", NT * E)
        wgt = sb("wgt", NT * E)
        route = sb("route", 16)
        counts = sb("counts", E)
        n_items = sb("n_items", 1, I32)
        over = sb("over", 16)
        over_e = sb("over_e", 1, I32)
        with ExitStack() as front_ctx:
            def fsb(name, cols, dt=F32):
                return front_ctx.enter_context(nc.sbuf_tensor(name, [P, cols], dt))

            attn_sb = fsb("attn_sb", CHUNK)
            y_r = fsb("y_r", 6 * 1024, F32R)
            gate_b = fsb("gate_b", 2048)
            gate_ca = fsb("gate_ca", CHUNK)
            model_r = fsb("model_r", CHUNK, F32R)
            stage_r = fsb("stage_r", STAGES * 2048, F32R)
        ring_b = sb("ring_b", (RING - FRONT_RING) * CHUNK)
        qT, kT = (cube(attn_sb[:, 1024 * n:1024 * (n + 1)], WC) for n in range(2))
        v_moba, v_mem = (cube(attn_sb[:, 1024 * n:1024 * (n + 1)], NT) for n in (2, 3))
        qmT, kmT = (cube(bgu_all[:, 1024 * n:1024 * (n + 1)], WC) for n in range(2))
        v_sgu, ya = cube(bdown_all[:, :], NT), cube(pool_b[:, 512:1536], NT)
        gates = [cube(g, NT) for g in (gate_ca[:, 2048:4096], gate_b[:, :], gate_ca[:, 0:2048])]
        mem_nat, merged_nat = gates[1], gates[0]
        nat = [cube(gate_ca[:, 1024 * n:1024 * (n + 1)], NT) for n in range(2)]
        hT = mergedT = tuple(cube(model_r[:, 2048 * n:2048 * (n + 1)], KC) for n in range(2))
        memT = tuple(cube(y_r[:, 2048 * n:2048 * (n + 1)], KC) for n in range(2))
        yT = [tuple(cube(y_r[:, 1024 * n:1024 * (n + 1)], WC) for n in (2 * b, 2 * b + 1)) for b in range(3)]
        stages = [tuple(cube(stage_r[:, 1024 * n:1024 * (n + 1)], 2) for n in (2 * i, 2 * i + 1))
                  for i in range(STAGES)]
        wsT3 = cube(wsT[:, :], GROUPS)
        wr3 = cube(wr_sb[:, :], KC)
        sel3, slot3, wgt3 = (cube(a[:, :], NT) for a in (sel, slot1, wgt))

        psum = ctx.enter_context(nc.psum_tensor("psum", [P, 8 * 512], F32))
        pp = [psum[:, 0:1024], psum[:, 1024:2048]]
        ps_score = [psum[:, 2048:2560], psum[:, 2560:3072]]
        ps_t = psum[:, 3072:3584]
        ps_o = psum[:, 3584:4096]
        tb_banks = [ps_score[0], ps_score[1], ps_t, ps_o]
        ps_gate, ps_up = psum[:, 0:512], psum[:, 512:1024]
        ps_add = psum[:, 1024:2048]
        last_sum = psum[:, 0:1024]
        ps_y = psum[:, 2048:2560]
        ps_hT = psum[:, 2560:3072]
        ps_x = psum[:, 3072:3584]
        ps_s = psum[:, 3584:4096]

        first_in = sem("first_in")
        x_in, mem_in = [sem(f"x_in{t}") for t in range(NT)], sem("mem_in")
        gains_in, bcast_in, gains_scaled = sem("gains_in"), sem("bcast_in"), sem("gains_scaled")
        ws_in, bgu_in, bdown_in = sem("ws_in"), sem("bgu_in"), sem("bdown_in")
        ring_full = [sem(f"ring_full{n}") for n in range(RING)]
        ring_free = sem("ring_free")
        pool_const, masks_done, dve_const = sem("pool_const"), sem("masks_done"), sem("dve_const")
        sumsq, root, normed, head_ss = sem("sumsq"), sem("root"), sem("normed"), sem("head_ss")
        tb_done, tb_out = sem("tb_done"), sem("tb_out")
        tb_low = sem("tb_low")
        hi_done, lo_done = sem("hi_done"), sem("lo_done")
        step_done, sgu_done = sem("step_done"), sem("sgu_done")
        group_out = [sem(f"group_out{n}") for n in range(2)]
        s_done, max_done, exp_done = sem("s_done"), sem("max_done"), sem("exp_done")
        recip_done, prob_done = sem("recip_done"), sem("prob_done")
        pt_done, pt_out, pv_done, o_out = sem("pt_done"), sem("pt_out"), sem("pv_done"), sem("o_out")
        o_low = sem("o_low")
        gate_sig, pool_added, merged = sem("gate_sig"), sem("pool_added"), sem("merged")
        x_ss, x_sum, x_root, h2_done = sem("x_ss"), sem("x_sum"), sem("x_root"), sem("h2_done")
        x_rstd, h2_scaled, h2_pool, logits_done = sem("x_rstd"), sem("h2_scaled"), sem("h2_pool"), sem("logits_done")
        top_done, e_done, sel_done, rank_done = sem("top_done"), sem("e_done"), sem("sel_done"), sem("rank_done")
        wgt_done, wT_done, wT_out, items_done = sem("wgt_done"), sem("wT_done"), sem("wT_out"), sem("items_done")
        onehot_done, gathered, xg_out = sem("onehot_done"), sem("gathered"), sem("xg_out")
        xn_out, xt_done, o_xn, o_xt = sem("xn_out"), sem("xt_done"), sem("o_xn"), sem("o_xt")
        st_done, st_out = sem("st_done"), sem("st_out")
        glu_done, sig_done, h_done = sem("glu_done"), sem("sig_done"), sem("h_done")
        hT_done, hT_out, row_done = sem("hT_done"), sem("hT_out"), sem("row_done")
        y_out, scattered, summed = sem("y_out"), sem("scattered"), sem("summed")
        v_chain, e_chain, o_chain = sem("v_chain"), sem("e_chain"), sem("o_chain")
        o_item, o_onehot, o_gath, o_xg = sem("o_item"), sem("o_onehot"), sem("o_gath"), sem("o_xg")
        o_st, o_stout, o_full, o_up = sem("o_st"), sem("o_stout"), sem("o_full"), sem("o_up")
        o_glu, o_sig, o_h, o_down = sem("o_glu"), sem("o_sig"), sem("o_h"), sem("o_down")
        o_y, o_scat, o_sum = sem("o_y"), sem("o_scat"), sem("o_sum")
        o_hT, o_hTout, o_row = sem("o_hT"), sem("o_hTout"), sem("o_row")
        item_seen, out_done = sem("item_seen"), sem("out_done")

        def buffer(b):
            if b < FRONT_RING:
                return ring_a[:, b * CHUNK:(b + 1) * CHUNK]
            return ring_b[:, (b - FRONT_RING) * CHUNK:(b - FRONT_RING + 1) * CHUNK]

        def front_buffer(n):
            return n % FRONT_RING if n < NFRONT - 1 else FRONT_RING

        EARLY = C_BR + 1

        def slot(n):
            return buffer(front_buffer(n))

        def fills(n):
            return 16 * len([m for m in range(n + 1) if front_buffer(m) == front_buffer(n)])

        def expert_buffer(r, k):
            return ORDER[(PER_EXPERT * r + k) % RING]

        def expert_fills(turn, r, k):
            b = expert_buffer(r, k)
            before = len([n for n in range(NFRONT) if front_buffer(n) == b])
            m = PER_EXPERT * r + k
            return turn * (16 * TURN * PER_EXPERT // RING) + 16 * (before + m // RING + 1)

        def up_src(e, k):
            return w_gate_up[0, e][k * 2 * P:(k + 1) * 2 * P, :].rearrange("(c p) n -> p c n", p=P)

        def down_src(e, k):
            return w_down[0, e][k * 4 * P:(k + 1) * 4 * P, :].rearrange("(c p) n -> p c n", p=P)

        ALL_HEADS = HEADS + MHEADS
        HEAD_STEPS = 6 * 4

        def head_at(s):
            return [h for h in range(ALL_HEADS) if h * 3 // 2 == s]

        TO_PROBS, TO_OUTPUT = 3, 4
        YA_STEP = (ALL_HEADS - 1) * 3 // 2 + TO_OUTPUT + 1

        def is_moba(h):
            return h < HEADS

        def score_segments(h):
            return [(0, P, 0), (P, 3 * P, 1)] if is_moba(h) else [(0, 256, 0), (256, 512, 1)]

        def head_dst(h):
            return [part[:, h // 2 if is_moba(h) else h - HEADS, :] for part in yT[1 if is_moba(h) else 2]]

        def o_unit(h):
            return h // 2 if is_moba(h) else HEADS // 2 + (h - HEADS)

        SGU_GROUP = C_GATE + 1
        BR_GROUP, OUT_GROUP = C_BR + 1, C_BR + 1 + 2 * 3

        STEPS = 4 * NFRONT
        S_GATE, S_BR, S_OUT = 4 * C_GATE, 4 * C_BR, 4 * C_OUT

        OUT_ORDER = [(0, 0), (0, 1), (1, 0), (1, 1), (0, 2), (0, 3), (1, 2), (1, 3)]

        def chunk_part(i):
            if i < S_OUT:
                return divmod(i, 4)
            n, j = OUT_ORDER[i - S_OUT]
            return C_OUT + n, j

        def steps_through_chunk(n):
            return max(i for i in range(STEPS) if chunk_part(i)[0] == n) + 1

        def step_weights(i):
            n, j = chunk_part(i)
            w = cube(slot(n), front[n][1])
            if C_BR <= n < C_OUT:
                return w[:, 2 * (j % 2):2 * (j % 2) + 2, 512 * (j // 2):512 * (j // 2 + 1)]
            return w[:, 2 * j:2 * j + 2, :]

        def steps_through(g):
            if g < BR_GROUP:
                return 4 * (g + 1) if g < SGU_GROUP else 4 * g
            return S_BR + 2 * (g - BR_GROUP + 1) if g < OUT_GROUP else steps_through_chunk(C_OUT + g - OUT_GROUP)

        def lows_through(b):
            return sum(1 for n in range(b + 1) if TB_X <= n < TB_MEM + 4 or TB_YA <= n < TB_MERGED + 4)

        TB_X, TB_MEM, TB_YA, TB_MERGED = 1, 5, 18, 20

        SS_X, SS_MEM, SS_V, SS_X2, SS_X2SUM, SS_QK, SS_SUM, SS_MAX = 0, 2, 4, 6, 10, 16, 80, 88

        def stat_r(h, t):
            return rstd[:, SS_SUM + 2 * (h % 4) + t:SS_SUM + 2 * (h % 4) + t + 1]

        def stat_s(h, t):
            return ss[:, SS_SUM + 2 * (h % 4) + t:SS_SUM + 2 * (h % 4) + t + 1]

        def stat_m(h, t):
            return ss[:, SS_MAX + 2 * (h % 4) + t:SS_MAX + 2 * (h % 4) + t + 1]

        def group_is_out(eng, g):
            eng.wait_ge(group_out[g % 2], g // 2 + 1)

        block = ctx.enter_context(nc.Block())

        @block.sync
        def _(sp):
            x_tiles = x[0].rearrange("(t p) d -> p t d", p=P)
            for t in range(NT):
                sp.dma_start(x3[:, t, :], x_tiles[:, t, :]).then_inc(x_in[t], 16)
            for dst, src in ((rows[G_MIX:G_MIX + KC, :], g_mix[0].rearrange("(c p) -> c p", p=P)),
                             (rows[G_MEM:G_MEM + KC, :], g_mem[0].rearrange("(c p) -> c p", p=P)),
                             (rows[G_FFN:G_FFN + KC, :], g_ffn[0].rearrange("(c p) -> c p", p=P)),
                             (rows[B_SPATIAL:B_SPATIAL + GROUPS, :], b_spatial[0]),
                             (rows[G_Q:G_Q + 1, :].rearrange("a (r d) -> a r d", r=2),
                              g_q_moba.unsqueeze(1).to_broadcast([1, 2, DH])),
                             (rows[G_K:G_K + 1, :].rearrange("a (r d) -> a r d", r=2),
                              g_k_moba.unsqueeze(1).to_broadcast([1, 2, DH])),
                             (rows[G_QM:G_QM + 1, :], g_q_mem), (rows[G_KM:G_KM + 1, :], g_k_mem)):
                sp.dma_start(dst, src).then_inc(gains_in, 16)
            for n in (*range(EARLY), NFRONT - 1, *range(EARLY, NFRONT - 1)):
                src, c = front[n]
                if n == NFRONT - 1:
                    sp.wait_ge(pv_done, ALL_HEADS)
                elif n >= FRONT_RING:
                    sp.wait_ge(lo_done, 4 * (n - FRONT_RING + 1))
                if n == 0:
                    sp.dma_start(cube(slot(n), c)[:, 0:2, :], src[:, 0:2, :]).then_inc(first_in, 16)
                    sp.dma_start(cube(slot(n), c)[:, 2:c, :], src[:, 2:c, :]).then_inc(ring_full[0], 16)
                else:
                    sp.dma_start(cube(slot(n), c), src).then_inc(ring_full[front_buffer(n)], 16)
                if n == 0:
                    sp.dma_start(mem_nat, mem[0].rearrange("(t p) d -> p t d", p=P)).then_inc(mem_in, 16)
                if n == 1:
                    sp.dma_start(ws_nat, w_spatial[0].rearrange("g t s -> t g s")).then_inc(ws_in, 16)
                    for dst, src in ((gv_bc[:, :], g_sgu_v.to_broadcast([P, WIDTH])),
                                     (wr3, w_router[0].rearrange("(c p) e -> p c e", p=P)),
                                     (br_bc[:, :], b_router.to_broadcast([P, E])),
                                     (gffn_bc[:, :], g_ffn.to_broadcast([P, D]))):
                        sp.dma_start(dst, src).then_inc(bcast_in, 16)
                if n == NFRONT - 1:
                    sp.wait_ge(sgu_done, 1)
                    sp.dma_start(bdown_sb, b_down[0]).then_inc(bdown_in, 16)
                    sp.dma_start(bgu_sb, b_gate_up[0]).then_inc(bgu_in, 16)

            def expert_chunk(e, r, k):
                b = expert_buffer(r, k)
                src, c = (up_src(e, k), 2) if k < UP_CHUNKS else (down_src(e, k - UP_CHUNKS), 4)
                sp.dma_start(cube(buffer(b), c), src).then_inc(ring_full[b], 16)

            def buffer_left(b):
                if b <= FRONT_RING:
                    sp.wait_ge(lo_done, steps_through_chunk(max(n for n in range(NFRONT) if front_buffer(n) == b)))
                elif b == 3:
                    sp.wait_ge(step_done, steps_through(BR_GROUP + 3))
                elif b == 4:
                    sp.wait_ge(step_done, steps_through(BR_GROUP + 5))
                    sp.wait_ge(pool_added, 2)
                elif b == 5:
                    sp.wait_ge(tb_done, TB_MERGED + 4)
                else:
                    sp.wait_ge(step_done, STEPS)

            for m in range(2 * PER_EXPERT):
                e, k = divmod(m, PER_EXPERT)
                if m < RING:
                    buffer_left(ORDER[m])
                else:
                    sp.wait_ge(ring_free, m - RING + 1)
                expert_chunk(e, e, k)
            with sp.Fori(0, (E - 2) // TURN) as turn:
                for r in range(TURN):
                    e = turn * TURN + (r + 2)
                    for k in range(PER_EXPERT):
                        sp.wait_ge(ring_free, turn * (TURN * PER_EXPERT) + ((r + 2) * PER_EXPERT + k - RING + 1))
                        expert_chunk(e, (r + 2) % TURN, k)

            sp.wait_ge(items_done, 1)
            n_over = sp.value_load(n_items[0:1, 0:1], min_val=0, max_val=ITEMS)
            with sp.If(n_over > 0):
                with sp.Fori(0, ITEMS) as i:
                    with sp.If(n_over > i):
                        sp.wait_ge(o_item, i + 1)
                        sp.wait_ge(o_down, i + 1)
                        sp.wait_ge(ring_free, E * PER_EXPERT)
                        sp.sem_inc(item_seen, 1)
                        oe = sp.value_load(over_e[0:1, 0:1], min_val=0, max_val=E - 1)
                        for k in range(UP_CHUNKS):
                            sp.dma_start(cube(buffer(ORDER[k]), 2), up_src(oe, k)).then_inc(o_full, 16)
                        for k in range(DOWN_CHUNKS):
                            sp.dma_start(cube(buffer(ORDER[UP_CHUNKS + k]), 4), down_src(oe, k)).then_inc(o_full, 16)

            sp.wait_ge(o_sum, n_over * NT + 1)
            for t in range(NT):
                sp.wait_ge(summed, NT * E + t + 1)
                sp.dma_start(out[0][t * P:(t + 1) * P, :], x3[:, t, :]).then_inc(out_done, 16)
            sp.wait_ge(out_done, 16 * NT)

        @block.gpsimd
        def _(pool):
            nc.gpsimd.memset(ident[:, :], 0.0).then_inc(pool_const, 1)
            nc.gpsimd.memset(before[:, :], 1.0).then_inc(pool_const, 1)
            nc.gpsimd.memset(ones[:, :], 1.0).then_inc(pool_const, 1)
            pool.wait_ge(pool_const, 3)
            nc.gpsimd.affine_select(out=ident[:, :], in_=ident[:, :], compare_op=ALU.not_equal, fill=1.0,
                                    base=0, pattern=[[-1, P]], channel_multiplier=1).then_inc(masks_done, 1)

            nc.gpsimd.affine_select(out=before[:, :], in_=before[:, :], compare_op=ALU.is_gt, fill=0.0,
                                    base=0, pattern=[[1, P]], channel_multiplier=-1).then_inc(masks_done, 1)
            nc.gpsimd.iota(rel[:, 0:P], pattern=[[1, P]], base=0, channel_multiplier=-1,
                           allow_small_or_imprecise_dtypes=True).then_inc(pool_const, 1)
            nc.gpsimd.iota(rel[:, P:3 * P], pattern=[[1, 2 * P]], base=-P, channel_multiplier=-1,
                           allow_small_or_imprecise_dtypes=True).then_inc(pool_const, 1)
            nc.gpsimd.iota(iota1[:, :], pattern=[[0, 2], [1, SLOTS]], base=1, channel_multiplier=0,
                           allow_small_or_imprecise_dtypes=True).then_inc(pool_const, 1)
            nc.gpsimd.iota(part[:, :], pattern=[[0, SLOTS]], base=0, channel_multiplier=1,
                           allow_small_or_imprecise_dtypes=True).then_inc(pool_const, 1)
            nc.gpsimd.iota(item_e[:, :], pattern=[[0, BLOCKS - 1], [1, E]], base=0, channel_multiplier=0,
                           allow_small_or_imprecise_dtypes=True).then_inc(pool_const, 1)
            nc.gpsimd.iota(item_b[:, :], pattern=[[SLOTS, BLOCKS - 1], [0, E]], base=SLOTS,
                           channel_multiplier=0, allow_small_or_imprecise_dtypes=True).then_inc(pool_const, 1)
            pool.wait_ge(pool_const, 9)
            nc.gpsimd.affine_select(out=rel[:, 0:P], in_=rel[:, 0:P], compare_op=ALU.is_ge, fill=NEG,
                                    base=0, pattern=[[-1, P]], channel_multiplier=1).then_inc(masks_done, 1)
            nc.gpsimd.affine_select(out=rel[:, P:3 * P], in_=rel[:, P:3 * P], compare_op=ALU.is_ge, fill=NEG,
                                    base=P, pattern=[[-1, 2 * P]], channel_multiplier=1).then_inc(masks_done, 1)
            pool.wait_ge(ws_in, 16)
            nc.gpsimd.affine_select(out=ws_nat, in_=ws_nat, compare_op=ALU.is_ge, fill=0.0, base=0,
                                    pattern=[[0, GROUPS], [-1, P]], channel_multiplier=1).then_inc(masks_done, 1)

            for h in range(ALL_HEADS):
                pool.wait_ge(recip_done, h + 1)
                for a, b, t in score_segments(h):
                    last = nc.gpsimd.tensor_scalar(prob[h % 2][:, a:b], prob[h % 2][:, a:b],
                                                   stat_r(h, t), None, ALU.mult)
                last.then_inc(prob_done, 1)
            for half in range(2):
                group_is_out(pool, BR_GROUP + 2 + half)
                a = slice(512 * half, 512 * (half + 1))
                nc.gpsimd.tensor_tensor(merged_nat[:, :, a], merged_nat[:, :, a], gates[1][:, :, a],
                                        ALU.add).then_inc(pool_added, 1)
            pool.wait_ge(x_rstd, 1)
            pool.wait_ge(bcast_in, 4 * 16)
            for t in range(NT):
                nc.gpsimd.tensor_scalar(h2[:, t, 512:D], x3[:, t, 512:D],
                                        rstd[:, SS_X2SUM + t:SS_X2SUM + t + 1], None, ALU.mult).then_inc(h2_scaled, 1)
                pool.wait_ge(h2_scaled, t + 1)
                nc.gpsimd.tensor_tensor(h2[:, t, 512:D], h2[:, t, 512:D], gffn_bc[:, 512:D],
                                        ALU.mult).then_inc(h2_pool, 1)

        @block.scalar
        def _(act):
            def copy(dst, src, **kw):
                return nc.scalar.activation(dst, src, ACT.Copy, **kw)

            def take_root(cols_, n, count):
                return nc.scalar.activation(rstd[:, cols_:cols_ + n], ss[:, cols_:cols_ + n], ACT.Sqrt,
                                            bias=eps[:, 0:1], scale=1.0 / count).then_inc(root, 1)

            act.wait_ge(dve_const, 1)
            nc.scalar.activation(stat[:, 4:5], eps[:, :], ACT.Sqrt)
            for t in range(NT):
                act.wait_ge(x_in[t], 16)
                nc.scalar.activation(squares, x3[:, t, :], ACT.Square,
                                     accum_out=ss[:, SS_X + t:SS_X + t + 1]).then_inc(sumsq, 1)
                act.wait_ge(sumsq, t + 1)
            take_root(SS_X, NT, D)

            batch = [0]

            def batch_out(*copies):
                b = batch[0]
                act.wait_ge(tb_done, b + 1)
                for dst, col, width, scale in copies:
                    last = copy(dst, tb_banks[b % 4][:, col:col + width],
                                **({} if scale is None else {"scale": scale}))
                last.then_inc(tb_out, 1)
                batch[0] += 1

            def model_chunks(dstT, gain, ms=range(KC // 2)):
                for m in ms:
                    batch_out(*((dstT[0][:, 2 * m + c, :], 256 * c, 256,
                                 None if gain is None else cols[:, gain + 2 * m + c:gain + 2 * m + c + 1])
                                for c in range(2)))

            def heads_out(dstT, gain):
                for t in range(NT):
                    batch_out((dstT[:, :, t * P:(t + 1) * P], 0, 512,
                               None if gain is None else cols[:, gain:gain + 1]))

            split = [0]

            def high_parts(upto):
                for i in range(split[0], min(upto, STEPS)):
                    n, j = chunk_part(i)
                    if i == 0:
                        act.wait_ge(first_in, 16)
                    elif j == (1 if n == 0 else 0):
                        act.wait_ge(ring_full[front_buffer(n)], fills(n))
                    if i >= STAGES:
                        act.wait_ge(step_done, i - STAGES + 1)
                    copy(stages[i % STAGES][0], step_weights(i)).then_inc(hi_done, 1)
                    split[0] = i + 1

            def group_copy(g, dst, func=ACT.Copy, norm=SS_X):
                high_parts(steps_through(g) + STAGES)
                act.wait_ge(step_done, steps_through(g))
                for t in range(NT):
                    last = nc.scalar.activation(dst[t], pp[g % 2][:, 512 * t:512 * (t + 1)], func,
                                                scale=rstd[:, norm + t:norm + t + 1])
                last.then_inc(group_out[g % 2], 1)

            def halves(ap):
                return [ap[:, n, :] for n in range(2)]

            batch_out((cols[:, :], 0, NCOLS, None))
            act.wait_ge(tb_out, 1)
            for c, n in ((G_Q, DH), (G_QM, MDH)):
                copy(cols[:, c:c + 1], cols[:, c:c + 1], scale=float(n) ** -0.5).then_inc(gains_scaled, 1)
            model_chunks(hT, G_MIX, (0, 1, 2))
            high_parts(1)
            model_chunks(hT, G_MIX, (3,))
            high_parts(STAGES)
            act.wait_ge(mem_in, 16)
            for t in range(NT):
                nc.scalar.activation(squares, mem_nat[:, t, :], ACT.Square,
                                     accum_out=ss[:, SS_MEM + t:SS_MEM + t + 1]).then_inc(sumsq, 1)
                act.wait_ge(sumsq, NT + t + 1)
                high_parts(STAGES + t + 1)
            take_root(SS_MEM, NT, D)
            act.wait_ge(normed, 2)
            group_copy(C_QB, halves(nat[0]))
            model_chunks(memT, G_MEM)
            act.wait_ge(head_ss, 1)
            take_root(SS_QK, NT * HEADS, DH)
            group_copy(C_KB, halves(nat[1]))
            batch_out((wsT[:, :], 0, 512, None))
            act.wait_ge(gains_scaled, 2)
            heads_out(qT, G_Q)
            act.wait_ge(head_ss, 2)
            take_root(SS_QK + 16, NT * HEADS, DH)
            group_copy(C_VB, halves(v_moba))
            heads_out(kT, G_K)
            group_copy(C_QM, halves(nat[0]))
            high_parts(4 * C_MK + 4)
            act.wait_ge(head_ss, 3)
            take_root(SS_QK + 32, NT * MHEADS, MDH)
            group_copy(C_MK, halves(nat[1]), norm=SS_MEM)
            heads_out(qmT, G_QM)
            act.wait_ge(head_ss, 4)
            take_root(SS_QK + 48, NT * MHEADS, MDH)
            group_copy(C_MV, halves(v_mem), norm=SS_MEM)
            heads_out(kmT, G_KM)
            group_copy(C_VS, halves(v_sgu), ACT.Gelu)
            high_parts(steps_through(C_VS) + 2 + STAGES)
            act.wait_ge(head_ss, 5)
            take_root(SS_V, NT, WIDTH)
            group_copy(C_U, halves(ya), ACT.Gelu)

            def exps(h):
                act.wait_ge(max_done, h + 1)
                for a, b, t in score_segments(h):
                    src = prob[h % 2][:, a:b] if is_moba(h) else ps_score[h % 2][:, a:b]
                    last = nc.scalar.activation(prob[h % 2][:, a:b], src, ACT.Exp, bias=stat_m(h, t),
                                                accum_out=stat_s(h, t))
                last.then_inc(exp_done, 1)

            def prob_out(h):
                act.wait_ge(pt_done, h + 1)
                if h >= 2:
                    act.wait_ge(pv_done, h - 1)
                width = 3 * P if is_moba(h) else 4 * P
                copy(probT[h % 2][:, 0:width], ps_t[:, 0:width]).then_inc(pt_out, 1)

            def head_out(h):
                act.wait_ge(pv_done, h + 1)
                u = o_unit(h)
                copy(head_dst(h)[0], ps_o[:, 256 * (u % 2):256 * (u % 2 + 1)]).then_inc(o_out, 1)

            def gate_out(m):
                g = C_GATE if m == 0 else C_GATE + 1 + m
                group_copy(g, [gates[m // 2][:, t, 512 * (m % 2):512 * (m % 2 + 1)] for t in range(NT)],
                           ACT.Sigmoid if m >= 4 else ACT.Copy)

            for s in range(HEAD_STEPS):
                for h in head_at(s - TO_PROBS):
                    prob_out(h)
                for h in head_at(s):
                    exps(h)
                for h in head_at(s - TO_OUTPUT):
                    if not is_moba(h) or h % 2 == 1:
                        head_out(h)
                high_parts(S_GATE + s + 1 + STAGES)
                if s % 4 == 3:
                    gate_out(s // 4)
                if s == YA_STEP:
                    heads_out(yT[0][0], None)
                if s == YA_STEP:
                    for b in range(2):
                        group_is_out(act, C_GATE + 2 + 2 * b)
                        both = gates[b].rearrange("p t n -> p (t n)")
                        nc.scalar.activation(both, both, ACT.Sigmoid).then_inc(gate_sig, 1)
            high_parts(S_OUT - 2 + STAGES)
            model_chunks(mergedT, None, (0, 1))
            high_parts(S_OUT + 2 + STAGES)
            model_chunks(mergedT, None, (2, 3))
            high_parts(STEPS)
            nc.scalar.activation(stat[:, 5:6], eps[:, :], ACT.Sqrt)

            for n in range(2):
                if n == 1:
                    model_chunks((h2T,), G_FFN, (2, 3))
                group_is_out(act, OUT_GROUP + n)
                for t in range(NT):
                    last = nc.scalar.activation(junk[:, 1024 * n + 512 * t:1024 * n + 512 * (t + 1)],
                                                x3[:, t, 512 * n:512 * (n + 1)], ACT.Square,
                                                accum_out=ss[:, SS_X2 + 2 * t + n:SS_X2 + 2 * t + n + 1])
                last.then_inc(x_ss, 1)
                if n == 0:
                    model_chunks((h2T,), G_FFN, (0, 1))
            act.wait_ge(x_sum, 1)
            nc.scalar.activation(rstd[:, SS_X2SUM:SS_X2SUM + NT], ss[:, SS_X2SUM:SS_X2SUM + NT], ACT.Sqrt,
                                 bias=eps[:, 0:1], scale=1.0 / D).then_inc(x_root, 1)
            act.wait_ge(top_done, 1)
            for t in range(NT):
                last = nc.scalar.activation(e_exp[:, t, :], ext[:, t, 0:E], ACT.Exp, bias=stat[:, t:t + 1])
            last.then_inc(e_done, 1)

            def tokens_out(e, r):
                act.wait_ge(gathered, e + 1)
                copy(xn, ps_x).then_inc(xn_out, 1)
                act.wait_ge(st_done, e + 1)
                copy(scatter[r], ps_s[:, 0:NT * P]).then_inc(st_out, 1)
                act.wait_ge(xt_done, e + 1)
                copy(xg, ps_x).then_inc(xg_out, 1)

            def y_copy(e):
                act.wait_ge(ring_free, e * PER_EXPERT + PER_EXPERT)
                copy(y_sb, ps_y).then_inc(y_out, 1)

            def sigmoid(e):
                act.wait_ge(glu_done, e + 1)
                nc.scalar.activation(sig, glu, ACT.Sigmoid, scale=ALPHA).then_inc(sig_done, 1)

            def hidden_out(e):
                act.wait_ge(hT_done, e + 1)
                copy(hT_sb, ps_hT).then_inc(hT_out, 1)

            tokens_out(0, 0)
            act.wait_ge(wT_done, 1)
            copy(wT_sb, ps_y[0:E, 0:SEQ]).then_inc(wT_out, 1)
            sigmoid(0)
            tokens_out(1, 1)
            hidden_out(0)
            with act.Fori(0, (E - 2) // TURN) as turn:
                for r in range(TURN):
                    e = turn * TURN + (r + 1)
                    y_copy(e - 1)
                    sigmoid(e)
                    tokens_out(e + 1, (r + 2) % TURN)
                    hidden_out(e)
            y_copy(E - 2)
            sigmoid(E - 1)
            hidden_out(E - 1)
            y_copy(E - 1)

            act.wait_ge(items_done, 1)
            n_over = act.value_load(n_items[0:1, 0:1], min_val=0, max_val=ITEMS)
            with act.If(n_over > 0):
                with act.Fori(0, ITEMS) as i:
                    with act.If(n_over > i):
                        act.wait_ge(o_gath, i + 1)
                        copy(xn, ps_x).then_inc(o_xn, 1)
                        act.wait_ge(o_xt, i + 1)
                        copy(xg, ps_x).then_inc(o_xg, 1)
                        act.wait_ge(o_st, i + 2)
                        copy(scatter[0], ps_s[:, 0:NT * P]).then_inc(o_stout, 1)
                        act.wait_ge(o_glu, i + 1)
                        nc.scalar.activation(sig, glu, ACT.Sigmoid, scale=ALPHA).then_inc(o_sig, 1)
                        act.wait_ge(o_hT, i + 1)
                        copy(hT_sb, ps_hT).then_inc(o_hTout, 1)
                        act.wait_ge(o_down, i + 2)
                        copy(y_sb, ps_y).then_inc(o_y, 1)

        @block.tensor
        def _(pe):
            mm = nc.tensor.matmul
            batch = [0]

            def transposes(*parts):
                b = batch[0]
                if b >= 4:
                    pe.wait_ge(tb_out, b - 3)
                    if lows_through(b - 4):
                        pe.wait_ge(tb_low, lows_through(b - 4))
                for src, col in parts:
                    k = src.shape[0]
                    last = nc.tensor.transpose(tb_banks[b % 4][:, col:col + k], src, ident[0:k, 0:k])
                last.then_inc(tb_done, 1)
                batch[0] += 1

            def model_batches(src, ms=range(KC // 2)):
                for m in ms:
                    transposes(*((src[:, t, (2 * m + c) * P:(2 * m + c + 1) * P], 256 * c + P * t)
                                 for c in range(2) for t in range(NT)))

            def head_batches(src):
                for t in range(NT):
                    transposes(*((src[:, t, c * P:(c + 1) * P], P * c) for c in range(WC)))

            def start_group(g):
                if g >= 2:
                    group_is_out(pe, g - 2)

            def step(i, bank, lhsT, c0, first, last_):
                pe.wait_ge(lo_done, i + 1)
                for c in range(2):
                    for t in range(NT):
                        for a, b in ((0, 0), (0, 1), (1, 0)):
                            last = mm(bank[:, 512 * t:512 * (t + 1)], lhsT[a][:, c0 + c, t * P:(t + 1) * P],
                                      stages[i % STAGES][b][:, c, :],
                                      start=(first and c == 0 and (a, b) == (0, 0)),
                                      stop=(last_ and c == 1 and (a, b) == (1, 0)))
                last.then_inc(step_done, 1)

            def natural(n, g, lhsT, parts=False):
                start_group(g)
                for j in range(4):
                    if parts:
                        pe.wait_ge(tb_low, j + 1)
                    step(4 * n + j, pp[g % 2], lhsT, 2 * j, j == 0, j == 3)

            pe.wait_ge(masks_done, 1)
            pe.wait_ge(gains_in, 8 * 16)
            transposes((rows[0:NCOLS, :], 0))
            for t in range(NT):
                pe.wait_ge(x_in[t], 16)
            model_batches(x3)
            natural(C_QB, C_QB, hT, parts=True)
            pe.wait_ge(mem_in, 16)
            model_batches(mem_nat)
            natural(C_KB, C_KB, hT)
            pe.wait_ge(masks_done, 5)
            transposes(*((ws_nat[:, g, :], P * g) for g in range(GROUPS)))
            pe.wait_ge(normed, 2 + 1)
            head_batches(nat[0])
            natural(C_VB, C_VB, hT)
            pe.wait_ge(normed, 2 + 2)
            head_batches(nat[1])
            natural(C_QM, C_QM, hT)
            pe.wait_ge(tb_low, 8)
            natural(C_MK, C_MK, memT)
            pe.wait_ge(normed, 2 + 3)
            head_batches(nat[0])
            natural(C_MV, C_MV, memT)
            pe.wait_ge(normed, 2 + 4)
            head_batches(nat[1])
            natural(C_VS, C_VS, hT)
            natural(C_U, C_U, hT)

            pe.wait_ge(tb_out, batch[0])

            def scores(h):
                if is_moba(h):
                    if h % 2 == 1:
                        return
                    if h >= 2:
                        pe.wait_ge(exp_done, h)
                    for t in range(NT):
                        for n in range(2):
                            rows_, pair = slice(DH * n, DH * (n + 1)), h // 2
                            cols_, keys = (slice(0, P), slice(0, P)) if t == 0 else (slice(P, 3 * P), slice(0, 2 * P))
                            last = mm(ps_score[n][:, cols_], qT[rows_, pair, t * P:(t + 1) * P],
                                      kT[rows_, pair, keys], start=True, stop=True)
                            if t == 1:
                                last.then_inc(s_done, 1)
                    return
                pe.wait_ge(exp_done, h - 1)
                for t in range(NT):
                    last = mm(ps_score[h % 2][:, 256 * t:256 * (t + 1)], qmT[:, h - HEADS, t * P:(t + 1) * P],
                              kmT[:, h - HEADS, :], start=True, stop=True)
                last.then_inc(s_done, 1)

            def prob_transposes(h):
                pe.wait_ge(prob_done, h + 1)
                if h >= 1:
                    pe.wait_ge(pt_out, h)
                moves = [(0, 0), (1, 1), (2, 2)] if is_moba(h) else [(0, 0), (1, 2), (2, 1), (3, 3)]
                for a, b in moves:
                    last = nc.tensor.transpose(ps_t[:, b * P:(b + 1) * P], prob[h % 2][:, a * P:(a + 1) * P],
                                               ident[:, :])
                last.then_inc(pt_done, 1)

            def values(h):
                if is_moba(h) and h % 2 == 0:
                    return
                pe.wait_ge(pt_out, h + 1)
                u = o_unit(h)
                if u >= 1:
                    pe.wait_ge(o_low, u)
                c0 = 256 * (u % 2)
                if is_moba(h):
                    for t, (a, b) in enumerate(((0, 256), (P, 256))):
                        for n in range(2):
                            r0, hd = DH * n, h - 1 + n
                            last = mm(ps_o[r0:r0 + DH, c0 + a:c0 + b], v_moba[:, t, hd * DH:(hd + 1) * DH],
                                      probT[n][:, 256 * t:256 * t + b - a], start=(t == 0), stop=(t == 1),
                                      skip_group_check=True)
                            if t == 1:
                                last.then_inc(pv_done, 1)
                else:
                    for t in range(2):
                        last = mm(ps_o[:, c0:c0 + 256], v_mem[:, t, (h - HEADS) * MDH:(h - HEADS + 1) * MDH],
                                  probT[h % 2][:, 256 * t:256 * (t + 1)], start=(t == 0), stop=(t == 1))
                    last.then_inc(pv_done, 1)

            for s in range(HEAD_STEPS):
                for h in head_at(s - TO_OUTPUT):
                    values(h)
                for h in head_at(s - TO_PROBS):
                    prob_transposes(h)
                for h in head_at(s):
                    scores(h)
                m, j = divmod(s, 4)
                g = C_GATE if m == 0 else C_GATE + 1 + m
                if j == 0:
                    start_group(g)
                step(S_GATE + s, pp[g % 2], hT, 2 * j, j == 0, j == 3)
                if s == 3:
                    start_group(SGU_GROUP)
                    pe.wait_ge(normed, 2 + 5)
                    for gg in range(GROUPS):
                        for t in range(NT):
                            a = 512 * t + P * gg
                            last = mm(pp[SGU_GROUP % 2][:, a:a + P], wsT3[:, gg, :],
                                      v_sgu[:, t, gg * P:(gg + 1) * P], start=True, stop=True)
                    last.then_inc(sgu_done, 1)
                if s == YA_STEP:
                    assert batch[0] == TB_YA
                    pe.wait_ge(pt_out, ALL_HEADS)
                    pe.wait_ge(o_low, HEADS // 2 + MHEADS)
                    group_is_out(pe, SGU_GROUP)
                    head_batches(ya)

            for b in range(3):
                if b == 0:
                    pe.wait_ge(tb_low, lows_through(TB_YA + 1))
                else:
                    pe.wait_ge(o_low, WC * b)
                for half in range(2):
                    g = BR_GROUP + 2 * b + half
                    start_group(g)
                    for j in range(2):
                        i = S_BR + 4 * b + 2 * half + j
                        if i == S_OUT - 1:
                            pe.wait_ge(merged, 1)
                            model_batches(merged_nat, (0, 1))
                        step(i, pp[g % 2], yT[b], 2 * j, j == 0, j == 1)
            def logits(cs):
                pe.wait_ge(tb_out, batch[0])
                for t in range(NT):
                    for c in cs:
                        last = mm(pp[1][:, 512 * t:512 * t + E], h2T[:, c, t * P:(t + 1) * P], wr3[:, c, :],
                                  start=(c == 0), stop=(c == KC - 1), skip_group_check=True)
                return last

            def gather_mms():
                for t in range(NT):
                    for half in range(2):
                        last = mm(ps_x[SLOTS * half:SLOTS * (half + 1), :], onehot[:, t, 0:SLOTS],
                                  h2[:, t, 512 * half:512 * (half + 1)], start=(t == 0), stop=(t == NT - 1))
                return last

            def token_transposes():
                for c in range(4):
                    last = nc.tensor.transpose(ps_x[:, P * c:P * (c + 1)], xn[:, P * c:P * (c + 1)], ident[:, :])
                return last

            def scatter_transposes():
                for t in range(NT):
                    last = nc.tensor.transpose(ps_s[:, P * t:P * (t + 1)], onehot[:, t, :], ident[:, :])
                return last

            def bias_mms(bank, col):
                for half in range(2):
                    mm(bank[SLOTS * half:SLOTS * (half + 1), :], expert_row,
                       bgu_sb[:, col + 512 * half:col + 512 * (half + 1)], start=True, stop=False)

            def x_chunk(kc):
                return P * (kc % 4) + SLOTS * (kc // 4)

            def up_mms(k, b):
                w = cube(buffer(b), 2)
                for c in range(2):
                    kc = 2 * k + c
                    for bank, col in ((ps_gate, 0), (ps_up, F)):
                        for half in range(2):
                            last = mm(bank[SLOTS * half:SLOTS * (half + 1), :],
                                      xg[:, x_chunk(kc):x_chunk(kc) + SLOTS],
                                      w[:, c, col + 512 * half:col + 512 * (half + 1)],
                                      start=False, stop=(kc == KC - 1))
                return last

            def hidden_transposes():
                for c in range(4):
                    last = nc.tensor.transpose(ps_hT[:, P * c:P * (c + 1)], act_h[:, P * c:P * (c + 1)],
                                               ident[:, :])
                return last

            def down_mms(k, b):
                w = cube(buffer(b), 4)
                for c in range(4):
                    for half in range(2):
                        last = mm(ps_y[SLOTS * half:SLOTS * (half + 1), :],
                                  hT_sb[:, P * c + SLOTS * k:P * c + SLOTS * (k + 1)],
                                  w[:, c, 512 * half:512 * (half + 1)],
                                  start=(k == 0 and c == 0), stop=(k == 1 and c == 3))
                return last

            def gather(e, meanwhile=None):
                pe.wait_ge(onehot_done, e + 1)
                pe.wait_ge(xg_out, e)
                pe.wait_ge(st_out, e)
                gather_mms().then_inc(gathered, 1)
                scatter_transposes().then_inc(st_done, 1)
                if meanwhile:
                    meanwhile()
                pe.wait_ge(xn_out, e + 1)
                token_transposes().then_inc(xt_done, 1)

            def scatter_mms(t, r, dst=ps_add):
                for half in range(2):
                    rows_ = slice(SLOTS * half, SLOTS * (half + 1))
                    last = mm(dst[:, 512 * half:512 * (half + 1)], scatter[r][rows_, t * P:(t + 1) * P],
                              y_sb[rows_, :], start=True, stop=True)
                return last

            def scatter_back(e, t, r):
                if t == 0:
                    pe.wait_ge(y_out, e + 1)
                    pe.wait_ge(st_out, e + 1)
                pe.wait_ge(summed, e * NT + (NT + t))
                scatter_mms(t, r).then_inc(scattered, 1)

            def expert(turn, r, between, after, first=False):
                e = turn * TURN + r
                pe.wait_ge(xg_out, e + 1)
                if not first:
                    pe.wait_ge(row_done, e + 1)
                    bias_mms(ps_gate, 0)
                    bias_mms(ps_up, F)
                for k in range(PER_EXPERT):
                    if k == UP_CHUNKS:
                        after()
                        pe.wait_ge(h_done, e + 1)
                        hidden_transposes().then_inc(hT_done, 1)
                        pe.wait_ge(hT_out, e + 1)
                    b = expert_buffer(r % TURN, k)
                    pe.wait_ge(ring_full[b], expert_fills(turn, r, k))
                    last = up_mms(k, b) if k < UP_CHUNKS else down_mms(k - UP_CHUNKS, b)
                    last.then_inc(ring_free, 1)
                    if k == 1:
                        between()

            def bias_back(t):
                if t == 0:
                    pe.wait_ge(wT_out, 1)
                    pe.wait_ge(bdown_in, 16)
                else:
                    pe.wait_ge(summed, t)
                for n in range(2):
                    last = mm(ps_add[:, 512 * n:512 * (n + 1)], wT_sb[:, t * P:(t + 1) * P],
                              bdown_sb[:, 512 * n:512 * (n + 1)], start=True, stop=True)
                last.then_inc(scattered, 1)

            for q, (n, j) in enumerate(OUT_ORDER):
                g = OUT_GROUP + n
                if j == 0:
                    start_group(g)
                if q == 3:
                    pe.wait_ge(merged, 2)
                    model_batches(merged_nat, (2, 3))
                if q == len(OUT_ORDER) - 1:
                    group_is_out(pe, OUT_GROUP)
                    model_batches(x3, (0, 1))
                pe.wait_ge(tb_low, lows_through(TB_MERGED + j))
                step(S_OUT + q, pp[g % 2], mergedT, 2 * j, j == 0, j == 3)

            pe.wait_ge(bcast_in, 4 * 16)
            logits(range(KC // 2))
            group_is_out(pe, OUT_GROUP + 1)
            model_batches(x3, (2, 3))
            logits(range(KC // 2, KC)).then_inc(logits_done, 1)
            pe.wait_ge(bgu_in, 16)
            pe.wait_ge(row_done, 1)
            bias_mms(ps_gate, 0)
            pe.wait_ge(masks_done, 2)
            pe.wait_ge(sel_done, 1)
            mm(pp[1][:, 0:E], before[:, :], sel3[:, 0, :], start=True, stop=True)
            mm(pp[1][:, E:2 * E], ones[:, :], sel3[:, 0, :], start=True, stop=False)
            mm(pp[1][:, E:2 * E], before[:, :], sel3[:, 1, :], start=False, stop=True)
            mm(pp[1][:, 2 * E:3 * E], ones[:, :], sel3[:, 0, :], start=True, stop=False)
            mm(pp[1][:, 2 * E:3 * E], ones[:, :], sel3[:, 1, :], start=False, stop=True).then_inc(rank_done, 1)
            bias_mms(ps_up, F)

            def weight_transposes():
                pe.wait_ge(wgt_done, 1)
                for t in range(NT):
                    last = nc.tensor.transpose(ps_y[0:E, P * t:P * (t + 1)], wgt3[:, t, :], ident[:, :])
                last.then_inc(wT_done, 1)

            pe.wait_ge(h2_done, 1)
            pe.wait_ge(h2_pool, NT)
            gather(0)
            weight_transposes()

            def after_first():
                bias_back(1)
                gather(1)

            expert(0, 0, lambda: bias_back(0), after_first, first=True)
            with pe.Fori(0, (E - 2) // TURN) as turn:
                for r in range(1, TURN + 1):
                    e = turn * TURN + r

                    def between():
                        scatter_back(e - 1, 0, r - 1)

                    def after():
                        gather(e + 1, lambda: scatter_back(e - 1, 1, r - 1))

                    expert(turn, r, between, after)
            r = (E - 1) % TURN
            expert((E - 1) // TURN, r, lambda: scatter_back(E - 2, 0, r - 1), lambda: scatter_back(E - 2, 1, r - 1))
            scatter_back(E - 1, 0, r)
            scatter_mms(1, r, last_sum).then_inc(scattered, 1)

            pe.sem_inc(o_down, 1)
            pe.sem_inc(o_st, 1)
            pe.wait_ge(items_done, 1)
            n_over = pe.value_load(n_items[0:1, 0:1], min_val=0, max_val=ITEMS)
            with pe.If(n_over > 0):
                with pe.Fori(0, ITEMS) as i:
                    with pe.If(n_over > i):
                        pe.wait_ge(o_onehot, i + 1)
                        gather_mms().then_inc(o_gath, 1)
                        scatter_transposes().then_inc(o_st, 1)
                        pe.wait_ge(o_xn, i + 1)
                        token_transposes().then_inc(o_xt, 1)
                        pe.wait_ge(o_full, i * 96 + 96)
                        pe.wait_ge(o_xg, i + 1)
                        pe.wait_ge(o_row, i + 1)
                        bias_mms(ps_gate, 0)
                        bias_mms(ps_up, F)
                        for k in range(UP_CHUNKS):
                            last = up_mms(k, ORDER[k])
                        last.then_inc(o_up, 1)
                        pe.wait_ge(o_h, i + 1)
                        hidden_transposes().then_inc(o_hT, 1)
                        pe.wait_ge(o_hTout, i + 1)
                        for k in range(DOWN_CHUNKS):
                            last = down_mms(k, ORDER[UP_CHUNKS + k])
                        last.then_inc(o_down, 1)
                        pe.wait_ge(o_y, i + 1)
                        pe.wait_ge(o_stout, i + 1)
                        pe.wait_ge(summed, NT * (E + 1))
                        scatter_mms(0, 0).then_inc(o_scat, 1)
                        pe.wait_ge(o_sum, i * NT + 2)
                        scatter_mms(1, 0).then_inc(o_scat, 1)
                        pe.wait_ge(o_sum, i * NT + 3)

        @block.vector
        def _(dve):
            v = nc.vector
            links = [0]

            def link(ins):
                links[0] += 1
                ins.then_inc(v_chain, 1)
                dve.wait_ge(v_chain, links[0])

            link(v.memset(eps[:, :], EPS))
            link(v.memset(turn[:, :], 0.0))
            v.memset(rep8[:, :], SENTINEL).then_inc(dve_const, 1)

            def model_norm(n, col):
                dve.wait_ge(root, n + 1)
                v.reciprocal(rstd[:, col:col + NT], rstd[:, col:col + NT]).then_inc(normed, 1)

            def head_sums(n, g, src, heads, col):
                group_is_out(dve, g)
                if n == 0:
                    dve.wait_ge(sumsq, 2 * NT)
                link(v.tensor_tensor(cube(squares, NT), src, src, ALU.mult))
                v.tensor_reduce(ss[:, col:col + NT * heads],
                                squares.rearrange("p (th d) -> p th d", th=NT * heads), AX.X,
                                ALU.add).then_inc(head_ss, 1)

            def head_norm(n, src, heads, col):
                dve.wait_ge(root, 3 + n)
                link(v.reciprocal(rstd[:, col:col + NT * heads], rstd[:, col:col + NT * heads]))
                flat = src.rearrange("p t n -> p (t n)").rearrange("p (th d) -> p th d", th=NT * heads)
                scale = rstd[:, col:col + NT * heads].unsqueeze(2).to_broadcast(flat.shape)
                v.tensor_tensor(flat, flat, scale, ALU.mult).then_inc(normed, 1)

            split = [0]

            def low_parts(upto):
                for i in range(split[0], min(upto, STEPS)):
                    dve.wait_ge(hi_done, i + 1)
                    hi, lo = stages[i % STAGES]
                    v.tensor_tensor(lo, step_weights(i), hi.bitcast(F32), ALU.subtract).then_inc(lo_done, 1)
                    split[0] = i + 1

            def model_lows(batch, dstT, gain, ms=range(KC // 2)):
                for m in ms:
                    dve.wait_ge(tb_out, batch + m + 1)
                    bank = tb_banks[(batch + m) % 4]
                    hi, lo = (part[:, 2 * m:2 * m + 2, :] for part in dstT)
                    if gain is None:
                        last = v.tensor_tensor(lo, cube(bank, 2), hi.bitcast(F32), ALU.subtract)
                    else:
                        for c in range(2):
                            a = gain + 2 * m + c
                            last = v.scalar_tensor_tensor(lo[:, c, :], bank[:, 256 * c:256 * (c + 1)],
                                                          cols[:, a:a + 1], hi[:, c, :].bitcast(F32),
                                                          ALU.mult, ALU.subtract)
                    last.then_inc(tb_low, 1)

            model_norm(0, SS_X)
            for m in range(KC // 2):
                model_lows(TB_X, hT, G_MIX, (m,))
                if m >= 1:
                    low_parts(m)
            low_parts(STAGES)
            model_norm(1, SS_MEM)
            for n, (g, src, heads) in enumerate(((C_QB, nat[0], HEADS), (C_KB, nat[1], HEADS),
                                                 (C_QM, nat[0], MHEADS), (C_MK, nat[1], MHEADS))):
                low_parts(steps_through(g) + STAGES)
                head_sums(n, g, src, heads, SS_QK + 16 * n)
                if n == 0:
                    model_lows(TB_MEM, memT, G_MEM)
                low_parts(steps_through(g) + STAGES + (1 if g == C_QM else 0))
                head_norm(n, src, heads, SS_QK + 16 * n)
            low_parts(steps_through(C_VS) + STAGES)
            head_sums(4, C_VS, v_sgu, 1, SS_V)
            low_parts(steps_through(C_VS) + 2 + STAGES)
            dve.wait_ge(root, 7)
            dve.wait_ge(bcast_in, 4 * 16)
            link(v.reciprocal(rstd[:, SS_V:SS_V + NT], rstd[:, SS_V:SS_V + NT]))
            for t in range(NT):
                last = v.scalar_tensor_tensor(v_sgu[:, t, :], v_sgu[:, t, :], rstd[:, SS_V + t:SS_V + t + 1],
                                              gv_bc[:, :], ALU.mult, ALU.mult)
            last.then_inc(normed, 1)
            low_parts(steps_through(C_U) + STAGES)

            def maxima(h):
                dve.wait_ge(s_done, h + 1)
                if h >= 2:
                    dve.wait_ge(pt_done, h - 1)
                m0, m1 = stat_m(h, 0), stat_m(h, 1)
                both = ss[:, SS_MAX + 2 * (h % 4):SS_MAX + 2 * (h % 4) + 2]
                if is_moba(h):
                    logits = prob[h % 2]
                    scaled = 2.0 ** (-8.0 * (h + 1) / HEADS)
                    link(v.scalar_tensor_tensor(logits[:, 0:3 * P], rel[:, :], scaled,
                                                ps_score[h % 2][:, 0:3 * P], ALU.mult, ALU.add))
                    v.tensor_reduce(m0, logits[:, 0:P], AX.X, ALU.max)
                    link(v.tensor_reduce(m1, logits[:, P:3 * P], AX.X, ALU.max))
                else:
                    link(v.tensor_reduce(both, cube(ps_score[h % 2], 2), AX.X, ALU.max))
                v.tensor_scalar(both, both, -1.0, None, ALU.mult).then_inc(max_done, 1)

            def reciprocals(h):
                dve.wait_ge(exp_done, h + 1)
                c = SS_SUM + 2 * (h % 4)
                v.reciprocal(rstd[:, c:c + 2], ss[:, c:c + 2]).then_inc(recip_done, 1)

            dve.wait_ge(masks_done, 4)
            for s in range(HEAD_STEPS):
                for h in head_at(s):
                    maxima(h)
                    reciprocals(h)
                for h in head_at(s - TO_OUTPUT):
                    if not is_moba(h) or h % 2 == 1:
                        u = o_unit(h)
                        dve.wait_ge(o_out, u + 1)
                        hi, lo = head_dst(h)
                        v.tensor_tensor(lo, ps_o[:, 256 * (u % 2):256 * (u % 2 + 1)], hi.bitcast(F32),
                                        ALU.subtract).then_inc(o_low, 1)
                if s == 4:
                    dve.wait_ge(sgu_done, 1)
                    group_is_out(dve, C_U)
                    bank = cube(pp[SGU_GROUP % 2], NT)
                    for gg in range(GROUPS):
                        a = slice(P * gg, P * (gg + 1))
                        last = v.scalar_tensor_tensor(ya[:, :, a], bank[:, :, a],
                                                      cols[:, B_SPATIAL + gg:B_SPATIAL + gg + 1],
                                                      ya[:, :, a], ALU.add, ALU.mult)
                    last.then_inc(group_out[SGU_GROUP % 2], 1)
                low_parts(S_GATE + s + 1 + STAGES)
                if s == YA_STEP:
                    for t in range(NT):
                        dve.wait_ge(tb_out, TB_YA + t + 1)
                        hi, lo = (part[:, :, t * P:(t + 1) * P] for part in yT[0])
                        v.tensor_tensor(lo, cube(tb_banks[(TB_YA + t) % 4], WC), hi.bitcast(F32),
                                        ALU.subtract).then_inc(tb_low, 1)

            for b in range(3):
                if b < 2:
                    dve.wait_ge(gate_sig, b + 1)
                else:
                    group_is_out(dve, C_GATE + 6)
                for half in range(2):
                    g = BR_GROUP + 2 * b + half
                    if g == OUT_GROUP - 1:
                        low_parts(S_OUT)
                        model_lows(TB_MERGED, mergedT, None, (0, 1))
                    low_parts(steps_through(g) + (1 if g == OUT_GROUP - 2 else 2))
                    dve.wait_ge(step_done, steps_through(g))
                    a = slice(512 * half, 512 * (half + 1))
                    v.tensor_tensor(gates[b][:, :, a], cube(pp[g % 2], NT), gates[b][:, :, a],
                                    ALU.mult).then_inc(group_out[g % 2], 1)
                    if b == 2:
                        group_is_out(dve, g)
                        dve.wait_ge(pool_added, half + 1)
                        v.tensor_tensor(merged_nat[:, :, a], merged_nat[:, :, a], gates[2][:, :, a],
                                        ALU.add).then_inc(merged, 1)
            low_parts(S_OUT + 1 + STAGES)
            model_lows(TB_MERGED, mergedT, None, (2, 3))

            for n in range(2):
                g = OUT_GROUP + n
                low_parts(steps_through(g) + STAGES)
                dve.wait_ge(step_done, steps_through(g))
                for t in range(NT):
                    last = v.tensor_tensor(x3[:, t, 512 * n:512 * (n + 1)], pp[g % 2][:, 512 * t:512 * (t + 1)],
                                           x3[:, t, 512 * n:512 * (n + 1)], ALU.add)
                last.then_inc(group_out[g % 2], 1)
            v.memset(ext[:, :, E:E + 4], SENTINEL)
            dve.wait_ge(x_ss, 2)
            v.tensor_reduce(ss[:, SS_X2SUM:SS_X2SUM + NT], cube(ss[:, SS_X2:SS_X2 + 4], NT), AX.X,
                            ALU.add).then_inc(x_sum, 1)
            dve.wait_ge(x_root, 1)
            v.reciprocal(rstd[:, SS_X2SUM:SS_X2SUM + NT], rstd[:, SS_X2SUM:SS_X2SUM + NT]).then_inc(x_rstd, 1)
            dve.wait_ge(x_rstd, 1)

            def make_row(e):
                v.tensor_scalar(expert_row, part[0:E, :], turn[0:E, 0:1], None, ALU.is_equal).then_inc(row_done, 1)
                dve.wait_ge(row_done, e + 1)
                v.tensor_scalar(turn[:, :], turn[:, :], 1.0, None, ALU.add)

            dve.wait_ge(pool_const, 9)
            make_row(0)
            dve.wait_ge(logits_done, 1)
            for t in range(NT):
                last = v.scalar_tensor_tensor(ext[:, t, 0:E], pp[1][:, 512 * t:512 * t + E],
                                              rstd[:, SS_X2SUM + t:SS_X2SUM + t + 1], br_bc[:, :],
                                              ALU.mult, ALU.add)
            link(last)
            top3, rep3 = cube(top8[:, :], NT), cube(rep8[:, :], NT)
            for t in range(NT):
                last = v.max(top3[:, t, :], ext[:, t, :])
            link(last)
            v.tensor_scalar(stat[:, 0:NT], top3[:, :, 0], -1.0, None, ALU.mult).then_inc(top_done, 1)
            link(v.tensor_copy(rep3[:, :, 0:TOP_K], top3[:, :, 0:TOP_K]))
            for t in range(NT):
                last = v.match_replace(ext2[:, t, :], rep3[:, t, :], ext[:, t, :], REPLACED)
            link(last)
            v.tensor_tensor(sel3, ext2[:, :, 0:E], ext[:, :, 0:E], ALU.not_equal).then_inc(sel_done, 1)
            for t in range(NT):
                last = v.scalar_tensor_tensor(h2[:, t, 0:512], x3[:, t, 0:512],
                                              rstd[:, SS_X2SUM + t:SS_X2SUM + t + 1], gffn_bc[:, 0:512],
                                              ALU.mult, ALU.mult)
            last.then_inc(h2_done, 1)
            dve.wait_ge(rank_done, 1)
            link(v.scalar_tensor_tensor(slot3, cube(pp[1][:, 0:NT * E], NT), 1.0, sel3, ALU.add, ALU.mult))

            def make_onehot(e):
                dve.wait_ge(st_done, e)
                for t in range(NT):
                    last = v.tensor_scalar(onehot[:, t, :], iota1[:, :], slot1[:, bass.ds(e + E * t, 1)], None,
                                           ALU.is_equal)
                last.then_inc(onehot_done, 1)

            for t in range(NT):
                last = v.tensor_scalar(onehot[:, t, :], iota1[:, :], slot3[:, t, 0:1], None, ALU.is_equal)
            last.then_inc(onehot_done, 1)

            v.tensor_copy(counts[:, :], pp[1][:, 2 * E:3 * E])
            dve.wait_ge(e_done, 1)
            link(v.tensor_tensor(e_exp, e_exp, sel3, ALU.mult))
            link(v.tensor_reduce(route[:, 0:NT], e_exp, AX.X, ALU.add))
            link(v.reciprocal(route[:, NT:2 * NT], route[:, 0:NT]))
            for t in range(NT):
                last = v.tensor_scalar(wgt3[:, t, :], e_exp[:, t, :], route[:, NT + t:NT + t + 1], None, ALU.mult)
            last.then_inc(wgt_done, 1)

            for b in range(BLOCKS - 1):
                last = v.tensor_scalar(flags[:, E * b:E * (b + 1)], counts[:, :],
                                       float(SLOTS * (b + 1)), None, ALU.is_gt)
            link(last)
            link(v.tensor_tensor_scan(incl, ones[:, 0:NF], flags, 0.0, ALU.mult, ALU.add))
            v.tensor_copy(n_items[:, :], incl[:, NF - 1:NF])
            v.memset(over[:, 0:1], 1.0)
            v.tensor_tensor(order, incl, flags, ALU.mult).then_inc(items_done, 1)

            def swiglu(e):
                dve.wait_ge(ring_free, e * PER_EXPERT + UP_CHUNKS)

                def step(ins, n):
                    ins.then_inc(e_chain, 1)
                    dve.wait_ge(e_chain, e * 2 + n)

                v.tensor_scalar(glu, ps_gate, LIMIT, None, ALU.min).then_inc(glu_done, 1)
                step(v.tensor_scalar(ps_up, ps_up, -LIMIT, LIMIT, ALU.max, ALU.min), 1)
                step(v.scalar_tensor_tensor(ps_up, ps_up, 1.0, glu, ALU.add, ALU.mult), 2)
                dve.wait_ge(sig_done, e + 1)
                v.tensor_tensor(act_h, ps_up, sig, ALU.mult).then_inc(h_done, 1)

            def sum_up(e, t, src=ps_add):
                dve.wait_ge(scattered, e * NT + (NT + t + 1))
                v.scalar_tensor_tensor(x3[:, t, :], src, wgt[:, bass.ds(e + E * t, 1)], x3[:, t, :],
                                       ALU.mult, ALU.add).then_inc(summed, 1)

            def sum_bias(t):
                dve.wait_ge(scattered, t + 1)
                v.tensor_tensor(x3[:, t, :], ps_add, x3[:, t, :], ALU.add).then_inc(summed, 1)

            make_onehot(1)
            sum_bias(0)
            swiglu(0)
            make_row(1)
            sum_bias(1)
            with dve.Fori(1, E - 1) as e:
                make_onehot(e + 1)
                sum_up(e - 1, 0)
                swiglu(e)
                make_row(e + 1)
                sum_up(e - 1, 1)
            sum_up(E - 2, 0)
            swiglu(E - 1)
            sum_up(E - 2, 1)
            dve.sem_inc(o_sum, 1)
            sum_up(E - 1, 0)
            sum_up(E - 1, 1, last_sum)

            OLINKS = 14
            n_over = dve.value_load(n_items[0:1, 0:1], min_val=0, max_val=ITEMS)
            with dve.If(n_over > 0):
                with dve.Fori(0, ITEMS) as i:
                    with dve.If(n_over > i):
                        count = [0]

                        def step(ins):
                            count[0] += 1
                            ins.then_inc(o_chain, 1)
                            dve.wait_ge(o_chain, i * OLINKS + count[0])

                        step(v.tensor_scalar(pick, order, over[:, 0:1], None, ALU.is_equal))
                        step(v.tensor_tensor(pick2, pick, item_e[:, :], ALU.mult))
                        step(v.tensor_reduce(over[:, 1:2], pick2, AX.X, ALU.add))
                        v.tensor_copy(over_e[:, :], over[:, 1:2]).then_inc(o_item, 1)
                        step(v.tensor_tensor(pick2, pick, item_b[:, :], ALU.mult))
                        step(v.tensor_reduce(over[:, 2:3], pick2, AX.X, ALU.add))
                        step(v.tensor_tensor(pick_e, pick[:, 0:E], pick[:, E:2 * E], ALU.add))
                        step(v.tensor_tensor(pick_e, pick_e, pick[:, 2 * E:3 * E], ALU.add))
                        for dst, src in ((3, slot3), (5, wgt3)):
                            step(v.tensor_tensor(cube(pick2[:, 0:NT * E], NT), src,
                                                 pick_e.unsqueeze(1).to_broadcast([P, NT, E]), ALU.mult))
                            step(v.tensor_reduce(over[:, dst:dst + NT], cube(pick2[:, 0:NT * E], NT), AX.X, ALU.add))
                        step(v.tensor_scalar(over[:, 3:5], over[:, 3:5], over[:, 2:3], None, ALU.subtract))
                        dve.wait_ge(o_st, i + 1)
                        for t in range(NT):
                            last = v.tensor_scalar(onehot[:, t, :], iota1[:, :], over[:, 3 + t:4 + t], None,
                                                   ALU.is_equal)
                        last.then_inc(o_onehot, 1)
                        dve.wait_ge(o_down, i + 1)
                        v.tensor_scalar(expert_row, part[0:E, :], over[0:E, 1:2], None, ALU.is_equal).then_inc(o_row, 1)
                        v.tensor_scalar(over[:, 0:1], over[:, 0:1], 1.0, None, ALU.add)

                        dve.wait_ge(o_up, i + 1)
                        v.tensor_scalar(glu, ps_gate, LIMIT, None, ALU.min).then_inc(o_glu, 1)
                        step(v.tensor_scalar(ps_up, ps_up, -LIMIT, LIMIT, ALU.max, ALU.min))
                        step(v.scalar_tensor_tensor(ps_up, ps_up, 1.0, glu, ALU.add, ALU.mult))
                        assert count[0] == OLINKS
                        dve.wait_ge(o_sig, i + 1)
                        v.tensor_tensor(act_h, ps_up, sig, ALU.mult).then_inc(o_h, 1)
                        for t in range(NT):
                            dve.wait_ge(o_scat, i * NT + (t + 1))
                            v.scalar_tensor_tensor(x3[:, t, :], ps_add, over[:, 5 + t:6 + t], x3[:, t, :],
                                                   ALU.mult, ALU.add).then_inc(o_sum, 1)


_INS = ['x', 'mem', 'g_mix', 'w_in', 'g_sgu_v', 'w_spatial', 'b_spatial', 'g_q_moba', 'g_k_moba',
        'g_mem', 'w_mem_kv', 'g_q_mem', 'g_k_mem', 'w_br_sgu', 'w_br_moba', 'w_br_mem', 'w_out',
        'g_ffn', 'w_router', 'b_router', 'w_gate_up', 'b_gate_up', 'w_down', 'b_down']


def kernel(**inputs):
    import numpy as np
    import concourse.bacc as bacc
    from concourse.bass_utils import run_bass_kernel_spmd

    nc = bacc.Bacc("TRN2", target_bir_lowering=False, num_devices=1)
    arrays, args = {}, []
    for name in _INS:
        a = np.ascontiguousarray(inputs[name])
        arrays[f"in_{name}"] = a
        args.append(nc.dram_tensor(f"in_{name}", a.shape, mybir.dt.from_np(a.dtype), kind="ExternalInput").ap())
    shape = inputs["x"].shape
    args.append(nc.dram_tensor("out_0", shape, F32, kind="ExternalOutput").ap())
    build(nc, *args)
    r = run_bass_kernel_spmd(nc, [arrays], core_ids=[0])
    return r.results[0]["out_0"]
```
